# Optimizing a Trainium2 kernel written in Bass

```python
import math
import jax
import jax.numpy as jnp
from jax import lax
import numpy as np

D_MODEL = 1024
BATCH = 1
SEQ = 1024
DEPTH = 1

DA_HEADS = 4
DA_HEAD_DIM = 64
DA_V_DIM = 2 * DA_HEAD_DIM
GLA_HEADS = 4
GLA_DK = 64
GLA_DV = 128
GLA_GATE_RANK = 16
GLA_TAU = 16.0
GLA_CHUNK = 64
MEM_LEN = 256
XA_HEADS = 4
XA_HEAD_DIM = 128
N_BRANCH = 3
PEER_HEADS = 8
PEER_N_KEYS = 128
PEER_N_EXPERTS = PEER_N_KEYS * PEER_N_KEYS
PEER_QDIM = 256
PEER_TOPK = 16
PEER_TOKEN_BLOCK = 128
Q_BLOCK = 128
RMS_EPS = 1e-6
D_IN_PROJ = (3 * DA_HEADS * 2 * DA_HEAD_DIM + 2 * GLA_HEADS * GLA_DK + 2 * GLA_HEADS * GLA_DV + GLA_GATE_RANK + XA_HEADS * XA_HEAD_DIM + N_BRANCH * D_MODEL)

kernel_name = "hybrid_diffattn_gla_memxattn_peer"

def _in_proj_splits():
    sizes = [DA_HEADS * 2 * DA_HEAD_DIM, DA_HEADS * 2 * DA_HEAD_DIM, DA_HEADS * DA_V_DIM,
             GLA_HEADS * GLA_DK, GLA_HEADS * GLA_DK, GLA_HEADS * GLA_DV, GLA_HEADS * GLA_DV, GLA_GATE_RANK,
             XA_HEADS * XA_HEAD_DIM, N_BRANCH * D_MODEL]
    splits, acc = [], 0
    for s in sizes[:-1]:
        acc += s
        splits.append(acc)
    return splits

def _rmsnorm(t, w):
    tf = t.astype(jnp.float32)
    y = tf * lax.rsqrt(jnp.mean(tf * tf, axis=-1, keepdims=True) + RMS_EPS)
    return (y * w.astype(jnp.float32)).astype(t.dtype)

def _alibi_slopes(n_heads):
    return jnp.exp2(-8.0 * jnp.arange(1, n_heads + 1, dtype=jnp.float32) / n_heads)

def _diff_attention(q, k, v, lam, slopes):
    B, H, _, S, d = q.shape
    nblk = S // Q_BLOCK
    kpos = jnp.arange(S, dtype=jnp.int32)
    scale = d ** -0.5
    q_blocks = q.reshape(B, H, 2, nblk, Q_BLOCK, d).transpose(3, 0, 1, 2, 4, 5)

    def block(args):
        q_blk, i = args
        qpos = i * Q_BLOCK + jnp.arange(Q_BLOCK, dtype=jnp.int32)
        dist = qpos[:, None] - kpos[None, :]
        bias = -slopes[:, None, None] * dist.astype(jnp.float32)[None]
        s = jnp.einsum('bhmqd,bhmkd->bhmqk', q_blk, k).astype(jnp.float32) * scale + bias[None, :, None]
        s = jnp.where(dist[None, None, None] >= 0, s, -jnp.inf)
        p = jax.nn.softmax(s, axis=-1)
        w = p[:, :, 0] - lam * p[:, :, 1]
        return jnp.einsum('bhqk,bhkv->bhqv', w.astype(v.dtype), v)

    out = lax.map(block, (q_blocks, jnp.arange(nblk, dtype=jnp.int32)))
    return out.transpose(1, 2, 0, 3, 4).reshape(B, H, S, v.shape[-1])

def _gla(q, k, v, log_a):
    B, S, H, dk = q.shape
    dv = v.shape[-1]
    C = GLA_CHUNK
    n = S // C
    out_dtype = v.dtype

    def to_chunks(t):
        return t.astype(jnp.float32).reshape(B, n, C, H, t.shape[-1]).transpose(1, 0, 3, 2, 4)

    qc, kc, vc, gc = to_chunks(q * (dk ** -0.5)), to_chunks(k), to_chunks(v), to_chunks(log_a)
    causal = jnp.tril(jnp.ones((C, C), dtype=bool))

    def step(state, inp):
        qt, kt, vt, gt = inp
        b = jnp.cumsum(gt, axis=2)
        o_inter = jnp.einsum('bhcd,bhde->bhce', qt * jnp.exp(b), state)
        diff = b[:, :, :, None, :] - b[:, :, None, :, :]
        decay = jnp.exp(jnp.where(causal[:, :, None], diff, -jnp.inf))
        a = jnp.einsum('bhtd,bhsd,bhtsd->bhts', qt, kt, decay)
        o_intra = jnp.einsum('bhts,bhse->bhte', a, vt)
        b_last = b[:, :, -1:, :]
        k_dec = kt * jnp.exp(b_last - b)
        state = state * jnp.exp(b_last[:, :, 0, :])[..., None] + jnp.einsum('bhcd,bhce->bhde', k_dec, vt)
        return state, o_inter + o_intra

    state0 = jnp.zeros((B, H, dk, dv), jnp.float32)
    _, o = lax.scan(step, state0, (qc, kc, vc, gc))
    return o.transpose(1, 0, 3, 2, 4).reshape(B, S, H, dv).astype(out_dtype)

def _mem_attention(q, k, v):
    d = q.shape[-1]
    s = jnp.einsum('bshd,bmhd->bhsm', q, k).astype(jnp.float32) * (d ** -0.5)
    p = jax.nn.softmax(s, axis=-1)
    return jnp.einsum('bhsm,bmhd->bshd', p.astype(v.dtype), v)

def _peer(xn, w_q, sub_keys, expert_u, expert_v):
    B, S, D = xn.shape
    T = PEER_TOKEN_BLOCK
    K = PEER_TOPK
    H = PEER_HEADS
    x_blocks = xn.reshape(-1, T, D)

    def block(xb):
        q = (xb @ w_q).reshape(T, H, 2, PEER_QDIM // 2)
        s = jnp.einsum('thpc,pnc->thpn', q, sub_keys).astype(jnp.float32)
        top_s, top_i = lax.top_k(s, K)
        cand_s = top_s[:, :, 0, :, None] + top_s[:, :, 1, None, :]
        cand_i = top_i[:, :, 0, :, None] * PEER_N_KEYS + top_i[:, :, 1, None, :]
        best_s, best_j = lax.top_k(cand_s.reshape(T, H, K * K), K)
        idx = jnp.take_along_axis(cand_i.reshape(T, H, K * K), best_j, axis=-1)
        g = jax.nn.softmax(best_s, axis=-1)
        u = expert_u[idx]
        v = expert_v[idx]
        act = jax.nn.gelu(jnp.einsum('thkd,td->thk', u, xb).astype(jnp.float32), approximate=False)
        return jnp.einsum('thk,thkd->td', (g * act).astype(xb.dtype), v)

    return lax.map(block, x_blocks).reshape(B, S, D)

def setup_inputs(seed: int = 0) -> dict:
    key = jax.random.key(seed)
    ks = iter(jax.random.split(key, 32))
    L, D = DEPTH, D_MODEL
    f32 = jnp.float32

    def nrm(shape, scale):
        return jax.random.normal(next(ks), shape, f32) * scale

    def gain(shape):
        return 1.0 + 0.02 * jax.random.normal(next(ks), shape, f32)

    da_w = DA_HEADS * DA_V_DIM
    gla_w = GLA_HEADS * GLA_DV
    xa_w = XA_HEADS * XA_HEAD_DIM
    return {
        'x': nrm((BATCH, SEQ, D), 1.0),
        'mem': nrm((BATCH, MEM_LEN, D), 1.0),
        'mix_norm_w': gain((L, D)),
        'w_in': nrm((L, D, D_IN_PROJ), D ** -0.5),
        'da_q_norm_w': gain((L, DA_HEAD_DIM)),
        'da_k_norm_w': gain((L, DA_HEAD_DIM)),
        'da_lambda': nrm((L, 4, DA_HEAD_DIM), 0.1),
        'da_out_norm_w': gain((L, DA_V_DIM)),
        'gla_w_gate': nrm((L, GLA_GATE_RANK, GLA_HEADS * GLA_DK), GLA_GATE_RANK ** -0.5),
        'gla_b_gate': nrm((L, GLA_HEADS * GLA_DK), 0.01),
        'gla_out_norm_w': gain((L, GLA_DV)),
        'mem_norm_w': gain((L, D)),
        'w_mem_kv': nrm((L, D, 2 * xa_w), D ** -0.5),
        'xa_q_norm_w': gain((L, XA_HEAD_DIM)),
        'xa_k_norm_w': gain((L, XA_HEAD_DIM)),
        'w_br_da': nrm((L, da_w, D), da_w ** -0.5),
        'w_br_gla': nrm((L, gla_w, D), gla_w ** -0.5),
        'w_br_xa': nrm((L, xa_w, D), xa_w ** -0.5),
        'w_out': nrm((L, D, D), D ** -0.5),
        'ffn_norm_w': gain((L, D)),
        'peer_w_q': nrm((L, D, PEER_HEADS * PEER_QDIM), D ** -0.5),
        'peer_sub_keys': nrm((L, 2, PEER_N_KEYS, PEER_QDIM // 2), (PEER_QDIM // 2) ** -0.5),
        'peer_u': nrm((L, PEER_N_EXPERTS, D), D ** -0.5),
        'peer_v': nrm((L, PEER_N_EXPERTS, D), 0.1),
    }

def reference(x, mem, mix_norm_w, w_in, da_q_norm_w, da_k_norm_w, da_lambda, da_out_norm_w,
              gla_w_gate, gla_b_gate, gla_out_norm_w, mem_norm_w, w_mem_kv, xa_q_norm_w, xa_k_norm_w,
              w_br_da, w_br_gla, w_br_xa, w_out, ffn_norm_w, peer_w_q, peer_sub_keys, peer_u, peer_v):
    B, S, D = x.shape
    M = mem.shape[1]
    slopes = _alibi_slopes(DA_HEADS)
    splits = _in_proj_splits()
    for l in range(DEPTH):
        xn = _rmsnorm(x, mix_norm_w[l])
        proj = xn @ w_in[l]
        (da_q, da_k, da_v, gl_q, gl_k, gl_v, gl_r, gl_g, xa_q, gate_logits) = jnp.split(proj, splits, axis=-1)

        dq = _rmsnorm(da_q.reshape(B, S, DA_HEADS, 2, DA_HEAD_DIM), da_q_norm_w[l]).transpose(0, 2, 3, 1, 4)
        dk = _rmsnorm(da_k.reshape(B, S, DA_HEADS, 2, DA_HEAD_DIM), da_k_norm_w[l]).transpose(0, 2, 3, 1, 4)
        dv = da_v.reshape(B, S, DA_HEADS, DA_V_DIM).transpose(0, 2, 1, 3)
        lam_init = 0.8 - 0.6 * math.exp(-0.3 * l)
        lvec = da_lambda[l].astype(jnp.float32)
        lam = jnp.exp(jnp.sum(lvec[0] * lvec[1])) - jnp.exp(jnp.sum(lvec[2] * lvec[3])) + lam_init
        o_da = _diff_attention(dq, dk, dv, lam, slopes)
        o_da = (_rmsnorm(o_da, da_out_norm_w[l]) * (1.0 - lam_init)).transpose(0, 2, 1, 3).reshape(B, S, DA_HEADS * DA_V_DIM)

        log_a = jax.nn.log_sigmoid((gl_g @ gla_w_gate[l] + gla_b_gate[l]).astype(jnp.float32)) / GLA_TAU
        o_gla = _gla(gl_q.reshape(B, S, GLA_HEADS, GLA_DK), gl_k.reshape(B, S, GLA_HEADS, GLA_DK),
                     gl_v.reshape(B, S, GLA_HEADS, GLA_DV), log_a.reshape(B, S, GLA_HEADS, GLA_DK))
        o_gla = _rmsnorm(o_gla, gla_out_norm_w[l]).reshape(B, S, GLA_HEADS * GLA_DV) * jax.nn.silu(gl_r)

        mem_n = _rmsnorm(mem, mem_norm_w[l])
        mk, mv = jnp.split(mem_n @ w_mem_kv[l], 2, axis=-1)
        xq = _rmsnorm(xa_q.reshape(B, S, XA_HEADS, XA_HEAD_DIM), xa_q_norm_w[l])
        mk = _rmsnorm(mk.reshape(B, M, XA_HEADS, XA_HEAD_DIM), xa_k_norm_w[l])
        mv = mv.reshape(B, M, XA_HEADS, XA_HEAD_DIM)
        o_xa = _mem_attention(xq, mk, mv).reshape(B, S, XA_HEADS * XA_HEAD_DIM)

        g = jax.nn.sigmoid(gate_logits.astype(jnp.float32)).astype(x.dtype).reshape(B, S, N_BRANCH, D)
        merged = (g[:, :, 0] * (o_da @ w_br_da[l]) + g[:, :, 1] * (o_gla @ w_br_gla[l])
                  + g[:, :, 2] * (o_xa @ w_br_xa[l]))
        x = x + merged @ w_out[l]

        x = x + _peer(_rmsnorm(x, ffn_norm_w[l]), peer_w_q[l], peer_sub_keys[l], peer_u[l], peer_v[l])
    return x


_drawn_inputs = setup_inputs


def setup_inputs(seed=0):
    import zlib

    import numpy as np

    out = dict(_drawn_inputs(seed))
    spreads = {}
    factors = {'mix_norm_w': 3.014,
     'da_q_norm_w': 7.815,
     'da_k_norm_w': 6.785,
     'da_out_norm_w': 49.592,
     'gla_b_gate': 21.89,
     'gla_out_norm_w': 20.088,
     'mem_norm_w': 8.0,
     'xa_q_norm_w': 8.0,
     'xa_k_norm_w': 8.0,
     'ffn_norm_w': 58.279}
    for name, (base, spread) in spreads.items():
        noise = np.random.default_rng([zlib.crc32(name.encode()), seed]).standard_normal(out[name].shape)
        drawn = base * np.exp(spread * noise) if base else spread * noise
        out[name] = jnp.asarray(drawn.astype(out[name].dtype))
    for name, factor in factors.items():
        out[name] = (out[name] * factor).astype(out[name].dtype)
    return out
```

```python
from contextlib import ExitStack

import numpy as np

import concourse.bass as bass
from concourse import mybir

F32 = mybir.dt.float32
U32 = mybir.dt.uint32
ALU = mybir.AluOpType
ACT = mybir.ActivationFunctionType
AX = mybir.AxisListType.X

P = 128
D = 1024
SEQ = 1024
KC = D // P
NT = 2
T = NT * P
STEPS = SEQ // T
EPS = 1e-6
DA_H, DA_D, DA_V = 4, 64, 128
GL_H, GL_K, GL_V, GL_R, GL_TAU = 4, 64, 128, 16, 16.0
CH = 64
SUB = 16
CLAMP = 60.0 * GL_TAU
XA_H, XA_D = 4, 128
HEADS, NKEY, TOPK = 8, 128, 16
LAM_INIT = 0.8 - 0.6 * 1.0
SLOPE = [2.0 ** (-8.0 * (h + 1) / DA_H) for h in range(DA_H)]
MASKED = -1.0e30
LOWEST = -3.0e38

C_DAQ, C_DAK, C_DAV = 0, 512, 1024
C_GQK, C_GV, C_GR, C_GG = 1536, 2048, 2560, 3072
C_XQ, C_GATE = 3088, 3600
HALF = 512

K_ID, K_TRI, K_RESET, K_IOTA, K_DIST, K_QS, K_END = 0, 128, 192, 448, 464, 1488, 1496


def constant_table():
    c = np.zeros((P, K_END), np.float32)
    p = np.arange(P)[:, None]
    c[:, K_ID:K_TRI] = np.eye(P)
    c[:, K_TRI:K_RESET] = (p % CH) <= np.arange(CH)[None]
    c[:, K_RESET:K_IOTA] = (np.arange(T) % CH != 0)[None]
    c[:, K_IOTA:K_DIST] = np.arange(TOPK)[None]
    dist = np.arange(SEQ)[None] - (SEQ - P) - p
    c[:, K_DIST:K_QS] = np.where(dist <= 0, dist, MASKED)
    c[:, K_QS:K_END] = [DA_D ** -0.5 / SLOPE[m // 2] for m in range(2 * DA_H)]
    return c


def units():
    return [(t, h) for t in range(NT) for h in range(DA_H)]


def jobs_of(n):
    out = [("XT", n, t) for t in range(NT)]
    if n == 0:
        return out + [("MK", 0), ("MV", 0), ("MKT", 0)]
    out += [("Q", n), ("K", n), ("V", n)]
    out += [("QT", n, t) for t in range(NT)] + [("KT", n, t) for t in range(NT)]
    out += [("GQK", n), ("GG", n), ("GL", n), ("GV", n), ("GR", n), ("XQ", n)]
    out += [("XQT", n), ("XS", n, 0), ("XS", n, 1), ("XPT", n, 0), ("XO", n, 0), ("XPT", n, 1), ("XO", n, 1)]
    last = None
    for u in range(len(units())):
        out += [("S", n, u, 0), ("S", n, u, 1)]
        if u:
            out += [("WT", n, u - 1), ("OV", n, u - 1)]
        last = u
    out += [("WT", n, last), ("OV", n, last)]
    out += [("KD", n)] + [("AT", n, t) for t in range(NT)]
    for c in range(T // CH):
        out += [("GO", n, c), ("SU", n, c)]
    out += [("OT", n, 0), ("OT", n, 1)]
    for hf in range(2):
        for b in range(3):
            out += [("GATE", n, hf, b), ("BR", n, hf, b)]
    out += [("WO", n, 0), ("WO", n, 1)] + [("X2T", n, t) for t in range(NT)]
    out += [("WQ", n, 0), ("WQ", n, 1), ("SC", n, 0), ("WQ", n, 2), ("SC", n, 1), ("WQ", n, 3), ("SC", n, 2), ("SC", n, 3)]
    return out


NBANK = 3
JOBS = [job for n in range(STEPS + 1) for job in jobs_of(n)]
PLACE = {job: (i % NBANK, i // NBANK) for i, job in enumerate(JOBS)}

W_BLOCKS = [("mkv", 0, ("MK", 0)), ("mkv", 1, ("MV", 0))]
for _n in range(1, STEPS + 1):
    W_BLOCKS += [("in", C_DAQ, ("Q", _n)), ("in", C_DAK, ("K", _n)), ("in", C_DAV, ("V", _n)),
                 ("in", C_GQK, ("GQK", _n)), ("in", C_GV, ("GV", _n)), ("in", C_GR, ("GR", _n)),
                 ("in", C_XQ, ("XQ", _n))]
    for _hf in range(2):
        for _b in range(3):
            W_BLOCKS += [("in", C_GATE + _b * D + _hf * HALF, ("GATE", _n, _hf, _b)), (f"br{_b}", _hf, ("BR", _n, _hf, _b))]
    W_BLOCKS += [("out", nb, ("WO", _n, nb)) for nb in range(2)]
    W_BLOCKS += [("wq", j, ("WQ", _n, j)) for j in range(4)]
W_SLOTS = 2
W_AT = {user: i for i, (_, _, user) in enumerate(W_BLOCKS)}

NORMS = [("MK", 0)] + [(what, n) for n in range(1, STEPS + 1) for what in ("Q", "K", "XQ", "DA", "GLA")]

BATCH, RING = 2, 4
NB = HEADS * TOPK // BATCH


def build(nc, a):
    with ExitStack() as ctx:
        def sb(name, shape, dt=F32):
            return ctx.enter_context(nc.sbuf_tensor(name, shape, dt))

        def sem(name):
            return ctx.enter_context(nc.semaphore(name))

        consts = sb("consts", [P, K_END])
        ident = consts[:, K_ID:K_TRI]
        tri = consts[:, K_TRI:K_RESET]
        reset = consts[:, K_RESET:K_IOTA]
        iota = consts[:, K_IOTA:K_DIST]
        dist = consts[:, K_DIST:K_QS]
        qscale = consts[:, K_QS:K_END]
        eps = sb("eps", [P, 1])
        w_cols = sb("w_cols", [P, 2, KC])
        w_q64 = sb("w_q64", [P, DA_D])
        w_qs = sb("w_qs", [P, 2 * DA_H, DA_D])
        w_k64 = sb("w_k64", [P, DA_D])
        w_dao = sb("w_dao", [P, DA_V])
        w_glo = sb("w_glo", [P, GL_V])
        w_xq = sb("w_xq", [P, XA_D])
        w_xk = sb("w_xk", [P, XA_D])
        w_ffn = sb("w_ffn", [P, D])
        lam = sb("lam", [P, 4])
        b_gate = sb("b_gate", [P, 2])
        w_gate = sb("w_gate", [GL_R, GL_H * GL_K])
        w_gg = sb("w_gg", [P, KC, GL_R])
        keysT = sb("keysT", [P, 2, NKEY])
        mkT = sb("mkT", [P, XA_H, T])
        mv = sb("mv", [P, NT, XA_H * XA_D])
        kT = sb("kT", [P, DA_H, SEQ])
        V = sb("V", [P, SEQ // P, DA_H * DA_V])
        state = sb("state", [P, GL_H, GL_V])
        W = sb("W", [P, W_SLOTS, KC, HALF])
        xs = sb("xs", [P, NT, D])
        xnT = sb("xnT", [P, KC, T])
        oT_xa = sb("oT_xa", [P, 4, T])
        xn2 = sb("xn2", [P, NT, D])
        idx = sb("idx", [P, 2, NT, HEADS * TOPK], U32)
        gw = sb("gw", [P, 2, NT, HEADS * TOPK])
        st2 = sb("st2", [P, 8])
        hs = sb("hs", [P, 3, 16])
        small = sb("small", [P, 32])
        ub = sb("ub", [P, 2 * BATCH, D])
        vb = sb("vb", [P, 2 * BATCH, D])
        diag = sb("diag", [P, 2 * BATCH, P])
        stage = sb("stage", [P, RING, BATCH], U32)
        dots = sb("dots", [P, RING, BATCH])
        acts = sb("acts", [P, RING, BATCH])
        fin = sb("fin", [P, D])
        gebl = sb("gebl", [P, 8])
        gv = sb("gv", [P, NT, GL_H * GL_V])
        gr = sb("gr", [P, NT, GL_H * GL_V])
        qT = sb("qT", [P, DA_H, T])
        tv = sb("tv", [P, NT, 16, TOPK])
        ti = sb("ti", [P, NT, 16, TOPK], U32)
        bj = sb("bj", [P, 2, HEADS, TOPK], U32)
        AREA = 6144
        arena = sb("arena", [P, AREA])

        def parts(x, *shape):
            names = "abcd"[:len(shape)]
            if len(shape) == 1:
                return x
            return x.rearrange(f"p ({' '.join(names)}) -> p {' '.join(names)}", **{c: s for c, s in zip(names[1:], shape[1:])})

        def area(at, *shape):
            assert at + int(np.prod(shape)) <= AREA
            return parts(arena[:, at:at + int(np.prod(shape))], *shape)

        sq = area(AREA - 1024, 1024)
        wT = area(AREA - 1024, SEQ)
        xhat = area(0, NT, D)
        lam_in = area(2048, 4 * DA_D)
        gqk = area(0, 4, T)
        gb = area(1024, 2, T)
        qn = area(1536, NT, 2 * DA_H, DA_D)
        kn = area(2560, NT, 2 * DA_H, DA_D)
        xq = area(3584, NT, XA_H, XA_D)
        ggT = area(4608, T)[0:GL_R, :]
        xqT = area(1536, XA_H, T)
        px = area(2560, XA_H, T)
        pxT = area(3584, XA_H, 2, P)
        pw = area(1536, 2, SEQ)
        p1 = area(3584, SEQ)
        oda = parts(xs[:, 0, :], NT, DA_H, DA_V)
        ogl = parts(xs[:, 1, :], NT, GL_H, GL_V)
        gqi = area(1536, 2, T)
        gqt = area(2048, 2, T)
        gkt = area(2560, 2, 4, 256)
        gkd = area(4608, 2, T)
        kdT = area(0, NT, 2, P)
        at_s = area(512, NT, 2, GL_H, CH)
        oT = [area(4096, 4, T), area(5120, 4, T), oT_xa]
        merged = area(0, KC, T)
        sg = area(2048, 4, T)
        tmp = area(3072, 4, T)
        sc = area(0, NT, 4, NKEY)
        xn2T = area(1024, KC, T)
        qp = area(3072, 2, 4 * T)
        cand = area(1024, HEADS, TOPK, TOPK)
        bv = area(3072, HEADS, TOPK)
        bf = area(3200, 6, HEADS, TOPK)
        tif = area(3968, 16, TOPK)

        bank = [ctx.enter_context(nc.psum_tensor(f"bank{i}", [P, 1024], F32)) for i in range(NBANK)]
        acc = ctx.enter_context(nc.psum_tensor("acc", [P, D], F32))

        bank_full = [sem(f"bank_full{i}") for i in range(NBANK)]
        bank_free = [sem(f"bank_free{i}") for i in range(NBANK)]
        consts_in = sem("consts_in")
        x_in = [sem(f"x_in{t}") for t in range(NT)]
        w_in = [sem(f"w_in{i}") for i in range(W_SLOTS)]
        x1_out = sem("x1_out")
        fin_in = sem("fin_in")
        y_out = sem("y_out")
        const_ready = sem("const_ready")
        lam_exp = sem("lam_exp")
        norm_sq = sem("norm_sq")
        norm_rs = sem("norm_rs")
        xhat_ready = sem("xhat_ready")
        hn_sq = sem("hn_sq")
        hn_ss = sem("hn_ss")
        hn_rt = sem("hn_rt")
        hn_done = sem("hn_done")
        sig_ready = sem("sig_ready")
        gla_ln = sem("gla_ln")
        gla_args = sem("gla_args")
        gla_exps = sem("gla_exps")
        gla_ops = sem("gla_ops")
        gr_ready = sem("gr_ready")
        state_zero = sem("state_zero")
        smax_ready = sem("smax_ready")
        wgt_ready = sem("wgt_ready")
        xmax_ready = sem("xmax_ready")
        px_ready = sem("px_ready")
        gate_used = sem("gate_used")
        merged_ready = sem("merged_ready")
        xn2_ready = sem("xn2_ready")
        top_done = sem("top_done")
        sm_arg = sem("sm_arg")
        sm_exp = sem("sm_exp")
        route_done = sem("route_done")
        staged = sem("staged")
        u_landed = [sem(f"u_landed{k}") for k in range(2 * BATCH)]
        v_landed = [sem(f"v_landed{k}") for k in range(2 * BATCH)]
        dot_done = sem("dot_done")
        gelu_done = sem("gelu_done")
        diag_ready = sem("diag_ready")
        rows_added = sem("rows_added")
        y_ready = sem("y_ready")
        act_own = sem("act_own")
        dve_own = sem("dve_own")

        def claim(eng, job):
            b, n = PLACE[job]
            if n:
                eng.wait_ge(bank_free[b], n)
            return bank[b], bank_full[b]

        def filled(job):
            b, n = PLACE[job]
            return bank_full[b], n + 1

        def evacuated(job):
            b, n = PLACE[job]
            return bank_free[b], n + 1

        def free_sem(job):
            return bank_free[PLACE[job][0]]

        def view(job, *shape):
            return parts(bank[PLACE[job][0]][:, 0:int(np.prod(shape))], *shape)

        def hold(eng, s, value):
            if not isinstance(value, int):
                value = eng.to_reg(value)
                eng.wait_ge(consts_in, 16)
            eng.wait_ge(s, value)

        def w_slot(user):
            i = W_AT[user]
            return W[:, i % W_SLOTS, :, :], w_in[i % W_SLOTS], 16 * (i // W_SLOTS + 1)

        def norm_no(what, n):
            return NORMS.index((what, n)) + 1

        def landed(b, q):
            return (b - q % 2) * 8 + 16

        block = ctx.enter_context(nc.Block())

        CONST_LOADS = [
            (consts[:, :], a["consts"]), (w_cols[:, 0, :], a["mem_w"]), (w_cols[:, 1, :], a["mix_w"]),
            (w_q64[:, :], a["q_w"].partition_broadcast(P)), (w_k64[:, :], a["k_w"].partition_broadcast(P)),
            (w_dao[:, :], a["dao_w"].partition_broadcast(P)), (w_glo[:, :], a["glo_w"].partition_broadcast(P)),
            (w_xq[:, :], a["xq_w"].partition_broadcast(P)), (w_xk[:, :], a["xk_w"].partition_broadcast(P)),
            (w_ffn[:, :], a["ffn_w"].partition_broadcast(P)), (lam_in[:, :], a["lam"].partition_broadcast(P)),
            (b_gate[:, :], a["b_gate"]), (w_gate[:, :], a["w_gate"]),
            (w_gg[:, :, :], a["w_in"][:, C_GG:C_GG + GL_R].rearrange("(k p) n -> p k n", p=P)),
            (keysT[:, :, :], a["keysT"]),
        ]
        N_CONST = 16 * len(CONST_LOADS)
        x_tiles = a["x"].rearrange("(g p) d -> g p d", p=P)
        mem_tiles = a["mem"].rearrange("(g p) d -> g p d", p=P)
        y_tiles = a["y"].rearrange("(g p) d -> g p d", p=P)
        w_dram = {"in": a["w_in"].rearrange("(k p) n -> p k n", p=P), "mkv": a["w_mkv"].rearrange("(k p) n -> p k n", p=P),
                  **{f"br{b}": a[f"br{b}"].rearrange("(k p) n -> p k n", p=P) for b in range(3)},
                  "out": a["w_out"].rearrange("(k p) n -> p k n", p=P), "wq": a["w_q"].rearrange("(k p) n -> p k n", p=P)}

        @block.sync
        def _(sp):
            for dst, src in CONST_LOADS:
                sp.dma_start(dst, src).then_inc(consts_in, 16)
            loaded = [0]

            def load_blocks(n_blocks):
                for i in range(loaded[0], loaded[0] + n_blocks):
                    kind, where, _ = W_BLOCKS[i]
                    if i >= W_SLOTS:
                        sp.wait_ge(*filled(W_BLOCKS[i - W_SLOTS][2]))
                    at = where if kind == "in" else where * HALF
                    rows = w_dram[kind].shape[1]
                    sp.dma_start(W[:, i % W_SLOTS, 0:rows, :], w_dram[kind][:, :, at:at + HALF]).then_inc(w_in[i % W_SLOTS], 16)
                loaded[0] += n_blocks

            for n in range(STEPS + 1):
                for t in range(NT):
                    if n > 1:
                        sp.wait_ge(x1_out, 16 * NT * (n - 1))
                        sp.wait_ge(xn2_ready, NT * (n - 1))
                    elif n == 1:
                        sp.wait_ge(xhat_ready, t + 1)
                    src = mem_tiles[t] if n == 0 else x_tiles[NT * (n - 1) + t]
                    sp.dma_start(xs[:, t, :], src).then_inc(x_in[t], 16)
                if n == 0:
                    load_blocks(2)
                    continue
                load_blocks(7 + 2)
                sp.wait_ge(*filled(("OT", n, 1)))
                for t in range(NT):
                    sp.dma_start(xs[:, t, :], x_tiles[NT * (n - 1) + t]).then_inc(x_in[t], 16)
                load_blocks(10 + 2)
                sp.wait_ge(*evacuated(("WO", n, 1)))
                for t in range(NT):
                    sp.dma_start(y_tiles[NT * (n - 1) + t], xs[:, t, :]).then_inc(x1_out, 16)
                load_blocks(4)
                for t in range(NT):
                    g = NT * (n - 1) + t
                    sp.wait_ge(x1_out, 16 * NT * n)
                    if g:
                        sp.wait_ge(y_out, 16 * g)
                    sp.dma_start(fin[:, :], y_tiles[g]).then_inc(fin_in, 16)
                    sp.wait_ge(y_ready, g + 1)
                    sp.dma_start(y_tiles[g], fin[:, :]).then_inc(y_out, 16)
            sp.wait_ge(y_out, 16 * SEQ // P)

        @block.gpsimd
        def _(pool):
            def gather_u(b, q):
                hold(pool, staged, b + 1)
                for k in range(BATCH):
                    if not isinstance(b, int) or b >= 2:
                        hold(pool, dot_done, (b - 2) * BATCH + k + 1)
                    s = (q % 2) * BATCH + k
                    pool.indirect_dma_start(ub[:, s, :], None, a["peer_u"],
                                            bass.IndirectOffsetOnAxis(ap=stage[:, q, k:k + 1], axis=0)).then_inc(u_landed[s], 16)

            def gather_v(b, q):
                if not isinstance(b, int) or b >= 2:
                    hold(pool, rows_added, b - 1)
                for k in range(BATCH):
                    s = (q % 2) * BATCH + k
                    pool.indirect_dma_start(vb[:, s, :], None, a["peer_v"],
                                            bass.IndirectOffsetOnAxis(ap=stage[:, q, k:k + 1], axis=0)).then_inc(v_landed[s], 16)

            pool.wait_ge(consts_in, N_CONST)
            for g in range(SEQ // P):
                first = g * NB
                for q in range(RING):
                    gather_u(first + q, q)
                    gather_v(first + q, q)
                with pool.Fori(1, NB // RING) as j:
                    for q in range(RING):
                        gather_u(j * RING + (first + q), q)
                        gather_v(j * RING + (first + q), q)

        @block.tensor
        def _(pe):
            def token_major(job, user, out_of):
                ps, full = claim(pe, job)
                w, s, v = w_slot(user)
                pe.wait_ge(s, v)
                for t in range(NT):
                    for k in range(KC):
                        mm = pe.matmul(ps[:, t * HALF:(t + 1) * HALF], out_of[:, k, t * P:(t + 1) * P], w[:, k, :],
                                       start=k == 0, stop=k == KC - 1)
                mm.then_inc(full, 1)

            def channel_major(job, user, rhs):
                ps, full = claim(pe, job)
                w, s, v = w_slot(user)
                pe.wait_ge(s, v)
                for c in range(4):
                    for k in range(KC):
                        mm = pe.matmul(ps[:, c * T:(c + 1) * T], w[:, k, c * P:(c + 1) * P], rhs[:, k, :],
                                       start=k == 0, stop=k == KC - 1)
                mm.then_inc(full, 1)

            def turn(job, blocks, after):
                ps, full = claim(pe, job)
                for w in after:
                    pe.wait_ge(*w)
                for i, src in enumerate(blocks):
                    mm = pe.transpose(ps[:, i * P:(i + 1) * P], src, ident)
                mm.then_inc(full, 1)

            def project(n):
                token_major(("Q", n), ("Q", n), xnT)
                token_major(("K", n), ("K", n), xnT)
                token_major(("V", n), ("V", n), xnT)
                for t in range(NT):
                    turn(("QT", n, t), [qn[:, t, 2 * h:2 * h + 2, :].rearrange("p a b -> p (a b)") for h in range(DA_H)],
                         [(hn_done, norm_no("Q", n))])
                for t in range(NT):
                    turn(("KT", n, t), [kn[:, t, 2 * h:2 * h + 2, :].rearrange("p a b -> p (a b)") for h in range(DA_H)],
                         [(hn_done, norm_no("K", n))])
                channel_major(("GQK", n), ("GQK", n), xnT)
                ps, full = claim(pe, ("GG", n))
                for k in range(KC):
                    mm = pe.matmul(ps[0:GL_R, 0:T], w_gg[:, k, :], xnT[:, k, :], start=k == 0, stop=k == KC - 1)
                mm.then_inc(full, 1)
                ps, full = claim(pe, ("GL", n))
                pe.wait_ge(*evacuated(("GG", n)))
                for hp in range(2):
                    mm = pe.matmul(ps[:, hp * T:(hp + 1) * T], w_gate[:, hp * P:(hp + 1) * P], ggT, start=True, stop=True)
                mm.then_inc(full, 1)
                token_major(("GV", n), ("GV", n), xnT)
                token_major(("GR", n), ("GR", n), xnT)
                token_major(("XQ", n), ("XQ", n), xnT)

            def memory_attention(n):
                turn(("XQT", n), [xq[:, t, h, :] for h in range(XA_H) for t in range(NT)], [(hn_done, norm_no("XQ", n))])
                for t in range(NT):
                    ps, full = claim(pe, ("XS", n, t))
                    pe.wait_ge(*evacuated(("XQT", n)))
                    for h in range(XA_H):
                        mm = pe.matmul(ps[:, h * T:(h + 1) * T], xqT[:, h, t * P:(t + 1) * P], mkT[:, h, :], start=True, stop=True)
                    mm.then_inc(full, 1)
                for t in range(NT):
                    turn(("XPT", n, t), [px[:, h, m * P:(m + 1) * P] for h in range(XA_H) for m in range(2)],
                         [(px_ready, NT * (n - 1) + t + 1)])
                    ps, full = claim(pe, ("XO", n, t))
                    pe.wait_ge(*evacuated(("XPT", n, t)))
                    for h in range(XA_H):
                        for m in range(2):
                            mm = pe.matmul(ps[:, h * P:(h + 1) * P], mv[:, m, h * XA_D:(h + 1) * XA_D], pxT[:, h, m, :],
                                           start=m == 0, stop=m == 1)
                    mm.then_inc(full, 1)

            def diff_attention(n):
                us = units()

                def scores(u):
                    t, h = us[u]
                    cols = (NT * (n - 1) + t + 1) * P
                    for m in range(2):
                        ps, full = claim(pe, ("S", n, u, m))
                        if u == 0 and m == 0:
                            pe.wait_ge(*evacuated(("QT", n, 1)))
                            pe.wait_ge(*evacuated(("KT", n, 1)))
                        rows = slice(DA_D * m, DA_D * (m + 1))
                        for c in range(0, cols, HALF):
                            w = min(HALF, cols - c)
                            mm = pe.matmul(ps[:, c:c + w], qT[rows, h, t * P:(t + 1) * P], kT[rows, h, c:c + w], start=True, stop=True)
                        mm.then_inc(full, 1)

                def values(u):
                    t, h = us[u]
                    nb = NT * (n - 1) + t + 1
                    turn(("WT", n, u), [pw[:, u % 2, k * P:(k + 1) * P] for k in range(nb)],
                         [(wgt_ready, len(us) * (n - 1) + u + 1)])
                    ps, full = claim(pe, ("OV", n, u))
                    pe.wait_ge(*evacuated(("WT", n, u)))
                    for k in range(nb):
                        mm = pe.matmul(ps[:, 0:P], wT[:, k * P:(k + 1) * P], V[:, k, h * DA_V:(h + 1) * DA_V], start=k == 0, stop=k == nb - 1)
                    mm.then_inc(full, 1)

                for u in range(len(us)):
                    scores(u)
                    if u:
                        values(u - 1)
                values(len(us) - 1)

            def gla(n):
                turn(("KD", n), [gkd[:, hp, t * P:(t + 1) * P] for t in range(NT) for hp in range(2)], [(gla_ops, n)])
                for t in range(NT):
                    ps, full = claim(pe, ("AT", n, t))
                    for c2 in range(2):
                        c = 2 * t + c2
                        for h in range(GL_H):
                            rows = slice(GL_K * (h % 2), GL_K * (h % 2 + 1))
                            for i in range(CH // SUB):
                                at = (h % 2) * HALF + (h // 2) * CH + i * SUB
                                mm = pe.matmul(ps[CH * c2:CH * (c2 + 1), at:at + SUB],
                                               gkt[rows, h // 2, c, i * CH:(i + 1) * CH],
                                               gqt[rows, h // 2, c * CH + i * SUB:c * CH + (i + 1) * SUB], start=True, stop=True)
                    mm.then_inc(full, 1)
                for c in range(T // CH):
                    t, c2 = c // 2, c % 2
                    tok = slice(CH * c2, CH * (c2 + 1))
                    ps, full = claim(pe, ("GO", n, c))
                    if c == 0:
                        pe.wait_ge(*evacuated(("KD", n)))
                        pe.wait_ge(*evacuated(("GV", n)))
                        pe.wait_ge(*(evacuated(("SU", n - 1, T // CH - 1)) if n > 1 else (state_zero, 1)))
                    else:
                        pe.wait_ge(*evacuated(("SU", n, c - 1)))
                    pe.wait_ge(*evacuated(("AT", n, t)))
                    for h in range(GL_H):
                        pe.matmul(ps[tok, h * GL_V:(h + 1) * GL_V], gqi[:, h // 2, c * CH:(c + 1) * CH], state[:, h, :],
                                  start=True, stop=False)
                        mm = pe.matmul(ps[tok, h * GL_V:(h + 1) * GL_V], at_s[:, t, c2, h, :], gv[:, t, h * GL_V:(h + 1) * GL_V],
                                       start=False, stop=True)
                    mm.then_inc(full, 1)
                    ps, full = claim(pe, ("SU", n, c))
                    for h in range(GL_H):
                        rows = slice(GL_K * (h % 2), GL_K * (h % 2 + 1))
                        mm = pe.matmul(ps[rows, (h // 2) * GL_V:(h // 2 + 1) * GL_V], kdT[tok, t, h // 2, GL_K * (h % 2):GL_K * (h % 2 + 1)],
                                       gv[tok, t, h * GL_V:(h + 1) * GL_V], start=True, stop=True)
                    mm.then_inc(full, 1)

            def merge(n):
                turn(("OT", n, 0), [oda[:, t, h, :] for h in range(4) for t in range(NT)], [(hn_done, norm_no("DA", n))])
                turn(("OT", n, 1), [ogl[:, t, h, :] for h in range(4) for t in range(NT)], [(hn_done, norm_no("GLA", n))])
                for hf in range(2):
                    for b in range(3):
                        channel_major(("GATE", n, hf, b), ("GATE", n, hf, b), xnT)
                        ps, full = claim(pe, ("BR", n, hf, b))
                        w, s, v = w_slot(("BR", n, hf, b))
                        pe.wait_ge(s, v)
                        pe.wait_ge(*evacuated(("OT", n, b) if b < 2 else ("XO", n, 1)))
                        for c in range(4):
                            for k in range(4):
                                mm = pe.matmul(ps[:, c * T:(c + 1) * T], w[:, k, c * P:(c + 1) * P], oT[b][:, k, :], start=k == 0, stop=k == 3)
                        mm.then_inc(full, 1)
                pe.wait_ge(merged_ready, n)
                for nb in range(2):
                    token_major(("WO", n, nb), ("WO", n, nb), merged)

            def route(n):
                for t in range(NT):
                    turn(("X2T", n, t), [xn2[:, t, k * P:(k + 1) * P] for k in range(KC)], [(xn2_ready, NT * (n - 1) + t + 1)])

                def score(j):
                    ps, full = claim(pe, ("SC", n, j))
                    pe.wait_ge(*evacuated(("WQ", n, j)))
                    for t in range(NT):
                        for i in range(4):
                            mm = pe.matmul(ps[:, (4 * t + i) * NKEY:(4 * t + i + 1) * NKEY], qp[:, j % 2, i * T + t * P:i * T + (t + 1) * P],
                                           keysT[:, i % 2, :], start=True, stop=True)
                    mm.then_inc(full, 1)

                pe.wait_ge(*evacuated(("X2T", n, 1)))
                for j in range(4):
                    channel_major(("WQ", n, j), ("WQ", n, j), xn2T)
                    if j:
                        score(j - 1)
                score(3)

            def add_rows(b, q, start=False, stop=False):
                hold(pe, diag_ready, b + 1)
                for k in range(BATCH):
                    s = (q % 2) * BATCH + k
                    hold(pe, v_landed[s], landed(b, q))
                    for c in range(2):
                        mm = pe.matmul(acc[:, c * HALF:(c + 1) * HALF], diag[:, s, :], vb[:, s, c * HALF:(c + 1) * HALF],
                                       start=start and k == 0, stop=stop and k == BATCH - 1)
                mm.then_inc(rows_added, 1)

            def experts(g):
                first = g * NB
                if g:
                    pe.wait_ge(y_ready, g)
                for q in range(RING):
                    add_rows(first + q, q, start=q == 0)
                with pe.Fori(1, NB // RING - 1) as j:
                    for q in range(RING):
                        add_rows(j * RING + (first + q), q)
                for q in range(RING):
                    add_rows(first + NB - RING + q, q, stop=q == RING - 1)

            pe.wait_ge(consts_in, N_CONST)
            for n in range(STEPS + 1):
                for t in range(NT):
                    turn(("XT", n, t), [xhat[:, t, k * P:(k + 1) * P] for k in range(KC)], [(xhat_ready, NT * n + t + 1)])
                pe.wait_ge(*evacuated(("XT", n, 1)))
                if n == 0:
                    token_major(("MK", 0), ("MK", 0), xnT)
                    token_major(("MV", 0), ("MV", 0), xnT)
                    turn(("MKT", 0), [xq[:, t, h, :] for h in range(XA_H) for t in range(NT)], [(hn_done, 1)])
                    continue
                project(n)
                memory_attention(n)
                diff_attention(n)
                gla(n)
                merge(n)
                route(n)
                for t in range(NT):
                    experts(NT * (n - 1) + t)

        @block.scalar
        def _(act):
            own = [0]

            def after(ins):
                own[0] += 1
                ins.then_inc(act_own, 1)
                act.wait_ge(act_own, own[0])

            def copy(job, dst, *shape):
                act.wait_ge(*filled(job))
                act.activation(dst, view(job, *shape), ACT.Copy).then_inc(free_sem(job), 1)

            def norm_rows(which, ready):
                for t in range(NT):
                    act.wait_ge(*ready[t])
                    after(act.activation(sq, xs[:, t, :], ACT.Square, accum_out=st2[:, t:t + 1]))
                act.activation(st2[:, 2:4], st2[:, 0:2], ACT.Sqrt, scale=1.0 / D, bias=eps[:, 0:1]).then_inc(norm_sq, 1)

            def norm_heads(no, src, ready, groups, width):
                act.wait_ge(*ready)
                if no > 1:
                    act.wait_ge(hn_ss, no - 1)
                act.activation(sq, src, ACT.Square).then_inc(hn_sq, 1)
                act.wait_ge(hn_ss, no)
                act.activation(hs[:, 1, 0:groups], hs[:, 0, 0:groups], ACT.Sqrt, scale=1.0 / width, bias=eps[:, 0:1]).then_inc(hn_rt, 1)

            def project(n):
                norm_heads(norm_no("Q", n), view(("Q", n), 1024), filled(("Q", n)), 16, DA_D)
                norm_heads(norm_no("K", n), view(("K", n), 1024), filled(("K", n)), 16, DA_D)
                g = NT * (n - 1)
                copy(("V", n), V[:, g:g + NT, :].rearrange("p a b -> p (a b)"), 1024)
                for t in range(NT):
                    copy(("QT", n, t), qT[:, :, t * P:(t + 1) * P], DA_H, P)
                for t in range(NT):
                    copy(("KT", n, t), kT[:, :, (g + t) * P:(g + t + 1) * P], DA_H, P)
                copy(("GQK", n), gqk.rearrange("p a b -> p (a b)"), 1024)
                act.wait_ge(*filled(("GG", n)))
                act.activation(ggT, view(("GG", n), T)[0:GL_R, :], ACT.Copy).then_inc(free_sem(("GG", n)), 1)
                act.wait_ge(*filled(("GL", n)))
                for hp in range(2):
                    ins = act.activation(gb[:, hp, :], view(("GL", n), 2, T)[:, hp, :], ACT.Identity, bias=b_gate[:, hp:hp + 1])
                ins.then_inc(free_sem(("GL", n)), 1)
                copy(("GV", n), gv[:, :, :].rearrange("p a b -> p (a b)"), 1024)
                act.wait_ge(*filled(("GR", n)))
                act.activation(gr[:, :, :].rearrange("p a b -> p (a b)"), view(("GR", n), 1024), ACT.Sigmoid).then_inc(sig_ready, 1)
                norm_heads(norm_no("XQ", n), view(("XQ", n), 1024), filled(("XQ", n)), 8, XA_D)

            def gla_prepare(n):
                a1 = gqi.rearrange("p a b -> p (a b)")
                act.wait_ge(*evacuated(("GL", n)))
                act.wait_ge(*evacuated(("OV", n, 7)))
                after(act.activation(a1, gb.rearrange("p a b -> p (a b)"), ACT.Abs))
                after(act.activation(a1, a1, ACT.Exp, scale=-1.0))
                act.activation(a1, a1, ACT.Ln, bias=1.0).then_inc(gla_ln, 1)
                act.wait_ge(gla_args, n)
                act.activation(a1, gb.rearrange("p a b -> p (a b)"), ACT.Exp, scale=1.0 / GL_TAU)
                a2 = gqt.rearrange("p a b -> p (a b)")
                act.activation(a2, a2, ACT.Exp, scale=1.0 / GL_TAU)
                a3 = gkt.rearrange("p a b c -> p (a b c)")
                act.activation(a3, a3, ACT.Exp, scale=1.0 / GL_TAU)
                a4 = gkd.rearrange("p a b -> p (a b)")
                act.activation(a4, a4, ACT.Exp, scale=1.0 / GL_TAU)
                last = gb.rearrange("p a (c s) -> p (a c) s", s=CH)[:, :, CH - 1]
                act.activation(gebl[:, :], last, ACT.Exp, scale=1.0 / GL_TAU).then_inc(gla_exps, 1)

            def memory_attention(n):
                copy(("XQT", n), xqT.rearrange("p a b -> p (a b)"), 1024)
                for t in range(NT):
                    job = ("XS", n, t)
                    act.wait_ge(xmax_ready, NT * (n - 1) + t + 1)
                    if t:
                        act.wait_ge(*filled(("XPT", n, t - 1)))
                    for h in range(XA_H):
                        ins = act.activation(px[:, h, :], view(job, XA_H, T)[:, h, :], ACT.Exp, scale=XA_D ** -0.5,
                                             bias=small[:, 4 + h:5 + h], accum_out=small[:, 8 + h:9 + h])
                    ins.then_inc(free_sem(job), 1)
                    copy(("XPT", n, t), pxT.rearrange("p a b c -> p (a b c)"), 1024)
                    copy(("XO", n, t), oT[2][:, :, t * P:(t + 1) * P], 4, P)

            def diff_attention(n):
                us = units()

                def exps(u):
                    t, h = us[u]
                    cols = (NT * (n - 1) + t + 1) * P
                    for m in range(2):
                        job = ("S", n, u, m)
                        act.wait_ge(smax_ready, 16 * (n - 1) + 2 * u + m + 1)
                        if m == 0 and u >= 2:
                            act.wait_ge(*filled(("WT", n, u - 2)))
                        if m == 1 and u:
                            act.wait_ge(wgt_ready, 8 * (n - 1) + u)
                        dst = pw[:, u % 2, 0:cols] if m == 0 else p1[:, 0:cols]
                        act.activation(dst, view(job, cols), ACT.Exp, scale=SLOPE[h], bias=small[:, 14 + 2 * (u % 2) + m:15 + 2 * (u % 2) + m],
                                       accum_out=small[:, 18 + 2 * (u % 2) + m:19 + 2 * (u % 2) + m]).then_inc(free_sem(job), 1)

                def evacuate(u):
                    t, h = us[u]
                    cols = (NT * (n - 1) + t + 1) * P
                    copy(("WT", n, u), wT[:, 0:cols], cols)

                for u in range(len(us)):
                    exps(u)
                    if u:
                        evacuate(u - 1)
                evacuate(len(us) - 1)

            def gla(n):
                copy(("KD", n), kdT.rearrange("p a b c -> p (a b c)"), 512)
                for c in range(T // CH):
                    t, c2 = c // 2, c % 2
                    tok = slice(CH * c2, CH * (c2 + 1))
                    job = ("GO", n, c)
                    act.wait_ge(*filled(job))
                    act.activation(ogl[tok, t, :, :].rearrange("p a b -> p (a b)"), view(job, 512)[tok, :], ACT.Copy).then_inc(free_sem(job), 1)

            def merge(n):
                norm_heads(norm_no("DA", n), oda[:, :, :, :].rearrange("p a b c -> p (a b c)"), evacuated(("OV", n, 7)), 8, DA_V)
                act.wait_ge(*evacuated(("GO", n, T // CH - 1)))
                norm_heads(norm_no("GLA", n), ogl[:, :, :, :].rearrange("p a b c -> p (a b c)"), evacuated(("GO", n, T // CH - 1)), 8, GL_V)
                copy(("OT", n, 0), oT[0].rearrange("p a b -> p (a b)"), 1024)
                copy(("OT", n, 1), oT[1].rearrange("p a b -> p (a b)"), 1024)
                for i in range(6):
                    job = ("GATE", n, i // 3, i % 3)
                    act.wait_ge(*filled(job))
                    if i:
                        act.wait_ge(*evacuated(("BR", n, (i - 1) // 3, (i - 1) % 3)))
                    act.activation(sg.rearrange("p a b -> p (a b)"), view(job, 1024), ACT.Sigmoid).then_inc(free_sem(job), 1)

            def route(n):
                norm_rows(None, [evacuated(("WO", n, 1))] * NT)
                for t in range(NT):
                    copy(("X2T", n, t), xn2T[:, :, t * P:(t + 1) * P], KC, P)

                def scores(j):
                    if j:
                        act.wait_ge(top_done, 4 * (n - 1) + j)
                    copy(("SC", n, j), sc.rearrange("p a b c -> p (a b c)"), 1024)

                for j in range(4):
                    copy(("WQ", n, j), qp[:, j % 2, :], 1024)
                    if j:
                        scores(j - 1)
                scores(3)
                for t in range(NT):
                    i = NT * (n - 1) + t + 1
                    act.wait_ge(sm_arg, i)
                    act.activation(bf[:, 4, :, :].rearrange("p a b -> p (a b)"), bf[:, 4, :, :].rearrange("p a b -> p (a b)"), ACT.Exp).then_inc(sm_exp, 1)

            def gelu(b, q):
                hold(act, dot_done, b * BATCH + BATCH)
                act.activation(acts[:, q, :], dots[:, q, :], ACT.Gelu).then_inc(gelu_done, 1)

            act.wait_ge(const_ready, 1)
            act.activation(lam[:, 2:4], lam[:, 0:2], ACT.Exp).then_inc(lam_exp, 1)
            for n in range(STEPS + 1):
                norm_rows(n, [(x_in[t], 16 * max(2 * n, 1)) for t in range(NT)])
                act.wait_ge(norm_rs, n + 1)
                for t in range(NT):
                    act.activation(xhat[:, t, :], xs[:, t, :], ACT.Copy, scale=st2[:, 4 + t:5 + t]).then_inc(xhat_ready, 1)
                if n == 0:
                    norm_heads(1, view(("MK", 0), 1024), filled(("MK", 0)), 8, XA_D)
                    copy(("MV", 0), mv[:, :, :].rearrange("p a b -> p (a b)"), 1024)
                    copy(("MKT", 0), mkT[:, :, :].rearrange("p a b -> p (a b)"), 1024)
                    continue
                project(n)
                memory_attention(n)
                diff_attention(n)
                gla_prepare(n)
                gla(n)
                merge(n)
                route(n)
                for t in range(NT):
                    first = (NT * (n - 1) + t) * NB
                    with act.Fori(0, NB // RING) as j:
                        for q in range(RING):
                            gelu(j * RING + (first + q), q)

        @block.vector
        def _(dve):
            own = [0]

            def after(ins):
                own[0] += 1
                ins.then_inc(dve_own, 1)
                dve.wait_ge(dve_own, own[0])

            def flat(x):
                names = "abcd"[:len(x.shape) - 1]
                return x.rearrange(f"p {' '.join(names)} -> p ({' '.join(names)})")

            def wide(x, *shape):
                return x.broadcast_to([x.shape[0], *shape])

            def norm_rows(no):
                dve.wait_ge(norm_sq, no)
                ins = dve.reciprocal(st2[:, 4:6], st2[:, 2:4])
                return ins

            def norm_heads(no, src, dst, groups, width, weight, release=None):
                dve.wait_ge(hn_sq, no)
                dve.tensor_reduce(hs[:, 0, 0:groups], sq.rearrange("p (g d) -> p g d", d=width), AX, ALU.add).then_inc(hn_ss, 1)
                dve.wait_ge(hn_rt, no)
                after(dve.reciprocal(hs[:, 2, 0:groups], hs[:, 1, 0:groups]))
                ins = dve.tensor_tensor(dst, src, wide(hs[:, 2, 0:groups].unsqueeze(2), groups, width), ALU.mult)
                if release is not None:
                    ins.then_inc(free_sem(release), 1)
                    dve.wait_ge(*evacuated(release))
                else:
                    after(ins)
                dve.tensor_tensor(weight[0](dst), weight[0](dst), weight[1], ALU.mult).then_inc(hn_done, 1)

            def grouped(x):
                return x

            def by_tile(x):
                return x.rearrange("p (t g) d -> p t g d", t=NT)

            def heads_of(x):
                return x.rearrange("p a b c -> p (a b) c")

            def project(n):
                norm_heads(norm_no("Q", n), view(("Q", n), 16, DA_D), heads_of(qn), 16, DA_D,
                           (by_tile, wide(w_qs[:, :, :].unsqueeze(1), NT, 2 * DA_H, DA_D)), ("Q", n))
                norm_heads(norm_no("K", n), view(("K", n), 16, DA_D), heads_of(kn), 16, DA_D,
                           (grouped, wide(w_k64[:, :].unsqueeze(1), 16, DA_D)), ("K", n))
                job = ("GR", n)
                dve.wait_ge(sig_ready, n)
                g2 = flat(gr[:, :, :])
                dve.tensor_tensor(g2, view(job, 1024), g2, ALU.mult).then_inc(free_sem(job), 1)
                dve.wait_ge(*evacuated(job))
                g3 = gr[:, :, :].rearrange("p t (h d) -> p (t h) d", d=GL_V)
                dve.tensor_tensor(g3, g3, wide(w_glo[:, :].unsqueeze(1), 8, GL_V), ALU.mult).then_inc(gr_ready, 1)
                norm_heads(norm_no("XQ", n), view(("XQ", n), 8, XA_D), heads_of(xq), 8, XA_D,
                           (grouped, wide(w_xq[:, :].unsqueeze(1), 8, XA_D)), ("XQ", n))

            def gla_prepare(n):
                dve.wait_ge(gla_ln, n)
                after(dve.scalar_tensor_tensor(flat(gqt), flat(gb), 0.0, flat(gqi), ALU.min, ALU.subtract))
                for hp in range(2):
                    ins = dve.tensor_tensor_scan(gb[:, hp, :], reset, gqt[:, hp, :], 0.0, ALU.mult, ALU.add)
                after(ins)
                blocks = gb.rearrange("p a (i s) -> p (a i) s", s=SUB)
                ref = blocks[:, :, SUB // 2]
                dve.tensor_tensor(gqt.rearrange("p a (i s) -> p (a i) s", s=SUB), blocks,
                                  wide(ref.unsqueeze(2), 2 * T // SUB, SUB), ALU.subtract)
                chunks = gb.rearrange("p a (c s) -> p a c s", s=CH)
                for hp in range(2):
                    r = gb[:, hp, :].rearrange("p (c i s) -> p c i s", i=CH // SUB, s=SUB)[:, :, :, SUB // 2]
                    dve.tensor_tensor(gkt[:, hp, :, :].rearrange("p c (i s) -> p c i s", s=CH),
                                      wide(r.unsqueeze(3), T // CH, CH // SUB, CH),
                                      wide(chunks[:, hp, :, :].unsqueeze(2), T // CH, CH // SUB, CH), ALU.subtract)
                c2 = gb.rearrange("p a (c s) -> p (a c) s", s=CH)
                after(dve.tensor_tensor(gkd.rearrange("p a (c s) -> p (a c) s", s=CH), wide(c2[:, :, CH - 1:CH], 2 * T // CH, CH), c2, ALU.subtract))
                dve.tensor_scalar(flat(gqt), flat(gqt), CLAMP, None, ALU.min)
                dve.tensor_scalar(flat(gkt), flat(gkt), CLAMP, None, ALU.min).then_inc(gla_args, 1)
                dve.wait_ge(gla_exps, n)
                q = flat(gqk[:, 0:2, :])
                dve.scalar_tensor_tensor(flat(gqi), q, GL_K ** -0.5, flat(gqi), ALU.mult, ALU.mult)
                dve.scalar_tensor_tensor(flat(gqt), q, GL_K ** -0.5, flat(gqt), ALU.mult, ALU.mult)
                for hp in range(2):
                    x = gkt[:, hp, :, :].rearrange("p c (i s) -> p c i s", s=CH)
                    k = gqk[:, 2 + hp, :].rearrange("p (c s) -> p c s", s=CH)
                    dve.tensor_tensor(x, x, wide(k.unsqueeze(2), T // CH, CH // SUB, CH), ALU.mult)
                dve.tensor_tensor(flat(gkd), flat(gkd), flat(gqk[:, 2:4, :]), ALU.mult).then_inc(gla_ops, 1)

            def memory_attention(n):
                for t in range(NT):
                    job = ("XS", n, t)
                    dve.wait_ge(*filled(job))
                    after(dve.tensor_reduce(small[:, 0:4], view(job, XA_H, T), AX, ALU.max))
                    dve.tensor_scalar(small[:, 4:8], small[:, 0:4], -XA_D ** -0.5, None, ALU.mult).then_inc(xmax_ready, 1)
                    dve.wait_ge(*evacuated(job))
                    after(dve.reciprocal(small[:, 8:12], small[:, 8:12]))
                    dve.tensor_tensor(px, px, wide(small[:, 8:12].unsqueeze(2), XA_H, T), ALU.mult).then_inc(px_ready, 1)

            def diff_attention(n):
                us = units()

                def maxima(u):
                    t, h = us[u]
                    g = NT * (n - 1) + t
                    cols = (g + 1) * P
                    for m in range(2):
                        job = ("S", n, u, m)
                        i = 2 * (u % 2) + m
                        dve.wait_ge(*filled(job))
                        ps = view(job, cols)
                        after(dve.tensor_tensor_reduce(out=ps, in0=ps, in1=dist[:, SEQ - P - g * P:SEQ - P - g * P + cols], scale=1.0, scalar=LOWEST,
                                                       op0=ALU.add, op1=ALU.max, accum_out=small[:, 22 + i:23 + i]))
                        dve.tensor_scalar(small[:, 14 + i:15 + i], small[:, 22 + i:23 + i], -SLOPE[h], None, ALU.mult).then_inc(smax_ready, 1)

                def combine(u):
                    t, h = us[u]
                    cols = (NT * (n - 1) + t + 1) * P
                    z = 18 + 2 * (u % 2)
                    dve.wait_ge(*evacuated(("S", n, u, 0)))
                    dve.wait_ge(*evacuated(("S", n, u, 1)))
                    after(dve.reciprocal(small[:, z:z + 2], small[:, z:z + 2]))
                    after(dve.tensor_scalar(p1[:, 0:cols], p1[:, 0:cols], small[:, z + 1:z + 2], lam[:, 0:1], ALU.mult, ALU.mult))
                    w = pw[:, u % 2, 0:cols]
                    dve.scalar_tensor_tensor(w, w, small[:, z:z + 1], p1[:, 0:cols], ALU.mult, ALU.add).then_inc(wgt_ready, 1)

                def values(u):
                    t, h = us[u]
                    job = ("OV", n, u)
                    dve.wait_ge(*filled(job))
                    dve.tensor_copy(oda[:, t, h, :], view(job, P)).then_inc(free_sem(job), 1)

                for u in range(len(us)):
                    maxima(u)
                    combine(u)
                    if u:
                        values(u - 1)
                values(len(us) - 1)

            def gla(n):
                dve.wait_ge(gla_ops, n)
                after(dve.memset(at_s, 0.0))
                for t in range(NT):
                    job = ("AT", n, t)
                    dve.wait_ge(*filled(job))
                    ps = view(job, 2, HALF)[:, :, 0:2 * CH].rearrange("p two (hp s) -> p two hp s", s=CH)
                    for c2 in range(2):
                        tok = slice(CH * c2, CH * (c2 + 1))
                        ins = dve.tensor_tensor(at_s[tok, t, c2, :, :].rearrange("p (hp two) s -> p two hp s", two=2), ps[tok, :, :, :],
                                                tri[tok, :].unsqueeze(1).unsqueeze(1).broadcast_to([CH, 2, 2, CH]), ALU.mult)
                    ins.then_inc(free_sem(job), 1)
                for c in range(T // CH):
                    job = ("SU", n, c)
                    dve.wait_ge(*filled(job))
                    for h in range(GL_H):
                        i = 4 * (h // 2) + c
                        rows = slice(GL_K * (h % 2), GL_K * (h % 2 + 1))
                        ins = dve.scalar_tensor_tensor(state[rows, h, :], state[rows, h, :], gebl[rows, i:i + 1], view(job, 2, GL_V)[rows, h // 2, :],
                                                       ALU.mult, ALU.add)
                    ins.then_inc(free_sem(job), 1)
                    dve.wait_ge(*evacuated(job))

            def merge(n):
                norm_heads(norm_no("DA", n), heads_of(oda[:, :, :, :]), heads_of(oda[:, :, :, :]), 8, DA_V,
                           (grouped, wide(w_dao[:, :].unsqueeze(1), 8, DA_V)))
                dve.wait_ge(gr_ready, n)
                norm_heads(norm_no("GLA", n), heads_of(ogl[:, :, :, :]), heads_of(ogl[:, :, :, :]), 8, GL_V,
                           (grouped, gr[:, :, :].rearrange("p t (h d) -> p (t h) d", d=GL_V)))
                for hf in range(2):
                    m = flat(merged[:, 4 * hf:4 * hf + 4, :])
                    for b in range(3):
                        job = ("BR", n, hf, b)
                        dve.wait_ge(*evacuated(("GATE", n, hf, b)))
                        dve.wait_ge(*filled(job))
                        dve.tensor_tensor(m if b == 0 else flat(tmp), view(job, 1024), flat(sg), ALU.mult).then_inc(free_sem(job), 1)
                        dve.wait_ge(*evacuated(job))
                        if b:
                            ins = dve.tensor_tensor(m, m, flat(tmp), ALU.add)
                            if (hf, b) == (1, 2):
                                ins.then_inc(merged_ready, 1)
                            else:
                                after(ins)
                for t in range(NT):
                    dve.wait_ge(x_in[t], 16 * (2 * n + 1))
                for nb in range(2):
                    job = ("WO", n, nb)
                    dve.wait_ge(*filled(job))
                    x = xs[:, :, nb * HALF:(nb + 1) * HALF]
                    dve.tensor_tensor(x, view(job, NT, HALF), x, ALU.add).then_inc(free_sem(job), 1)

            def top16(values, best, where):
                for step in range(2):
                    s = slice(8 * step, 8 * step + 8)
                    for v, b in zip(values, best):
                        ins = dve.max(b[:, s], v)
                    after(ins)
                    for v, b, w in zip(values, best, where):
                        ins = dve.max_index(w[:, s], b[:, s], v)
                    after(ins)
                    if step == 0:
                        for v, b in zip(values, best):
                            ins = dve.match_replace(v, b[:, s], v, LOWEST)
                        after(ins)

            def route(n):
                after(norm_rows(2 * n + 1))
                for t in range(NT):
                    dve.scalar_tensor_tensor(xn2[:, t, :], xs[:, t, :], st2[:, 4 + t:5 + t], w_ffn[:, :], ALU.mult, ALU.mult).then_inc(xn2_ready, 1)
                for j in range(4):
                    dve.wait_ge(*evacuated(("SC", n, j)))
                    rows = [(t, i) for t in range(NT) for i in range(4)]
                    top16([sc[:, t, i, :] for t, i in rows], [tv[:, t, 4 * j + i, :] for t, i in rows], [ti[:, t, 4 * j + i, :] for t, i in rows])
                    dve.memset(st2[:, 7:8], 0.0).then_inc(top_done, 1)
                for t in range(NT):
                    v = tv[:, t, :, :].rearrange("p (h two) k -> p h two k", two=2)
                    for h in range(HEADS):
                        ins = dve.tensor_tensor(cand[:, h, :, :], wide(v[:, h, 0, :].unsqueeze(2), TOPK, TOPK),
                                                wide(v[:, h, 1, :].unsqueeze(1), TOPK, TOPK), ALU.add)
                    after(ins)
                    flats = [cand[:, h, :, :].rearrange("p a b -> p (a b)") for h in range(HEADS)]
                    top16(flats, [bv[:, h, :] for h in range(HEADS)], [bj[:, 0, h, :] for h in range(HEADS)])
                    dve.tensor_tensor(bf[:, 4, :, :], bv, wide(bv[:, :, 0:1], HEADS, TOPK), ALU.subtract).then_inc(sm_arg, 1)
                    after(dve.tensor_scalar(flat(bj[:, 1, :, :]), flat(bj[:, 0, :, :]), 4, None, ALU.logical_shift_right))
                    after(dve.tensor_scalar(flat(bj[:, 0, :, :]), flat(bj[:, 0, :, :]), TOPK - 1, None, ALU.bitwise_and))
                    dve.tensor_copy(flat(bf[:, 0, :, :]), flat(bj[:, 1, :, :]))
                    dve.tensor_copy(flat(bf[:, 1, :, :]), flat(bj[:, 0, :, :]))
                    after(dve.tensor_copy(flat(tif), flat(ti[:, t, :, :])))
                    keys = tif.rearrange("p (h two) k -> p h two k", two=2)
                    for s in range(2):
                        for h in range(HEADS):
                            ins = dve.tensor_tensor(cand[:, h, :, :], wide(bf[:, s, h, :].unsqueeze(2), TOPK, TOPK),
                                                    wide(iota.unsqueeze(1), TOPK, TOPK), ALU.is_equal)
                        after(ins)
                        for h in range(HEADS):
                            ins = dve.tensor_tensor(cand[:, h, :, :], cand[:, h, :, :], wide(keys[:, h, s, :].unsqueeze(1), TOPK, TOPK), ALU.mult)
                        after(ins)
                        after(dve.tensor_reduce(flat(bf[:, 2 + s, :, :]), cand.rearrange("p h a b -> p (h a) b"), AX, ALU.add))
                    dve.scalar_tensor_tensor(idx[:, n % 2, t, :], flat(bf[:, 2, :, :]), float(NKEY), flat(bf[:, 3, :, :]), ALU.mult, ALU.add)
                    dve.wait_ge(sm_exp, NT * (n - 1) + t + 1)
                    after(dve.tensor_reduce(bf[:, 5, :, 0], bf[:, 4, :, :], AX, ALU.add))
                    after(dve.reciprocal(bf[:, 5, :, 1], bf[:, 5, :, 0]))
                    after(dve.tensor_tensor(gw[:, n % 2, t, :].rearrange("p (h k) -> p h k", k=TOPK), bf[:, 4, :, :],
                                            wide(bf[:, 5, :, 1].unsqueeze(2), HEADS, TOPK), ALU.mult))

            def experts(n, t):
                g = NT * (n - 1) + t
                first = g * NB

                def put(rel, q):
                    dve.tensor_copy(stage[:, q, :], idx[:, n % 2, t, bass.ds(rel * BATCH, BATCH)]).then_inc(staged, 1)

                def dot(b, q):
                    for k in range(BATCH):
                        s = (q % 2) * BATCH + k
                        hold(dve, u_landed[s], landed(b, q))
                        u = ub[:, s, :]
                        dve.tensor_tensor_reduce(out=u, in0=u, in1=xn2[:, t, :], scale=1.0, scalar=0.0, op0=ALU.mult, op1=ALU.add,
                                                 accum_out=dots[:, q, k:k + 1]).then_inc(dot_done, 1)

                def weigh(b, rel, q):
                    hold(dve, gelu_done, b + 1)
                    if not isinstance(b, int) or b >= 2:
                        hold(dve, rows_added, b - 1)
                    for k in range(BATCH):
                        ins = dve.tensor_scalar(diag[:, (q % 2) * BATCH + k, :], ident, acts[:, q, k:k + 1],
                                                gw[:, n % 2, t, bass.ds(rel * BATCH + k, 1)], ALU.mult, ALU.mult)
                    ins.then_inc(diag_ready, 1)

                if g:
                    dve.wait_ge(rows_added, first)
                put(0, 0)
                put(1, 1)
                dot(first, 0)
                put(2, 2)

                for i in range(RING):
                    dot(first + i + 1, (i + 1) % RING)
                    weigh(first + i, i, i)
                    put(i + 3, (i + 3) % RING)
                with dve.Fori(1, NB // RING - 1) as j:
                    for i in range(RING):
                        dot(j * RING + (first + i + 1), (i + 1) % RING)
                        weigh(j * RING + (first + i), j * RING + i, i)
                        put(j * RING + (i + 3), (i + 3) % RING)
                tail = NB - RING
                for i in range(RING):
                    if i < RING - 1:
                        dot(first + tail + i + 1, i + 1)
                    weigh(first + tail + i, tail + i, i)
                    if i == 0:
                        put(tail + 3, 3)
                dve.wait_ge(fin_in, 16 * (g + 1))
                dve.wait_ge(rows_added, first + NB)
                dve.tensor_tensor(fin[:, :], acc[:, :], fin[:, :], ALU.add).then_inc(y_ready, 1)

            dve.memset(eps[:, :], EPS)
            dve.memset(state[:, :, :], 0.0).then_inc(state_zero, 1)
            dve.wait_ge(consts_in, N_CONST)
            dve.tensor_tensor(w_qs[:, :, :], wide(w_q64[:, :].unsqueeze(1), 2 * DA_H, DA_D), wide(qscale.unsqueeze(2), 2 * DA_H, DA_D), ALU.mult)
            dve.tensor_scalar(w_dao[:, :], w_dao[:, :], 1.0 - LAM_INIT, None, ALU.mult)
            for i in range(2):
                x, z = lam_in[:, 2 * i * DA_D:(2 * i + 1) * DA_D], lam_in[:, (2 * i + 1) * DA_D:(2 * i + 2) * DA_D]
                ins = dve.tensor_tensor_reduce(out=x, in0=x, in1=z, scale=1.0, scalar=0.0, op0=ALU.mult, op1=ALU.add, accum_out=lam[:, i:i + 1])
            ins.then_inc(const_ready, 1)
            dve.wait_ge(lam_exp, 1)
            after(dve.tensor_tensor(lam[:, 1:2], lam[:, 3:4], lam[:, 2:3], ALU.subtract))
            after(dve.tensor_scalar(lam[:, 0:1], lam[:, 1:2], -LAM_INIT, None, ALU.add))

            for n in range(STEPS + 1):
                norm_rows(max(2 * n, 1)).then_inc(norm_rs, 1)
                for t in range(NT):
                    job = ("XT", n, t)
                    dve.wait_ge(*filled(job))
                    dve.tensor_tensor(xnT[:, :, t * P:(t + 1) * P], view(job, KC, P), wide(w_cols[:, min(n, 1), :].unsqueeze(2), KC, P),
                                      ALU.mult).then_inc(free_sem(job), 1)
                if n == 0:
                    norm_heads(1, view(("MK", 0), 8, XA_D), heads_of(xq), 8, XA_D, (grouped, wide(w_xk[:, :].unsqueeze(1), 8, XA_D)), ("MK", 0))
                    continue
                project(n)
                memory_attention(n)
                diff_attention(n)
                gla_prepare(n)
                gla(n)
                merge(n)
                route(n)
                for t in range(NT):
                    experts(n, t)


def kernel(x, mem, mix_norm_w, w_in, da_q_norm_w, da_k_norm_w, da_lambda, da_out_norm_w,
           gla_w_gate, gla_b_gate, gla_out_norm_w, mem_norm_w, w_mem_kv, xa_q_norm_w, xa_k_norm_w,
           w_br_da, w_br_gla, w_br_xa, w_out, ffn_norm_w, peer_w_q, peer_sub_keys, peer_u, peer_v):
    import concourse.bacc as bacc
    from concourse.bass_utils import run_bass_kernel_spmd

    def cols(w):
        return np.ascontiguousarray(np.asarray(w).reshape(-1, P).T)

    arrays = {
        "x": np.asarray(x)[0], "mem": np.asarray(mem)[0], "consts": constant_table(),
        "mix_w": cols(mix_norm_w), "mem_w": cols(mem_norm_w), "w_in": np.asarray(w_in)[0],
        "q_w": np.asarray(da_q_norm_w)[0], "k_w": np.asarray(da_k_norm_w)[0], "lam": np.asarray(da_lambda).reshape(-1),
        "dao_w": np.asarray(da_out_norm_w)[0], "w_gate": np.asarray(gla_w_gate)[0], "b_gate": cols(gla_b_gate),
        "glo_w": np.asarray(gla_out_norm_w)[0], "w_mkv": np.asarray(w_mem_kv)[0], "xq_w": np.asarray(xa_q_norm_w)[0],
        "xk_w": np.asarray(xa_k_norm_w)[0], "br0": np.asarray(w_br_da)[0], "br1": np.asarray(w_br_gla)[0],
        "br2": np.asarray(w_br_xa)[0], "w_out": np.asarray(w_out)[0], "ffn_w": np.asarray(ffn_norm_w)[0],
        "w_q": np.asarray(peer_w_q)[0], "keysT": np.ascontiguousarray(np.asarray(peer_sub_keys)[0].transpose(2, 0, 1)),
        "peer_u": np.asarray(peer_u)[0], "peer_v": np.asarray(peer_v)[0],
    }
    nc = bacc.Bacc("TRN2", target_bir_lowering=False, num_devices=1)
    args = {}
    feed = {}
    for name, v in arrays.items():
        feed[f"in_{name}"] = np.ascontiguousarray(v)
        args[name] = nc.dram_tensor(f"in_{name}", v.shape, mybir.dt.from_np(v.dtype), kind="ExternalInput").ap()
    args["y"] = nc.dram_tensor("out_y", (SEQ, D), F32, kind="ExternalOutput").ap()
    build(nc, args)
    r = run_bass_kernel_spmd(nc, [feed], core_ids=[0])
    return r.results[0]["out_y"].reshape(1, SEQ, D)
```

```python
from contextlib import ExitStack

import numpy as np

import concourse.bass as bass
from concourse import mybir

F32 = mybir.dt.float32
U32 = mybir.dt.uint32
ALU = mybir.AluOpType
ACT = mybir.ActivationFunctionType
AX = mybir.AxisListType.X

P = 128
D = 1024
SEQ = 1024
KC = D // P
NT = 2
T = NT * P
STEPS = SEQ // T
EPS = 1e-6
DA_H, DA_D, DA_V = 4, 64, 128
GL_H, GL_K, GL_V, GL_R, GL_TAU = 4, 64, 128, 16, 16.0
CH = 64
SUB = 16
CLAMP = 60.0 * GL_TAU
XA_H, XA_D = 4, 128
HEADS, NKEY, TOPK = 8, 128, 16
LAM_INIT = 0.8 - 0.6 * 1.0
SLOPE = [2.0 ** (-8.0 * (h + 1) / DA_H) for h in range(DA_H)]
MASKED = -1.0e30
LOWEST = -3.0e38

C_DAQ, C_DAK, C_DAV = 0, 512, 1024
C_GQK, C_GV, C_GR, C_GG = 1536, 2048, 2560, 3072
C_XQ, C_GATE = 3088, 3600
HALF = 512

K_ID, K_TRI, K_RESET, K_IOTA, K_DIST, K_QS, K_END = 0, 128, 192, 448, 464, 1488, 1496


def constant_table():
    c = np.zeros((P, K_END), np.float32)
    p = np.arange(P)[:, None]
    c[:, K_ID:K_TRI] = np.eye(P)
    c[:, K_TRI:K_RESET] = (p % CH) <= np.arange(CH)[None]
    c[:, K_RESET:K_IOTA] = (np.arange(T) % CH != 0)[None]
    c[:, K_IOTA:K_DIST] = np.arange(TOPK)[None]
    dist = np.arange(SEQ)[None] - (SEQ - P) - p
    c[:, K_DIST:K_QS] = np.where(dist <= 0, dist, MASKED)
    c[:, K_QS:K_END] = [DA_D ** -0.5 / SLOPE[m // 2] for m in range(2 * DA_H)]
    return c


def units():
    return [(t, h) for t in range(NT) for h in range(DA_H)]


def jobs_of(n):
    out = [("XT", n, t) for t in range(NT)]
    if n == 0:
        return out + [("MK", 0), ("MV", 0), ("MKT", 0)]
    out += [("Q", n), ("K", n), ("V", n)]
    out += [("QT", n, t) for t in range(NT)] + [("KT", n, t) for t in range(NT)]
    out += [("GQK", n), ("GG", n), ("GL", n), ("XQ", n)]
    out += [("XQT", n), ("XS", n, 0), ("XS", n, 1), ("XPT", n, 0), ("XO", n, 0), ("XPT", n, 1), ("XO", n, 1)]
    last = None
    for u in range(len(units())):
        out += [("S", n, u, 0), ("S", n, u, 1)]
        if u:
            out += [("WT", n, u - 1), ("OV", n, u - 1)]
        last = u
    out += [("WT", n, last), ("OV", n, last)]
    out += [("GV", n), ("KD", n)] + [("AT", n, t) for t in range(NT)]
    for c in range(T // CH):
        out += [("GO", n, c), ("SU", n, c)]
    out += [("GR", n), ("OT", n, 0), ("OT", n, 1)]
    for hf in range(2):
        for b in range(3):
            out += [("GATE", n, hf, b), ("BR", n, hf, b)]
    out += [("WO", n, 0), ("WO", n, 1)] + [("X2T", n, t) for t in range(NT)]
    out += [("WQ", n, 0), ("WQ", n, 1), ("SC", n, 0), ("WQ", n, 2), ("SC", n, 1), ("WQ", n, 3), ("SC", n, 2), ("SC", n, 3)]
    return out


NBANK = 3
JOBS = [job for n in range(STEPS + 1) for job in jobs_of(n)]
PLACE = {job: (i % NBANK, i // NBANK) for i, job in enumerate(JOBS)}

W_BLOCKS = [("mkv", 0, ("MK", 0)), ("mkv", 1, ("MV", 0))]
for _n in range(1, STEPS + 1):
    W_BLOCKS += [("in", C_DAQ, ("Q", _n)), ("in", C_DAK, ("K", _n)), ("in", C_DAV, ("V", _n)),
                 ("in", C_GQK, ("GQK", _n)), ("in", C_XQ, ("XQ", _n)), ("in", C_GV, ("GV", _n)),
                 ("in", C_GR, ("GR", _n))]
    for _hf in range(2):
        for _b in range(3):
            W_BLOCKS += [("in", C_GATE + _b * D + _hf * HALF, ("GATE", _n, _hf, _b)), (f"br{_b}", _hf, ("BR", _n, _hf, _b))]
    W_BLOCKS += [("out", nb, ("WO", _n, nb)) for nb in range(2)]
    W_BLOCKS += [("wq", j, ("WQ", _n, j)) for j in range(4)]
W_SLOTS = 2
W_AT = {user: i for i, (_, _, user) in enumerate(W_BLOCKS)}

NORMS = [("MK", 0)] + [(what, n) for n in range(1, STEPS + 1) for what in ("Q", "K", "XQ", "DA", "GLA")]

BATCH, RING, LAG, LEAD = 2, 8, 4, 2
NB = HEADS * TOPK // BATCH
TURNS = NT * NB // RING

SPAN = {"XT": 2, "Q": 14, "K": 14, "V": 14, "GQK": 15, "XQ": 14, "XQT": 1, "XS": 4, "S": 3, "OV": 3, "GV": 14, "KD": 6,
        "AT": 3, "GO": 2, "SU": 2, "GR": 14, "OT": 4, "GATE": 15, "BR": 8, "WO": 14, "X2T": 4, "WQ": 15, "SC": 6, "R": 6}
RANKS = 8
BEFORE = {}


def spread():
    for n in range(STEPS + 1):
        row = jobs_of(n) + [("R", n, i) for i in range(RANKS if n else 0)]
        total = sum(SPAN.get(j[0], 0) for j in row)
        so_far = 0
        for j in row:
            so_far += SPAN.get(j[0], 0)
            BEFORE[j] = 0 if n < 2 else NT * NB * (n - 2) + NT * NB * so_far // total


spread()


class Batches:

    def __init__(self, slot):
        self.slot, self.done = slot, 0

    def upto(self, job, before=None):
        target = BEFORE[job]
        if before is not None:
            last = max([v for v in (self.done,)])
            target = self.done + int((target - last) * before)
        while self.done < target:
            self.slot(self.done)
            self.done += 1


def build(nc, a):
    with ExitStack() as ctx:
        def sb(name, shape, dt=F32):
            return ctx.enter_context(nc.sbuf_tensor(name, shape, dt))

        def sem(name):
            return ctx.enter_context(nc.semaphore(name))

        consts = sb("consts", [P, K_END])
        ident = consts[:, K_ID:K_TRI]
        tri = consts[:, K_TRI:K_RESET]
        reset = consts[:, K_RESET:K_IOTA]
        iota = consts[:, K_IOTA:K_DIST]
        dist = consts[:, K_DIST:K_QS]
        qscale = consts[:, K_QS:K_END]
        eps = sb("eps", [P, 1])
        w_cols = sb("w_cols", [P, 2, KC])
        w_q64 = sb("w_q64", [P, DA_D])
        w_qs = sb("w_qs", [P, 2 * DA_H, DA_D])
        w_k64 = sb("w_k64", [P, DA_D])
        w_dao = sb("w_dao", [P, DA_V])
        w_glo = sb("w_glo", [P, GL_V])
        w_xq = sb("w_xq", [P, XA_D])
        w_xk = sb("w_xk", [P, XA_D])
        w_ffn = sb("w_ffn", [P, D])
        lam = sb("lam", [P, 4])
        b_gate = sb("b_gate", [P, 2])
        w_gate = sb("w_gate", [GL_R, GL_H * GL_K])
        w_gg = sb("w_gg", [P, KC, GL_R])
        keysT = sb("keysT", [P, 2, NKEY])
        mkT = sb("mkT", [P, XA_H, T])
        mv = sb("mv", [P, NT, XA_H * XA_D])
        kT = sb("kT", [P, DA_H, SEQ])
        V = sb("V", [P, SEQ // P, DA_H * DA_V])
        state = sb("state", [P, GL_H, GL_V])
        W = sb("W", [P, W_SLOTS, KC, HALF])
        xs = sb("xs", [P, NT, D])
        xnT = sb("xnT", [P, KC, T])
        oT_xa = sb("oT_xa", [P, 4, T])
        xn2 = sb("xn2", [P, 2, NT, D])
        idx = sb("idx", [P, 2, NT * HEADS * TOPK], U32)
        gw = sb("gw", [P, 2, NT * HEADS * TOPK])
        st2 = sb("st2", [P, 8])
        hs = sb("hs", [P, 3, 16])
        small = sb("small", [P, 32])
        ub = sb("ub", [P, 2 * BATCH, D])
        vb = sb("vb", [P, 2 * BATCH, D])
        diag = sb("diag", [P, 2 * BATCH, P])
        stage = sb("stage", [P, RING, BATCH], U32)
        dots = sb("dots", [P, RING, BATCH])
        acts = sb("acts", [P, RING, BATCH])
        fin = sb("fin", [P, D])
        gebl = sb("gebl", [P, 8])
        qT = sb("qT", [P, DA_H, T])
        AREA = 6144
        arena = sb("arena", [P, AREA])

        def parts(x, *shape):
            names = "abcd"[:len(shape)]
            if len(shape) == 1:
                return x
            return x.rearrange(f"p ({' '.join(names)}) -> p {' '.join(names)}", **{c: s for c, s in zip(names[1:], shape[1:])})

        def area(at, *shape):
            assert at + int(np.prod(shape)) <= AREA
            return parts(arena[:, at:at + int(np.prod(shape))], *shape)

        sq = area(AREA - 1024, 1024)
        wT = area(AREA - 1024, SEQ)
        xhat = area(0, NT, D)
        lam_in = area(2048, 4 * DA_D)
        gqk = area(0, 4, T)
        gb = area(1024, 2, T)
        qn = area(1536, NT, 2 * DA_H, DA_D)
        kn = area(2560, NT, 2 * DA_H, DA_D)
        xq = area(3584, NT, XA_H, XA_D)
        ggT = area(4608, T)[0:GL_R, :]
        xqT = area(1536, XA_H, T)
        px = area(2560, XA_H, T)
        pxT = area(3584, XA_H, 2, P)
        pw = area(1536, 2, SEQ)
        p1 = area(3584, SEQ)
        oda = parts(xs[:, 0, :], NT, DA_H, DA_V)
        ogl = parts(xs[:, 1, :], NT, GL_H, GL_V)
        gqi = area(1536, 2, T)
        gqt = area(2048, 2, T)
        gkt = area(2560, 2, 4, 256)
        gkd = area(4608, 2, T)
        kdT = area(0, NT, 2, P)
        at_s = area(512, NT, 2, GL_H, CH)
        gv = area(AREA - 1024, NT, GL_H * GL_V)
        gr = area(0, NT, GL_H * GL_V)
        oT = [area(4096, 4, T), area(5120, 4, T), oT_xa]
        merged = area(0, KC, T)
        sg = area(2048, 4, T)
        tmp = area(3072, 4, T)
        sc = area(0, NT, 4, NKEY)
        xn2T = area(1024, KC, T)
        qp = area(3072, 2, 4 * T)
        cand = area(1024, HEADS, TOPK, TOPK)
        bv = area(3072, HEADS, TOPK)
        bf = area(3200, 6, HEADS, TOPK)
        tif = area(3968, 16, TOPK)
        bj = area(4224, 2, HEADS, TOPK).bitcast(U32)
        tv = area(5120, NT, 16, TOPK)
        ti = area(5632, NT, 16, TOPK).bitcast(U32)

        bank = [ctx.enter_context(nc.psum_tensor(f"bank{i}", [P, 1024], F32)) for i in range(NBANK)]
        acc = ctx.enter_context(nc.psum_tensor("acc", [P, D], F32))

        bank_full = [sem(f"bank_full{i}") for i in range(NBANK)]
        bank_free = [sem(f"bank_free{i}") for i in range(NBANK)]
        consts_in = sem("consts_in")
        x_in = [sem(f"x_in{t}") for t in range(NT)]
        w_in = [sem(f"w_in{i}") for i in range(W_SLOTS)]
        x1_out = sem("x1_out")
        fin_in = sem("fin_in")
        y_out = sem("y_out")
        const_ready = sem("const_ready")
        lam_exp = sem("lam_exp")
        norm_sq = sem("norm_sq")
        norm_rs = sem("norm_rs")
        xhat_ready = sem("xhat_ready")
        hn_sq = sem("hn_sq")
        hn_ss = sem("hn_ss")
        hn_rt = sem("hn_rt")
        hn_done = sem("hn_done")
        sig_ready = sem("sig_ready")
        gla_ln = sem("gla_ln")
        gla_args = sem("gla_args")
        gla_exps = sem("gla_exps")
        gla_ops = sem("gla_ops")
        gr_ready = sem("gr_ready")
        state_zero = sem("state_zero")
        smax_ready = sem("smax_ready")
        wgt_ready = sem("wgt_ready")
        xmax_ready = sem("xmax_ready")
        px_ready = sem("px_ready")
        gate_used = sem("gate_used")
        merged_ready = sem("merged_ready")
        xn2_ready = sem("xn2_ready")
        top_done = sem("top_done")
        sm_arg = sem("sm_arg")
        sm_exp = sem("sm_exp")
        route_done = sem("route_done")
        staged = sem("staged")
        u_landed = [sem(f"u_landed{k}") for k in range(2 * BATCH)]
        v_landed = [sem(f"v_landed{k}") for k in range(2 * BATCH)]
        dot_done = sem("dot_done")
        gelu_done = sem("gelu_done")
        diag_ready = sem("diag_ready")
        rows_added = sem("rows_added")
        y_ready = sem("y_ready")
        act_own = sem("act_own")
        dve_own = sem("dve_own")

        def claim(eng, job):
            b, n = PLACE[job]
            if n:
                eng.wait_ge(bank_free[b], n)
            return bank[b], bank_full[b]

        def filled(job):
            b, n = PLACE[job]
            return bank_full[b], n + 1

        def evacuated(job):
            b, n = PLACE[job]
            return bank_free[b], n + 1

        def free_sem(job):
            return bank_free[PLACE[job][0]]

        def view(job, *shape):
            return parts(bank[PLACE[job][0]][:, 0:int(np.prod(shape))], *shape)

        def hold(eng, s, value):
            if not isinstance(value, int):
                value = eng.to_reg(value)
                eng.wait_ge(consts_in, 16)
            eng.wait_ge(s, value)

        def w_slot(user):
            i = W_AT[user]
            return W[:, i % W_SLOTS, :, :], w_in[i % W_SLOTS], 16 * (i // W_SLOTS + 1)

        def norm_no(what, n):
            return NORMS.index((what, n)) + 1

        def landed(b, q):
            return (b - q % 2) * 8 + 16

        block = ctx.enter_context(nc.Block())

        CONST_LOADS = [
            (consts[:, :], a["consts"]), (w_cols[:, 0, :], a["mem_w"]), (w_cols[:, 1, :], a["mix_w"]),
            (w_q64[:, :], a["q_w"].partition_broadcast(P)), (w_k64[:, :], a["k_w"].partition_broadcast(P)),
            (w_dao[:, :], a["dao_w"].partition_broadcast(P)), (w_glo[:, :], a["glo_w"].partition_broadcast(P)),
            (w_xq[:, :], a["xq_w"].partition_broadcast(P)), (w_xk[:, :], a["xk_w"].partition_broadcast(P)),
            (w_ffn[:, :], a["ffn_w"].partition_broadcast(P)), (lam_in[:, :], a["lam"].partition_broadcast(P)),
            (b_gate[:, :], a["b_gate"]), (w_gate[:, :], a["w_gate"]),
            (w_gg[:, :, :], a["w_in"][:, C_GG:C_GG + GL_R].rearrange("(k p) n -> p k n", p=P)),
            (keysT[:, :, :], a["keysT"]),
        ]
        N_CONST = 16 * len(CONST_LOADS)
        x_tiles = a["x"].rearrange("(g p) d -> g p d", p=P)
        mem_tiles = a["mem"].rearrange("(g p) d -> g p d", p=P)
        y_tiles = a["y"].rearrange("(g p) d -> g p d", p=P)
        w_dram = {"in": a["w_in"].rearrange("(k p) n -> p k n", p=P), "mkv": a["w_mkv"].rearrange("(k p) n -> p k n", p=P),
                  **{f"br{b}": a[f"br{b}"].rearrange("(k p) n -> p k n", p=P) for b in range(3)},
                  "out": a["w_out"].rearrange("(k p) n -> p k n", p=P), "wq": a["w_q"].rearrange("(k p) n -> p k n", p=P)}

        @block.sync
        def _(sp):
            for dst, src in CONST_LOADS:
                sp.dma_start(dst, src).then_inc(consts_in, 16)
            loaded = [0]

            def load_blocks(n_blocks):
                for i in range(loaded[0], loaded[0] + n_blocks):
                    kind, where, _ = W_BLOCKS[i]
                    if i >= W_SLOTS:
                        sp.wait_ge(*filled(W_BLOCKS[i - W_SLOTS][2]))
                    at = where if kind == "in" else where * HALF
                    rows = w_dram[kind].shape[1]
                    sp.dma_start(W[:, i % W_SLOTS, 0:rows, :], w_dram[kind][:, :, at:at + HALF]).then_inc(w_in[i % W_SLOTS], 16)
                loaded[0] += n_blocks

            for n in range(STEPS + 1):
                for t in range(NT):
                    if n > 1:
                        sp.wait_ge(x1_out, 16 * NT * (n - 1))
                        sp.wait_ge(xn2_ready, NT * (n - 1))
                    elif n == 1:
                        sp.wait_ge(xhat_ready, t + 1)
                    src = mem_tiles[t] if n == 0 else x_tiles[NT * (n - 1) + t]
                    sp.dma_start(xs[:, t, :], src).then_inc(x_in[t], 16)
                if n == 0:
                    load_blocks(2)
                    continue
                load_blocks(7 + 2)
                sp.wait_ge(*filled(("OT", n, 1)))
                for t in range(NT):
                    sp.dma_start(xs[:, t, :], x_tiles[NT * (n - 1) + t]).then_inc(x_in[t], 16)
                load_blocks(10 + 2)
                sp.wait_ge(*evacuated(("WO", n, 1)))
                for t in range(NT):
                    sp.dma_start(y_tiles[NT * (n - 1) + t], xs[:, t, :]).then_inc(x1_out, 16)
                load_blocks(4)
            sp.wait_ge(y_out, 16 * SEQ // P)

        @block.gpsimd
        def _(pool):
            def gather_u(b, q):
                hold(pool, staged, b + 1)
                for k in range(BATCH):
                    if not isinstance(b, int) or b >= 2:
                        hold(pool, dot_done, (b - 2) * BATCH + k + 1)
                    s = (q % 2) * BATCH + k
                    pool.indirect_dma_start(ub[:, s, :], None, a["peer_u"],
                                            bass.IndirectOffsetOnAxis(ap=stage[:, q, k:k + 1], axis=0)).then_inc(u_landed[s], 16)

            def gather_v(b, q):
                if not isinstance(b, int) or b >= 2:
                    hold(pool, rows_added, b - 1)
                for k in range(BATCH):
                    s = (q % 2) * BATCH + k
                    pool.indirect_dma_start(vb[:, s, :], None, a["peer_v"],
                                            bass.IndirectOffsetOnAxis(ap=stage[:, q, k:k + 1], axis=0)).then_inc(v_landed[s], 16)

            def x1_back(n, t):
                g = NT * (n - 1) + t
                pool.wait_ge(x1_out, 16 * NT * n)
                if g:
                    pool.wait_ge(y_out, 16 * g)
                pool.dma_start(fin[:, :], y_tiles[g]).then_inc(fin_in, 16)

            def store(n, t):
                g = NT * (n - 1) + t
                pool.wait_ge(y_ready, g + 1)
                pool.dma_start(y_tiles[g], fin[:, :]).then_inc(y_out, 16)

            pool.wait_ge(consts_in, N_CONST)
            for n in range(1, STEPS + 1):
                first = NT * NB * (n - 1)
                for i in range(LAG):
                    gather_u(first + i, i)
                x1_back(n, 0)

                def turn(at, edge):
                    for q in range(RING):
                        gather_v(at + q, q)
                        if edge is None or edge * RING + q + LAG < NT * NB:
                            gather_u(at + q + LAG, (q + LAG) % RING)
                        if edge is not None and edge * RING + q == NB + 3:
                            store(n, 0)
                            x1_back(n, 1)

                for t in range(NT):
                    per = NB // RING
                    turn(first + t * NB, t * per)
                    with pool.Fori(1, per - 1) as j:
                        turn(j * RING + (first + t * NB), None)
                    turn(first + (t + 1) * NB - RING, (t + 1) * per - 1)
                store(n, 1)

        @block.tensor
        def _(pe):
            def token_major(job, user, out_of):
                ps, full = claim(pe, job)
                w, s, v = w_slot(user)
                pe.wait_ge(s, v)
                for t in range(NT):
                    if t:
                        batches.upto(job, 0.5)
                    for k in range(KC):
                        mm = pe.matmul(ps[:, t * HALF:(t + 1) * HALF], out_of[:, k, t * P:(t + 1) * P], w[:, k, :],
                                       start=k == 0, stop=k == KC - 1)
                mm.then_inc(full, 1)
                batches.upto(job)

            def channel_major(job, user, rhs):
                ps, full = claim(pe, job)
                w, s, v = w_slot(user)
                pe.wait_ge(s, v)
                for c in range(4):
                    if c:
                        batches.upto(job, c / 4)
                    for k in range(KC):
                        mm = pe.matmul(ps[:, c * T:(c + 1) * T], w[:, k, c * P:(c + 1) * P], rhs[:, k, :],
                                       start=k == 0, stop=k == KC - 1)
                mm.then_inc(full, 1)
                batches.upto(job)

            def turn(job, blocks, after):
                batches.upto(job)
                ps, full = claim(pe, job)
                for w in after:
                    pe.wait_ge(*w)
                for i, src in enumerate(blocks):
                    mm = pe.transpose(ps[:, i * P:(i + 1) * P], src, ident)
                mm.then_inc(full, 1)

            def project(n):
                token_major(("Q", n), ("Q", n), xnT)
                token_major(("K", n), ("K", n), xnT)
                token_major(("V", n), ("V", n), xnT)
                for t in range(NT):
                    turn(("QT", n, t), [qn[:, t, 2 * h:2 * h + 2, :].rearrange("p a b -> p (a b)") for h in range(DA_H)],
                         [(hn_done, norm_no("Q", n))])
                for t in range(NT):
                    turn(("KT", n, t), [kn[:, t, 2 * h:2 * h + 2, :].rearrange("p a b -> p (a b)") for h in range(DA_H)],
                         [(hn_done, norm_no("K", n))])
                channel_major(("GQK", n), ("GQK", n), xnT)
                batches.upto(("GG", n))
                ps, full = claim(pe, ("GG", n))
                for k in range(KC):
                    mm = pe.matmul(ps[0:GL_R, 0:T], w_gg[:, k, :], xnT[:, k, :], start=k == 0, stop=k == KC - 1)
                mm.then_inc(full, 1)
                batches.upto(("GL", n))
                ps, full = claim(pe, ("GL", n))
                pe.wait_ge(*evacuated(("GG", n)))
                for hp in range(2):
                    mm = pe.matmul(ps[:, hp * T:(hp + 1) * T], w_gate[:, hp * P:(hp + 1) * P], ggT, start=True, stop=True)
                mm.then_inc(full, 1)
                token_major(("XQ", n), ("XQ", n), xnT)

            def memory_attention(n):
                turn(("XQT", n), [xq[:, t, h, :] for h in range(XA_H) for t in range(NT)], [(hn_done, norm_no("XQ", n))])
                for t in range(NT):
                    batches.upto(("XS", n, t))
                    ps, full = claim(pe, ("XS", n, t))
                    pe.wait_ge(*evacuated(("XQT", n)))
                    for h in range(XA_H):
                        mm = pe.matmul(ps[:, h * T:(h + 1) * T], xqT[:, h, t * P:(t + 1) * P], mkT[:, h, :], start=True, stop=True)
                    mm.then_inc(full, 1)
                for t in range(NT):
                    turn(("XPT", n, t), [px[:, h, m * P:(m + 1) * P] for h in range(XA_H) for m in range(2)],
                         [(px_ready, NT * (n - 1) + t + 1)])
                    batches.upto(("XO", n, t))
                    ps, full = claim(pe, ("XO", n, t))
                    pe.wait_ge(*evacuated(("XPT", n, t)))
                    for h in range(XA_H):
                        for m in range(2):
                            mm = pe.matmul(ps[:, h * P:(h + 1) * P], mv[:, m, h * XA_D:(h + 1) * XA_D], pxT[:, h, m, :],
                                           start=m == 0, stop=m == 1)
                    mm.then_inc(full, 1)

            def diff_attention(n):
                us = units()

                def scores(u):
                    t, h = us[u]
                    cols = (NT * (n - 1) + t + 1) * P
                    for m in range(2):
                        batches.upto(("S", n, u, m))
                        ps, full = claim(pe, ("S", n, u, m))
                        if u == 0 and m == 0:
                            pe.wait_ge(*evacuated(("QT", n, 1)))
                            pe.wait_ge(*evacuated(("KT", n, 1)))
                        rows = slice(DA_D * m, DA_D * (m + 1))
                        for c in range(0, cols, HALF):
                            w = min(HALF, cols - c)
                            mm = pe.matmul(ps[:, c:c + w], qT[rows, h, t * P:(t + 1) * P], kT[rows, h, c:c + w], start=True, stop=True)
                        mm.then_inc(full, 1)

                def values(u):
                    t, h = us[u]
                    nb = NT * (n - 1) + t + 1
                    turn(("WT", n, u), [pw[:, u % 2, k * P:(k + 1) * P] for k in range(nb)],
                         [(wgt_ready, len(us) * (n - 1) + u + 1)])
                    batches.upto(("OV", n, u))
                    ps, full = claim(pe, ("OV", n, u))
                    pe.wait_ge(*evacuated(("WT", n, u)))
                    for k in range(nb):
                        mm = pe.matmul(ps[:, 0:P], wT[:, k * P:(k + 1) * P], V[:, k, h * DA_V:(h + 1) * DA_V], start=k == 0, stop=k == nb - 1)
                    mm.then_inc(full, 1)

                for u in range(len(us)):
                    scores(u)
                    if u:
                        values(u - 1)
                values(len(us) - 1)

            def gla(n):
                token_major(("GV", n), ("GV", n), xnT)
                turn(("KD", n), [gkd[:, hp, t * P:(t + 1) * P] for t in range(NT) for hp in range(2)], [(gla_ops, n)])
                for t in range(NT):
                    batches.upto(("AT", n, t))
                    ps, full = claim(pe, ("AT", n, t))
                    for c2 in range(2):
                        c = 2 * t + c2
                        for h in range(GL_H):
                            rows = slice(GL_K * (h % 2), GL_K * (h % 2 + 1))
                            for i in range(CH // SUB):
                                at = (h % 2) * HALF + (h // 2) * CH + i * SUB
                                mm = pe.matmul(ps[CH * c2:CH * (c2 + 1), at:at + SUB],
                                               gkt[rows, h // 2, c, i * CH:(i + 1) * CH],
                                               gqt[rows, h // 2, c * CH + i * SUB:c * CH + (i + 1) * SUB], start=True, stop=True)
                    mm.then_inc(full, 1)
                for c in range(T // CH):
                    t, c2 = c // 2, c % 2
                    tok = slice(CH * c2, CH * (c2 + 1))
                    batches.upto(("GO", n, c))
                    ps, full = claim(pe, ("GO", n, c))
                    if c == 0:
                        pe.wait_ge(*evacuated(("KD", n)))
                        pe.wait_ge(*evacuated(("GV", n)))
                        pe.wait_ge(*(evacuated(("SU", n - 1, T // CH - 1)) if n > 1 else (state_zero, 1)))
                    else:
                        pe.wait_ge(*evacuated(("SU", n, c - 1)))
                    pe.wait_ge(*evacuated(("AT", n, t)))
                    for h in range(GL_H):
                        pe.matmul(ps[tok, h * GL_V:(h + 1) * GL_V], gqi[:, h // 2, c * CH:(c + 1) * CH], state[:, h, :],
                                  start=True, stop=False)
                        mm = pe.matmul(ps[tok, h * GL_V:(h + 1) * GL_V], at_s[:, t, c2, h, :], gv[:, t, h * GL_V:(h + 1) * GL_V],
                                       start=False, stop=True)
                    mm.then_inc(full, 1)
                    batches.upto(("SU", n, c))
                    ps, full = claim(pe, ("SU", n, c))
                    for h in range(GL_H):
                        rows = slice(GL_K * (h % 2), GL_K * (h % 2 + 1))
                        mm = pe.matmul(ps[rows, (h // 2) * GL_V:(h // 2 + 1) * GL_V], kdT[tok, t, h // 2, GL_K * (h % 2):GL_K * (h % 2 + 1)],
                                       gv[tok, t, h * GL_V:(h + 1) * GL_V], start=True, stop=True)
                    mm.then_inc(full, 1)

            def merge(n):
                token_major(("GR", n), ("GR", n), xnT)
                turn(("OT", n, 0), [oda[:, t, h, :] for h in range(4) for t in range(NT)], [(hn_done, norm_no("DA", n))])
                turn(("OT", n, 1), [ogl[:, t, h, :] for h in range(4) for t in range(NT)], [(hn_done, norm_no("GLA", n))])
                for hf in range(2):
                    for b in range(3):
                        channel_major(("GATE", n, hf, b), ("GATE", n, hf, b), xnT)
                        batches.upto(("BR", n, hf, b))
                        ps, full = claim(pe, ("BR", n, hf, b))
                        w, s, v = w_slot(("BR", n, hf, b))
                        pe.wait_ge(s, v)
                        pe.wait_ge(*evacuated(("OT", n, b) if b < 2 else ("XO", n, 1)))
                        for c in range(4):
                            for k in range(4):
                                mm = pe.matmul(ps[:, c * T:(c + 1) * T], w[:, k, c * P:(c + 1) * P], oT[b][:, k, :], start=k == 0, stop=k == 3)
                        mm.then_inc(full, 1)
                pe.wait_ge(merged_ready, n)
                for nb in range(2):
                    token_major(("WO", n, nb), ("WO", n, nb), merged)

            def route(n):
                for t in range(NT):
                    turn(("X2T", n, t), [xn2[:, n % 2, t, k * P:(k + 1) * P] for k in range(KC)], [(xn2_ready, NT * (n - 1) + t + 1)])

                def score(j):
                    batches.upto(("SC", n, j))
                    ps, full = claim(pe, ("SC", n, j))
                    pe.wait_ge(*evacuated(("WQ", n, j)))
                    for t in range(NT):
                        for i in range(4):
                            mm = pe.matmul(ps[:, (4 * t + i) * NKEY:(4 * t + i + 1) * NKEY], qp[:, j % 2, i * T + t * P:i * T + (t + 1) * P],
                                           keysT[:, i % 2, :], start=True, stop=True)
                    mm.then_inc(full, 1)

                pe.wait_ge(*evacuated(("X2T", n, 1)))
                for j in range(4):
                    channel_major(("WQ", n, j), ("WQ", n, j), xn2T)
                    if j:
                        score(j - 1)
                score(3)

            def add_rows(b, q, start=False, stop=False):
                hold(pe, diag_ready, b + 1)
                for k in range(BATCH):
                    s = (q % 2) * BATCH + k
                    hold(pe, v_landed[s], landed(b, q))
                    for c in range(2):
                        mm = pe.matmul(acc[:, c * HALF:(c + 1) * HALF], diag[:, s, :], vb[:, s, c * HALF:(c + 1) * HALF],
                                       start=start and k == 0, stop=stop and k == BATCH - 1)
                mm.then_inc(rows_added, 1)

            def slot(b):
                if b % (NT * NB):
                    add(b - 1)

            def add(b):
                if b % NB == 0 and b:
                    pe.wait_ge(y_ready, b // NB)
                add_rows(b, b % RING, start=b % NB == 0, stop=b % NB == NB - 1)

            batches = Batches(slot)

            pe.wait_ge(consts_in, N_CONST)
            for n in range(STEPS + 1):
                for t in range(NT):
                    turn(("XT", n, t), [xhat[:, t, k * P:(k + 1) * P] for k in range(KC)], [(xhat_ready, NT * n + t + 1)])
                pe.wait_ge(*evacuated(("XT", n, 1)))
                if n == 0:
                    token_major(("MK", 0), ("MK", 0), xnT)
                    token_major(("MV", 0), ("MV", 0), xnT)
                    turn(("MKT", 0), [xq[:, t, h, :] for h in range(XA_H) for t in range(NT)], [(hn_done, 1)])
                    continue
                project(n)
                memory_attention(n)
                diff_attention(n)
                gla(n)
                merge(n)
                route(n)
                if n > 1:
                    batches.upto(("R", n, RANKS - 1))
                    add(NT * NB * (n - 1) - 1)
            first = NT * NB * (STEPS - 1)
            for t in range(NT):
                for b in range(first + t * NB, first + t * NB + RING):
                    add(b)
                with pe.Fori(1, NB // RING - 1) as j:
                    for q in range(RING):
                        add_rows(j * RING + (first + t * NB + q), q)
                for b in range(first + (t + 1) * NB - RING, first + (t + 1) * NB):
                    add(b)

        @block.scalar
        def _(act):
            own = [0]

            def after(ins):
                own[0] += 1
                ins.then_inc(act_own, 1)
                act.wait_ge(act_own, own[0])

            def copy(job, dst, *shape):
                batches.upto(job)
                act.wait_ge(*filled(job))
                act.activation(dst, view(job, *shape), ACT.Copy).then_inc(free_sem(job), 1)

            def norm_rows(which, ready):
                for t in range(NT):
                    act.wait_ge(*ready[t])
                    after(act.activation(sq, xs[:, t, :], ACT.Square, accum_out=st2[:, t:t + 1]))
                act.activation(st2[:, 2:4], st2[:, 0:2], ACT.Sqrt, scale=1.0 / D, bias=eps[:, 0:1]).then_inc(norm_sq, 1)

            def norm_heads(no, job, src, ready, groups, width):
                batches.upto(job)
                act.wait_ge(*ready)
                if no > 1:
                    act.wait_ge(hn_ss, no - 1)
                act.activation(sq, src, ACT.Square).then_inc(hn_sq, 1)
                act.wait_ge(hn_ss, no)
                act.activation(hs[:, 1, 0:groups], hs[:, 0, 0:groups], ACT.Sqrt, scale=1.0 / width, bias=eps[:, 0:1]).then_inc(hn_rt, 1)

            def project(n):
                norm_heads(norm_no("Q", n), ("Q", n), view(("Q", n), 1024), filled(("Q", n)), 16, DA_D)
                norm_heads(norm_no("K", n), ("K", n), view(("K", n), 1024), filled(("K", n)), 16, DA_D)
                g = NT * (n - 1)
                copy(("V", n), V[:, g:g + NT, :].rearrange("p a b -> p (a b)"), 1024)
                for t in range(NT):
                    copy(("QT", n, t), qT[:, :, t * P:(t + 1) * P], DA_H, P)
                for t in range(NT):
                    copy(("KT", n, t), kT[:, :, (g + t) * P:(g + t + 1) * P], DA_H, P)
                copy(("GQK", n), gqk.rearrange("p a b -> p (a b)"), 1024)
                batches.upto(("GG", n))
                act.wait_ge(*filled(("GG", n)))
                act.activation(ggT, view(("GG", n), T)[0:GL_R, :], ACT.Copy).then_inc(free_sem(("GG", n)), 1)
                batches.upto(("GL", n))
                act.wait_ge(*filled(("GL", n)))
                for hp in range(2):
                    ins = act.activation(gb[:, hp, :], view(("GL", n), 2, T)[:, hp, :], ACT.Identity, bias=b_gate[:, hp:hp + 1])
                ins.then_inc(free_sem(("GL", n)), 1)
                norm_heads(norm_no("XQ", n), ("XQ", n), view(("XQ", n), 1024), filled(("XQ", n)), 8, XA_D)

            def gla_prepare(n):
                a1 = gqi.rearrange("p a b -> p (a b)")
                act.wait_ge(*evacuated(("GL", n)))
                act.wait_ge(*evacuated(("OV", n, 7)))
                after(act.activation(a1, gb.rearrange("p a b -> p (a b)"), ACT.Abs))
                after(act.activation(a1, a1, ACT.Exp, scale=-1.0))
                act.activation(a1, a1, ACT.Ln, bias=1.0).then_inc(gla_ln, 1)
                act.wait_ge(gla_args, n)
                act.activation(a1, gb.rearrange("p a b -> p (a b)"), ACT.Exp, scale=1.0 / GL_TAU)
                a2 = gqt.rearrange("p a b -> p (a b)")
                act.activation(a2, a2, ACT.Exp, scale=1.0 / GL_TAU)
                a3 = gkt.rearrange("p a b c -> p (a b c)")
                act.activation(a3, a3, ACT.Exp, scale=1.0 / GL_TAU)
                a4 = gkd.rearrange("p a b -> p (a b)")
                act.activation(a4, a4, ACT.Exp, scale=1.0 / GL_TAU)
                last = gb.rearrange("p a (c s) -> p (a c) s", s=CH)[:, :, CH - 1]
                act.activation(gebl[:, :], last, ACT.Exp, scale=1.0 / GL_TAU).then_inc(gla_exps, 1)

            def memory_attention(n):
                copy(("XQT", n), xqT.rearrange("p a b -> p (a b)"), 1024)
                for t in range(NT):
                    job = ("XS", n, t)
                    batches.upto(job)
                    act.wait_ge(xmax_ready, NT * (n - 1) + t + 1)
                    if t:
                        batches.upto(("XPT", n, t - 1))
                        act.wait_ge(*filled(("XPT", n, t - 1)))
                    for h in range(XA_H):
                        ins = act.activation(px[:, h, :], view(job, XA_H, T)[:, h, :], ACT.Exp, scale=XA_D ** -0.5,
                                             bias=small[:, 4 + h:5 + h], accum_out=small[:, 8 + h:9 + h])
                    ins.then_inc(free_sem(job), 1)
                    copy(("XPT", n, t), pxT.rearrange("p a b c -> p (a b c)"), 1024)
                    copy(("XO", n, t), oT[2][:, :, t * P:(t + 1) * P], 4, P)

            def diff_attention(n):
                us = units()

                def exps(u):
                    t, h = us[u]
                    cols = (NT * (n - 1) + t + 1) * P
                    for m in range(2):
                        job = ("S", n, u, m)
                        batches.upto(job)
                        act.wait_ge(smax_ready, 16 * (n - 1) + 2 * u + m + 1)
                        if m == 0 and u >= 2:
                            batches.upto(("WT", n, u - 2))
                            act.wait_ge(*filled(("WT", n, u - 2)))
                        if m == 1 and u:
                            act.wait_ge(wgt_ready, 8 * (n - 1) + u)
                        dst = pw[:, u % 2, 0:cols] if m == 0 else p1[:, 0:cols]
                        act.activation(dst, view(job, cols), ACT.Exp, scale=SLOPE[h], bias=small[:, 14 + 2 * (u % 2) + m:15 + 2 * (u % 2) + m],
                                       accum_out=small[:, 18 + 2 * (u % 2) + m:19 + 2 * (u % 2) + m]).then_inc(free_sem(job), 1)

                def evacuate(u):
                    t, h = us[u]
                    cols = (NT * (n - 1) + t + 1) * P
                    copy(("WT", n, u), wT[:, 0:cols], cols)

                for u in range(len(us)):
                    exps(u)
                    if u:
                        evacuate(u - 1)
                evacuate(len(us) - 1)

            def gla(n):
                copy(("GV", n), gv.rearrange("p a b -> p (a b)"), 1024)
                copy(("KD", n), kdT.rearrange("p a b c -> p (a b c)"), 512)
                for c in range(T // CH):
                    t, c2 = c // 2, c % 2
                    tok = slice(CH * c2, CH * (c2 + 1))
                    job = ("GO", n, c)
                    batches.upto(job)
                    act.wait_ge(*filled(job))
                    act.activation(ogl[tok, t, :, :].rearrange("p a b -> p (a b)"), view(job, 512)[tok, :], ACT.Copy).then_inc(free_sem(job), 1)

            def merge(n):
                batches.upto(("GR", n))
                act.wait_ge(*filled(("GR", n)))
                act.activation(gr.rearrange("p a b -> p (a b)"), view(("GR", n), 1024), ACT.Sigmoid).then_inc(sig_ready, 1)
                norm_heads(norm_no("DA", n), ("GR", n), oda[:, :, :, :].rearrange("p a b c -> p (a b c)"), evacuated(("OV", n, 7)), 8, DA_V)
                act.wait_ge(*evacuated(("GO", n, T // CH - 1)))
                norm_heads(norm_no("GLA", n), ("GR", n), ogl[:, :, :, :].rearrange("p a b c -> p (a b c)"), evacuated(("GO", n, T // CH - 1)), 8, GL_V)
                copy(("OT", n, 0), oT[0].rearrange("p a b -> p (a b)"), 1024)
                copy(("OT", n, 1), oT[1].rearrange("p a b -> p (a b)"), 1024)
                for i in range(6):
                    job = ("GATE", n, i // 3, i % 3)
                    batches.upto(job)
                    act.wait_ge(*filled(job))
                    if i:
                        act.wait_ge(*evacuated(("BR", n, (i - 1) // 3, (i - 1) % 3)))
                    act.activation(sg.rearrange("p a b -> p (a b)"), view(job, 1024), ACT.Sigmoid).then_inc(free_sem(job), 1)

            def route(n):
                batches.upto(("WO", n, 1))
                norm_rows(None, [evacuated(("WO", n, 1))] * NT)
                for t in range(NT):
                    copy(("X2T", n, t), xn2T[:, :, t * P:(t + 1) * P], KC, P)

                def scores(j):
                    if j:
                        act.wait_ge(top_done, 4 * (n - 1) + j)
                    copy(("SC", n, j), sc.rearrange("p a b c -> p (a b c)"), 1024)

                for j in range(4):
                    copy(("WQ", n, j), qp[:, j % 2, :], 1024)
                    if j:
                        scores(j - 1)
                scores(3)
                for t in range(NT):
                    i = NT * (n - 1) + t + 1
                    batches.upto(("R", n, 4 * t + 1))
                    act.wait_ge(sm_arg, i)
                    act.activation(bf[:, 4, :, :].rearrange("p a b -> p (a b)"), bf[:, 4, :, :].rearrange("p a b -> p (a b)"), ACT.Exp).then_inc(sm_exp, 1)

            def gelu(b, q):
                hold(act, dot_done, b * BATCH + BATCH)
                act.activation(acts[:, q, :], dots[:, q, :], ACT.Gelu).then_inc(gelu_done, 1)

            def slot(b):
                if b % (NT * NB) + LEAD < NT * NB:
                    gelu(b + LEAD, (b + LEAD) % RING)

            batches = Batches(slot)
            act.wait_ge(const_ready, 1)
            act.activation(lam[:, 2:4], lam[:, 0:2], ACT.Exp).then_inc(lam_exp, 1)
            for n in range(STEPS + 1):
                norm_rows(n, [(x_in[t], 16 * max(2 * n, 1)) for t in range(NT)])
                act.wait_ge(norm_rs, n + 1)
                for t in range(NT):
                    act.activation(xhat[:, t, :], xs[:, t, :], ACT.Copy, scale=st2[:, 4 + t:5 + t]).then_inc(xhat_ready, 1)
                if n == 0:
                    norm_heads(1, ("MK", 0), view(("MK", 0), 1024), filled(("MK", 0)), 8, XA_D)
                    copy(("MV", 0), mv[:, :, :].rearrange("p a b -> p (a b)"), 1024)
                    copy(("MKT", 0), mkT[:, :, :].rearrange("p a b -> p (a b)"), 1024)
                    continue
                project(n)
                memory_attention(n)
                diff_attention(n)
                gla_prepare(n)
                gla(n)
                merge(n)
                route(n)
                batches.upto(("R", n, RANKS - 1))
                first = NT * NB * (n - 1)
                for b in range(first, first + LEAD):
                    gelu(b, b % RING)
            with act.Fori(0, TURNS - 1) as j:
                for q in range(RING):
                    gelu(j * RING + (first + LEAD + q), (LEAD + q) % RING)
            for b in range(first + NT * NB - RING + LEAD, first + NT * NB):
                gelu(b, b % RING)

        @block.vector
        def _(dve):
            own = [0]

            def after(ins):
                own[0] += 1
                ins.then_inc(dve_own, 1)
                dve.wait_ge(dve_own, own[0])

            def flat(x):
                names = "abcd"[:len(x.shape) - 1]
                return x.rearrange(f"p {' '.join(names)} -> p ({' '.join(names)})")

            def wide(x, *shape):
                return x.broadcast_to([x.shape[0], *shape])

            def norm_rows(no):
                dve.wait_ge(norm_sq, no)
                ins = dve.reciprocal(st2[:, 4:6], st2[:, 2:4])
                return ins

            def norm_heads(no, src, dst, groups, width, weight, release=None):
                if release is not None:
                    batches.upto(release)
                dve.wait_ge(hn_sq, no)
                dve.tensor_reduce(hs[:, 0, 0:groups], sq.rearrange("p (g d) -> p g d", d=width), AX, ALU.add).then_inc(hn_ss, 1)
                dve.wait_ge(hn_rt, no)
                after(dve.reciprocal(hs[:, 2, 0:groups], hs[:, 1, 0:groups]))
                ins = dve.tensor_tensor(dst, src, wide(hs[:, 2, 0:groups].unsqueeze(2), groups, width), ALU.mult)
                if release is not None:
                    ins.then_inc(free_sem(release), 1)
                    dve.wait_ge(*evacuated(release))
                else:
                    after(ins)
                dve.tensor_tensor(weight[0](dst), weight[0](dst), weight[1], ALU.mult).then_inc(hn_done, 1)

            def grouped(x):
                return x

            def by_tile(x):
                return x.rearrange("p (t g) d -> p t g d", t=NT)

            def heads_of(x):
                return x.rearrange("p a b c -> p (a b) c")

            def project(n):
                norm_heads(norm_no("Q", n), view(("Q", n), 16, DA_D), heads_of(qn), 16, DA_D,
                           (by_tile, wide(w_qs[:, :, :].unsqueeze(1), NT, 2 * DA_H, DA_D)), ("Q", n))
                norm_heads(norm_no("K", n), view(("K", n), 16, DA_D), heads_of(kn), 16, DA_D,
                           (grouped, wide(w_k64[:, :].unsqueeze(1), 16, DA_D)), ("K", n))
                norm_heads(norm_no("XQ", n), view(("XQ", n), 8, XA_D), heads_of(xq), 8, XA_D,
                           (grouped, wide(w_xq[:, :].unsqueeze(1), 8, XA_D)), ("XQ", n))

            def gla_prepare(n):
                dve.wait_ge(gla_ln, n)
                after(dve.scalar_tensor_tensor(flat(gqt), flat(gb), 0.0, flat(gqi), ALU.min, ALU.subtract))
                for hp in range(2):
                    ins = dve.tensor_tensor_scan(gb[:, hp, :], reset, gqt[:, hp, :], 0.0, ALU.mult, ALU.add)
                after(ins)
                blocks = gb.rearrange("p a (i s) -> p (a i) s", s=SUB)
                ref = blocks[:, :, SUB // 2]
                dve.tensor_tensor(gqt.rearrange("p a (i s) -> p (a i) s", s=SUB), blocks,
                                  wide(ref.unsqueeze(2), 2 * T // SUB, SUB), ALU.subtract)
                chunks = gb.rearrange("p a (c s) -> p a c s", s=CH)
                for hp in range(2):
                    r = gb[:, hp, :].rearrange("p (c i s) -> p c i s", i=CH // SUB, s=SUB)[:, :, :, SUB // 2]
                    dve.tensor_tensor(gkt[:, hp, :, :].rearrange("p c (i s) -> p c i s", s=CH),
                                      wide(r.unsqueeze(3), T // CH, CH // SUB, CH),
                                      wide(chunks[:, hp, :, :].unsqueeze(2), T // CH, CH // SUB, CH), ALU.subtract)
                c2 = gb.rearrange("p a (c s) -> p (a c) s", s=CH)
                after(dve.tensor_tensor(gkd.rearrange("p a (c s) -> p (a c) s", s=CH), wide(c2[:, :, CH - 1:CH], 2 * T // CH, CH), c2, ALU.subtract))
                dve.tensor_scalar(flat(gqt), flat(gqt), CLAMP, None, ALU.min)
                dve.tensor_scalar(flat(gkt), flat(gkt), CLAMP, None, ALU.min).then_inc(gla_args, 1)
                dve.wait_ge(gla_exps, n)
                q = flat(gqk[:, 0:2, :])
                dve.scalar_tensor_tensor(flat(gqi), q, GL_K ** -0.5, flat(gqi), ALU.mult, ALU.mult)
                dve.scalar_tensor_tensor(flat(gqt), q, GL_K ** -0.5, flat(gqt), ALU.mult, ALU.mult)
                for hp in range(2):
                    x = gkt[:, hp, :, :].rearrange("p c (i s) -> p c i s", s=CH)
                    k = gqk[:, 2 + hp, :].rearrange("p (c s) -> p c s", s=CH)
                    dve.tensor_tensor(x, x, wide(k.unsqueeze(2), T // CH, CH // SUB, CH), ALU.mult)
                dve.tensor_tensor(flat(gkd), flat(gkd), flat(gqk[:, 2:4, :]), ALU.mult).then_inc(gla_ops, 1)

            def memory_attention(n):
                for t in range(NT):
                    job = ("XS", n, t)
                    batches.upto(job)
                    dve.wait_ge(*filled(job))
                    after(dve.tensor_reduce(small[:, 0:4], view(job, XA_H, T), AX, ALU.max))
                    dve.tensor_scalar(small[:, 4:8], small[:, 0:4], -XA_D ** -0.5, None, ALU.mult).then_inc(xmax_ready, 1)
                    dve.wait_ge(*evacuated(job))
                    after(dve.reciprocal(small[:, 8:12], small[:, 8:12]))
                    dve.tensor_tensor(px, px, wide(small[:, 8:12].unsqueeze(2), XA_H, T), ALU.mult).then_inc(px_ready, 1)

            def diff_attention(n):
                us = units()

                def maxima(u):
                    t, h = us[u]
                    g = NT * (n - 1) + t
                    cols = (g + 1) * P
                    for m in range(2):
                        job = ("S", n, u, m)
                        i = 2 * (u % 2) + m
                        batches.upto(job)
                        dve.wait_ge(*filled(job))
                        ps = view(job, cols)
                        after(dve.tensor_tensor_reduce(out=ps, in0=ps, in1=dist[:, SEQ - P - g * P:SEQ - P - g * P + cols], scale=1.0, scalar=LOWEST,
                                                       op0=ALU.add, op1=ALU.max, accum_out=small[:, 22 + i:23 + i]))
                        dve.tensor_scalar(small[:, 14 + i:15 + i], small[:, 22 + i:23 + i], -SLOPE[h], None, ALU.mult).then_inc(smax_ready, 1)

                def combine(u):
                    t, h = us[u]
                    cols = (NT * (n - 1) + t + 1) * P
                    z = 18 + 2 * (u % 2)
                    dve.wait_ge(*evacuated(("S", n, u, 0)))
                    dve.wait_ge(*evacuated(("S", n, u, 1)))
                    after(dve.reciprocal(small[:, z:z + 2], small[:, z:z + 2]))
                    after(dve.tensor_scalar(p1[:, 0:cols], p1[:, 0:cols], small[:, z + 1:z + 2], lam[:, 0:1], ALU.mult, ALU.mult))
                    w = pw[:, u % 2, 0:cols]
                    dve.scalar_tensor_tensor(w, w, small[:, z:z + 1], p1[:, 0:cols], ALU.mult, ALU.add).then_inc(wgt_ready, 1)

                def values(u):
                    t, h = us[u]
                    job = ("OV", n, u)
                    batches.upto(job)
                    dve.wait_ge(*filled(job))
                    dve.tensor_copy(oda[:, t, h, :], view(job, P)).then_inc(free_sem(job), 1)

                for u in range(len(us)):
                    maxima(u)
                    combine(u)
                    if u:
                        values(u - 1)
                values(len(us) - 1)

            def gla(n):
                dve.wait_ge(gla_ops, n)
                after(dve.memset(at_s, 0.0))
                for t in range(NT):
                    job = ("AT", n, t)
                    batches.upto(job)
                    dve.wait_ge(*filled(job))
                    ps = view(job, 2, HALF)[:, :, 0:2 * CH].rearrange("p two (hp s) -> p two hp s", s=CH)
                    for c2 in range(2):
                        tok = slice(CH * c2, CH * (c2 + 1))
                        ins = dve.tensor_tensor(at_s[tok, t, c2, :, :].rearrange("p (hp two) s -> p two hp s", two=2), ps[tok, :, :, :],
                                                tri[tok, :].unsqueeze(1).unsqueeze(1).broadcast_to([CH, 2, 2, CH]), ALU.mult)
                    ins.then_inc(free_sem(job), 1)
                for c in range(T // CH):
                    job = ("SU", n, c)
                    batches.upto(job)
                    dve.wait_ge(*filled(job))
                    for h in range(GL_H):
                        i = 4 * (h // 2) + c
                        rows = slice(GL_K * (h % 2), GL_K * (h % 2 + 1))
                        ins = dve.scalar_tensor_tensor(state[rows, h, :], state[rows, h, :], gebl[rows, i:i + 1], view(job, 2, GL_V)[rows, h // 2, :],
                                                       ALU.mult, ALU.add)
                    ins.then_inc(free_sem(job), 1)
                    dve.wait_ge(*evacuated(job))

            def merge(n):
                job = ("GR", n)
                batches.upto(job)
                dve.wait_ge(sig_ready, n)
                g2 = flat(gr)
                dve.tensor_tensor(g2, view(job, 1024), g2, ALU.mult).then_inc(free_sem(job), 1)
                dve.wait_ge(*evacuated(job))
                g3 = gr.rearrange("p t (h d) -> p (t h) d", d=GL_V)
                dve.tensor_tensor(g3, g3, wide(w_glo[:, :].unsqueeze(1), 8, GL_V), ALU.mult).then_inc(gr_ready, 1)
                norm_heads(norm_no("DA", n), heads_of(oda[:, :, :, :]), heads_of(oda[:, :, :, :]), 8, DA_V,
                           (grouped, wide(w_dao[:, :].unsqueeze(1), 8, DA_V)))
                dve.wait_ge(gr_ready, n)
                norm_heads(norm_no("GLA", n), heads_of(ogl[:, :, :, :]), heads_of(ogl[:, :, :, :]), 8, GL_V,
                           (grouped, gr.rearrange("p t (h d) -> p (t h) d", d=GL_V)))
                for hf in range(2):
                    m = flat(merged[:, 4 * hf:4 * hf + 4, :])
                    for b in range(3):
                        job = ("BR", n, hf, b)
                        batches.upto(("GATE", n, hf, b))
                        dve.wait_ge(*evacuated(("GATE", n, hf, b)))
                        batches.upto(job)
                        dve.wait_ge(*filled(job))
                        dve.tensor_tensor(m if b == 0 else flat(tmp), view(job, 1024), flat(sg), ALU.mult).then_inc(free_sem(job), 1)
                        dve.wait_ge(*evacuated(job))
                        if b:
                            ins = dve.tensor_tensor(m, m, flat(tmp), ALU.add)
                            if (hf, b) == (1, 2):
                                ins.then_inc(merged_ready, 1)
                            else:
                                after(ins)
                for t in range(NT):
                    dve.wait_ge(x_in[t], 16 * (2 * n + 1))
                for nb in range(2):
                    job = ("WO", n, nb)
                    batches.upto(job)
                    dve.wait_ge(*filled(job))
                    x = xs[:, :, nb * HALF:(nb + 1) * HALF]
                    dve.tensor_tensor(x, view(job, NT, HALF), x, ALU.add).then_inc(free_sem(job), 1)

            def top16(values, best, where):
                for step in range(2):
                    s = slice(8 * step, 8 * step + 8)
                    for v, b in zip(values, best):
                        ins = dve.max(b[:, s], v)
                    after(ins)
                    for v, b, w in zip(values, best, where):
                        ins = dve.max_index(w[:, s], b[:, s], v)
                    after(ins)
                    if step == 0:
                        for v, b in zip(values, best):
                            ins = dve.match_replace(v, b[:, s], v, LOWEST)
                        after(ins)

            def route(n):
                batches.upto(("WO", n, 1))
                after(norm_rows(2 * n + 1))
                for t in range(NT):
                    dve.scalar_tensor_tensor(xn2[:, n % 2, t, :], xs[:, t, :], st2[:, 4 + t:5 + t], w_ffn[:, :], ALU.mult, ALU.mult).then_inc(xn2_ready, 1)
                for j in range(4):
                    batches.upto(("SC", n, j))
                    dve.wait_ge(*evacuated(("SC", n, j)))
                    rows = [(t, i) for t in range(NT) for i in range(4)]
                    top16([sc[:, t, i, :] for t, i in rows], [tv[:, t, 4 * j + i, :] for t, i in rows], [ti[:, t, 4 * j + i, :] for t, i in rows])
                    dve.memset(st2[:, 7:8], 0.0).then_inc(top_done, 1)
                for t in range(NT):
                    batches.upto(("R", n, 4 * t))
                    v = tv[:, t, :, :].rearrange("p (h two) k -> p h two k", two=2)
                    for h in range(HEADS):
                        ins = dve.tensor_tensor(cand[:, h, :, :], wide(v[:, h, 0, :].unsqueeze(2), TOPK, TOPK),
                                                wide(v[:, h, 1, :].unsqueeze(1), TOPK, TOPK), ALU.add)
                    after(ins)
                    flats = [cand[:, h, :, :].rearrange("p a b -> p (a b)") for h in range(HEADS)]
                    top16(flats, [bv[:, h, :] for h in range(HEADS)], [bj[:, 0, h, :] for h in range(HEADS)])
                    batches.upto(("R", n, 4 * t + 1))
                    dve.tensor_tensor(bf[:, 4, :, :], bv, wide(bv[:, :, 0:1], HEADS, TOPK), ALU.subtract).then_inc(sm_arg, 1)
                    after(dve.tensor_scalar(flat(bj[:, 1, :, :]), flat(bj[:, 0, :, :]), 4, None, ALU.logical_shift_right))
                    after(dve.tensor_scalar(flat(bj[:, 0, :, :]), flat(bj[:, 0, :, :]), TOPK - 1, None, ALU.bitwise_and))
                    dve.tensor_copy(flat(bf[:, 0, :, :]), flat(bj[:, 1, :, :]))
                    dve.tensor_copy(flat(bf[:, 1, :, :]), flat(bj[:, 0, :, :]))
                    after(dve.tensor_copy(flat(tif), flat(ti[:, t, :, :])))
                    keys = tif.rearrange("p (h two) k -> p h two k", two=2)
                    for s in range(2):
                        batches.upto(("R", n, 4 * t + 2 + s))
                        for h in range(HEADS):
                            ins = dve.tensor_tensor(cand[:, h, :, :], wide(bf[:, s, h, :].unsqueeze(2), TOPK, TOPK),
                                                    wide(iota.unsqueeze(1), TOPK, TOPK), ALU.is_equal)
                        after(ins)
                        for h in range(HEADS):
                            ins = dve.tensor_tensor(cand[:, h, :, :], cand[:, h, :, :], wide(keys[:, h, s, :].unsqueeze(1), TOPK, TOPK), ALU.mult)
                        after(ins)
                        after(dve.tensor_reduce(flat(bf[:, 2 + s, :, :]), cand.rearrange("p h a b -> p (h a) b"), AX, ALU.add))
                    dve.scalar_tensor_tensor(idx[:, n % 2, t * P:(t + 1) * P], flat(bf[:, 2, :, :]), float(NKEY), flat(bf[:, 3, :, :]), ALU.mult, ALU.add)
                    dve.wait_ge(sm_exp, NT * (n - 1) + t + 1)
                    after(dve.tensor_reduce(bf[:, 5, :, 0], bf[:, 4, :, :], AX, ALU.add))
                    after(dve.reciprocal(bf[:, 5, :, 1], bf[:, 5, :, 0]))
                    after(dve.tensor_tensor(gw[:, n % 2, t * P:(t + 1) * P].rearrange("p (h k) -> p h k", k=TOPK), bf[:, 4, :, :],
                                            wide(bf[:, 5, :, 1].unsqueeze(2), HEADS, TOPK), ALU.mult))

            def put(n, rel, q):
                dve.tensor_copy(stage[:, q, :], idx[:, n % 2, bass.ds(rel * BATCH, BATCH)]).then_inc(staged, 1)

            def dot(n, t, rel, q):
                for k in range(BATCH):
                    s = (q % 2) * BATCH + k
                    hold(dve, u_landed[s], landed(rel + NT * NB * (n - 1), q))
                    u = ub[:, s, :]
                    dve.tensor_tensor_reduce(out=u, in0=u, in1=xn2[:, n % 2, t, :], scale=1.0, scalar=0.0, op0=ALU.mult, op1=ALU.add,
                                             accum_out=dots[:, q, k:k + 1]).then_inc(dot_done, 1)

            def weigh(n, rel, q):
                b = rel + NT * NB * (n - 1)
                hold(dve, gelu_done, b + 1)
                if not isinstance(b, int) or b >= 2:
                    hold(dve, rows_added, b - 1)
                for k in range(BATCH):
                    ins = dve.tensor_scalar(diag[:, (q % 2) * BATCH + k, :], ident, acts[:, q, k:k + 1],
                                            gw[:, n % 2, bass.ds(rel * BATCH + k, 1)], ALU.mult, ALU.mult)
                ins.then_inc(diag_ready, 1)

            def begin(n):
                for rel in range(LAG + 2):
                    put(n, rel, rel)
                for rel in range(LAG):
                    dot(n, 0, rel, rel)

            def take(n, t, rel, q):
                inside = not isinstance(rel, int)
                if not inside and rel == NB + 1:
                    finish(n, 0)
                if inside or rel + LAG < NT * NB:
                    dot(n, t, rel + LAG, (q + LAG) % RING)
                weigh(n, rel, q)
                if inside or rel + LAG + 2 < NT * NB:
                    put(n, rel + LAG + 2, (q + LAG + 2) % RING)

            def finish(n, t):
                g = NT * (n - 1) + t
                dve.wait_ge(fin_in, 16 * (g + 1))
                dve.wait_ge(rows_added, (g + 1) * NB)
                dve.tensor_tensor(fin[:, :], acc[:, :], fin[:, :], ALU.add).then_inc(y_ready, 1)

            def slot(b):
                n, rel = b // (NT * NB) + 1, b % (NT * NB)
                take(n, min(rel + LAG, NT * NB - 1) // NB, rel, rel % RING)

            batches = Batches(slot)

            dve.memset(eps[:, :], EPS)
            dve.memset(state[:, :, :], 0.0).then_inc(state_zero, 1)
            dve.wait_ge(consts_in, N_CONST)
            dve.tensor_tensor(w_qs[:, :, :], wide(w_q64[:, :].unsqueeze(1), 2 * DA_H, DA_D), wide(qscale.unsqueeze(2), 2 * DA_H, DA_D), ALU.mult)
            dve.tensor_scalar(w_dao[:, :], w_dao[:, :], 1.0 - LAM_INIT, None, ALU.mult)
            for i in range(2):
                x, z = lam_in[:, 2 * i * DA_D:(2 * i + 1) * DA_D], lam_in[:, (2 * i + 1) * DA_D:(2 * i + 2) * DA_D]
                ins = dve.tensor_tensor_reduce(out=x, in0=x, in1=z, scale=1.0, scalar=0.0, op0=ALU.mult, op1=ALU.add, accum_out=lam[:, i:i + 1])
            ins.then_inc(const_ready, 1)
            dve.wait_ge(lam_exp, 1)
            after(dve.tensor_tensor(lam[:, 1:2], lam[:, 3:4], lam[:, 2:3], ALU.subtract))
            after(dve.tensor_scalar(lam[:, 0:1], lam[:, 1:2], -LAM_INIT, None, ALU.add))

            for n in range(STEPS + 1):
                norm_rows(max(2 * n, 1)).then_inc(norm_rs, 1)
                for t in range(NT):
                    job = ("XT", n, t)
                    batches.upto(job)
                    dve.wait_ge(*filled(job))
                    dve.tensor_tensor(xnT[:, :, t * P:(t + 1) * P], view(job, KC, P), wide(w_cols[:, min(n, 1), :].unsqueeze(2), KC, P),
                                      ALU.mult).then_inc(free_sem(job), 1)
                if n == 0:
                    norm_heads(1, view(("MK", 0), 8, XA_D), heads_of(xq), 8, XA_D, (grouped, wide(w_xk[:, :].unsqueeze(1), 8, XA_D)), ("MK", 0))
                    continue
                project(n)
                memory_attention(n)
                diff_attention(n)
                gla_prepare(n)
                gla(n)
                merge(n)
                route(n)
                if n > 1:
                    batches.upto(("R", n, RANKS - 1))
                    finish(n - 1, 1)
                begin(n)
            n = STEPS
            for t in range(NT):
                for rel in range(t * NB, t * NB + RING):
                    take(n, t, rel, rel % RING)
                with dve.Fori(1, NB // RING - 1) as j:
                    for q in range(RING):
                        take(n, t, j * RING + (t * NB + q), q)
                for rel in range((t + 1) * NB - RING, (t + 1) * NB):
                    take(n, min(rel + LAG, NT * NB - 1) // NB, rel, rel % RING)
            finish(n, 1)


def kernel(x, mem, mix_norm_w, w_in, da_q_norm_w, da_k_norm_w, da_lambda, da_out_norm_w,
           gla_w_gate, gla_b_gate, gla_out_norm_w, mem_norm_w, w_mem_kv, xa_q_norm_w, xa_k_norm_w,
           w_br_da, w_br_gla, w_br_xa, w_out, ffn_norm_w, peer_w_q, peer_sub_keys, peer_u, peer_v):
    import concourse.bacc as bacc
    from concourse.bass_utils import run_bass_kernel_spmd

    def cols(w):
        return np.ascontiguousarray(np.asarray(w).reshape(-1, P).T)

    arrays = {
        "x": np.asarray(x)[0], "mem": np.asarray(mem)[0], "consts": constant_table(),
        "mix_w": cols(mix_norm_w), "mem_w": cols(mem_norm_w), "w_in": np.asarray(w_in)[0],
        "q_w": np.asarray(da_q_norm_w)[0], "k_w": np.asarray(da_k_norm_w)[0], "lam": np.asarray(da_lambda).reshape(-1),
        "dao_w": np.asarray(da_out_norm_w)[0], "w_gate": np.asarray(gla_w_gate)[0], "b_gate": cols(gla_b_gate),
        "glo_w": np.asarray(gla_out_norm_w)[0], "w_mkv": np.asarray(w_mem_kv)[0], "xq_w": np.asarray(xa_q_norm_w)[0],
        "xk_w": np.asarray(xa_k_norm_w)[0], "br0": np.asarray(w_br_da)[0], "br1": np.asarray(w_br_gla)[0],
        "br2": np.asarray(w_br_xa)[0], "w_out": np.asarray(w_out)[0], "ffn_w": np.asarray(ffn_norm_w)[0],
        "w_q": np.asarray(peer_w_q)[0], "keysT": np.ascontiguousarray(np.asarray(peer_sub_keys)[0].transpose(2, 0, 1)),
        "peer_u": np.asarray(peer_u)[0], "peer_v": np.asarray(peer_v)[0],
    }
    nc = bacc.Bacc("TRN2", target_bir_lowering=False, num_devices=1)
    args = {}
    feed = {}
    for name, v in arrays.items():
        feed[f"in_{name}"] = np.ascontiguousarray(v)
        args[name] = nc.dram_tensor(f"in_{name}", v.shape, mybir.dt.from_np(v.dtype), kind="ExternalInput").ap()
    args["y"] = nc.dram_tensor("out_y", (SEQ, D), F32, kind="ExternalOutput").ap()
    build(nc, args)
    r = run_bass_kernel_spmd(nc, [feed], core_ids=[0])
    return r.results[0]["out_y"].reshape(1, SEQ, D)
```

```python
from contextlib import ExitStack

import numpy as np

import concourse.bass as bass
from concourse import mybir

F32 = mybir.dt.float32
U32 = mybir.dt.uint32
ALU = mybir.AluOpType
ACT = mybir.ActivationFunctionType
AX = mybir.AxisListType.X

P = 128
D = 1024
SEQ = 1024
KC = D // P
NT = 2
T = NT * P
STEPS = SEQ // T
EPS = 1e-6
DA_H, DA_D, DA_V = 4, 64, 128
GL_H, GL_K, GL_V, GL_R, GL_TAU = 4, 64, 128, 16, 16.0
CH = 64
SUB = 16
CLAMP = 60.0 * GL_TAU
XA_H, XA_D = 4, 128
HEADS, NKEY, TOPK = 8, 128, 16
LAM_INIT = 0.8 - 0.6 * 1.0
SLOPE = [2.0 ** (-8.0 * (h + 1) / DA_H) for h in range(DA_H)]
MASKED = -1.0e30
LOWEST = -3.0e38
WHOLE, SHORT = 4, 4
CAND = WHOLE * TOPK + (TOPK - WHOLE) * SHORT

C_DAQ, C_DAK, C_DAV = 0, 512, 1024
C_GQK, C_GV, C_GR, C_GG = 1536, 2048, 2560, 3072
C_XQ, C_GATE = 3088, 3600
HALF = 512

K_ID, K_TRI, K_RESET, K_IOTA, K_DIST, K_QS, K_END = 0, 128, 192, 448, 464, 1488, 1496


def constant_table():
    c = np.zeros((P, K_END), np.float32)
    p = np.arange(P)[:, None]
    c[:, K_ID:K_TRI] = np.eye(P)
    c[:, K_TRI:K_RESET] = (p % CH) <= np.arange(CH)[None]
    c[:, K_RESET:K_IOTA] = (np.arange(T) % CH != 0)[None]
    c[:, K_IOTA:K_DIST] = np.arange(TOPK)[None]
    dist = np.arange(SEQ)[None] - (SEQ - P) - p
    c[:, K_DIST:K_QS] = np.where(dist <= 0, dist, MASKED)
    c[:, K_QS:K_END] = [DA_D ** -0.5 / SLOPE[m // 2] for m in range(2 * DA_H)]
    return c


def units():
    return [(t, h) for t in range(NT) for h in range(DA_H)]


RANKS = 6


def front(n):
    return [("K", n), ("V", n), ("KT", n, 0), ("KT", n, 1), ("Q", n), ("GQK", n), ("QT", n, 0), ("QT", n, 1)]


def places_of(n):
    if n == 0:
        return [("XT", 0, 0), ("XT", 0, 1), ("MK", 0), ("MV", 0), ("MKT", 0), ("XT", 1, 0), ("XT", 1, 1)] + front(1)
    out = [("GG", n), ("GL", n), ("XQ", n)]
    out += [("XQT", n), ("XS", n, 0), ("XS", n, 1), ("XPT", n, 0), ("XO", n, 0), ("XPT", n, 1), ("XO", n, 1)]
    last = len(units()) - 1
    for u in range(len(units())):
        out += [("S", n, u, 0), ("S", n, u, 1)]
        if u:
            out += [("WT", n, u - 1), ("OV", n, u - 1)]
    out += [("WT", n, last), ("OV", n, last)]
    out += [("GV", n), ("KD", n)] + [("AT", n, t) for t in range(NT)]
    for c in range(T // CH):
        out += [("GO", n, c), ("SU", n, c)]
    out += [("GR", n), ("OT", n, 0), ("OT", n, 1)]
    for hf in range(2):
        for b in range(3):
            out += [("GATE", n, hf, b), ("BR", n, hf, b)]
    out += [("WO", n, 0), ("WO", n, 1)] + [("X2T", n, t) for t in range(NT)]
    out += [("WQ", n, 0), ("WQ", n, 1), ("SC", n, 0), ("WQ", n, 2), ("SC", n, 1)]
    if n < STEPS:
        out += [("XT", n + 1, 0), ("XT", n + 1, 1)]
    out += [("WQ", n, 3), ("SC", n, 2), ("SC", n, 3)]
    ranks = [[("R", n, t, i) for i in range(RANKS)] for t in range(NT)]
    if n < STEPS:
        f = front(n + 1)
        return out + f[:2] + ranks[0][:2] + f[2:4] + ranks[0][2:] + f[4:5] + ranks[1][:2] + f[5:] + ranks[1][2:]
    return out + ranks[0] + ranks[1]


NBANK = 3
JOBS = [job for n in range(STEPS + 1) for job in places_of(n) if job[0] != "R"]
PLACE = {job: (i % NBANK, i // NBANK) for i, job in enumerate(JOBS)}

W_BLOCKS = []


def need(kind, at, job, how):
    W_BLOCKS.extend((kind, at, job, (how, i)) for i in range(1 if how == "all" else 2))


for _nb in range(2):
    need("mkv", _nb * HALF, (("MK", 0), ("MV", 0))[_nb], "rows")
for _n in range(1, STEPS + 1):
    if _n == 1:
        for _job, _at in (("K", C_DAK), ("V", C_DAV), ("Q", C_DAQ), ("GQK", C_GQK)):
            need("in", _at, (_job, 1), "cols" if _job == "GQK" else "rows")
    for _job, _at in (("XQ", C_XQ), ("GV", C_GV), ("GR", C_GR)):
        need("in", _at, (_job, _n), "rows")
    for _hf in range(2):
        for _b in range(3):
            need("in", C_GATE + _b * D + _hf * HALF, ("GATE", _n, _hf, _b), "cols")
            need(f"br{_b}", _hf * HALF, ("BR", _n, _hf, _b), "all")
    for _nb in range(2):
        need("out", _nb * HALF, ("WO", _n, _nb), "rows")
    for _j in range(4):
        need("wq", _j * HALF, ("WQ", _n, _j), "cols")
    if _n < STEPS:
        for _job, _at in (("K", C_DAK), ("V", C_DAV), ("Q", C_DAQ), ("GQK", C_GQK)):
            need("in", _at, (_job, _n + 1), "cols" if _job == "GQK" else "rows")
W_SLOTS = 4
W_AT = {(job, part): i for i, (_, _, job, (_, part)) in enumerate(W_BLOCKS)}
W_FIRST = [job for _, _, job, part in W_BLOCKS if part in (("rows", 0), ("cols", 0))]

NORMS = [("MK", 0)] + [(what, n) for n in range(1, STEPS + 1) for what in ("K", "Q", "XQ", "DA", "GLA")]

RING, LAG, LEAD, PUT = 16, 4, 2, 12
DIAGS = 4
BEHIND = 2
NB = HEADS * TOPK


def row_slots(n):
    return 8 if n == STEPS else 4


assert PUT <= RING - DIAGS and NB % RING == 0

SPAN = {"GQK": 14, "QT": 1, "GG": 2, "GL": 2, "XQ": 14, "XQT": 3, "XS": 3, "XPT": 3, "XO": 3, "S": 3.3, "WT": 1, "OV": 3, "GV": 30, "KD": 3,
        "AT": 5, "GO": 2, "SU": 2, "GR": 14, "OT": 3, "GATE": 15, "BR": 8, "WO": 14, "X2T": 4, "WQ": 15, "SC": 5, "XT": 2,
        "K": 14, "V": 14, "Q": 14, "KT": 1, "R": 6}
BEFORE, SINCE = {}, {}


def spread():
    places = [p for n in range(STEPS + 1) for p in places_of(n)]
    starts = [places.index(("R", m, 1, 0)) for m in range(1, STEPS + 1)]
    for p in places[:starts[0]]:
        BEFORE[p] = SINCE[p] = 0
    for m, (at, end) in enumerate(zip(starts, starts[1:] + [len(places)])):
        total = sum(SPAN[p[0]] for p in places[at:end])
        count = NT * NB if m + 1 < STEPS else RING
        so_far = 0
        for p in places[at:end]:
            SINCE[p] = NT * NB * m + count * so_far / total
            so_far += SPAN[p[0]]
            BEFORE[p] = NT * NB * m + count * so_far / total


spread()


class Picks:

    def __init__(self, slot):
        self.slot, self.done = slot, 0

    def upto(self, job, share=1.0):
        target = int(SINCE[job] + (BEFORE[job] - SINCE[job]) * share + 0.001)
        while self.done < target:
            self.slot(self.done)
            self.done += 1


def build(nc, a):
    with ExitStack() as ctx:
        def sb(name, shape, dt=F32):
            return ctx.enter_context(nc.sbuf_tensor(name, shape, dt))

        def sem(name):
            return ctx.enter_context(nc.semaphore(name))

        consts = sb("consts", [P, K_END])
        ident = consts[:, K_ID:K_TRI]
        tri = consts[:, K_TRI:K_RESET]
        reset = consts[:, K_RESET:K_IOTA]
        iota = consts[:, K_IOTA:K_DIST]
        dist = consts[:, K_DIST:K_QS]
        qscale = consts[:, K_QS:K_END]
        eps = sb("eps", [P, 1])
        w_cols = sb("w_cols", [P, 2, KC])
        w_q64 = sb("w_q64", [P, DA_D])
        w_qs = sb("w_qs", [P, 2 * DA_H, DA_D])
        w_k64 = sb("w_k64", [P, DA_D])
        w_dao = sb("w_dao", [P, DA_V])
        w_glo = sb("w_glo", [P, GL_V])
        w_xq = sb("w_xq", [P, XA_D])
        w_xk = sb("w_xk", [P, XA_D])
        w_ffn = sb("w_ffn", [P, D])
        lam = sb("lam", [P, 4])
        b_gate = sb("b_gate", [P, 2])
        w_gate = sb("w_gate", [GL_R, GL_H * GL_K])
        w_gg = sb("w_gg", [P, KC, GL_R])
        keysT = sb("keysT", [P, 2, NKEY])
        mkT = sb("mkT", [P, XA_H, T])
        mv = sb("mv", [P, NT, XA_H * XA_D])
        kT = sb("kT", [P, DA_H, SEQ])
        V = sb("V", [P, SEQ // P, DA_H * DA_V])
        state = sb("state", [P, GL_H, GL_V])
        W = sb("W", [P, W_SLOTS, KC * HALF // 2])
        xs = sb("xs", [P, NT, D])
        xnT = sb("xnT", [P, KC, T])
        oT_xa = sb("oT_xa", [P, 4, T])
        xn2 = sb("xn2", [P, 2, NT, D])
        idx = sb("idx", [P, 2, NT * HEADS * TOPK], U32)
        gw = sb("gw", [P, 2, NT * HEADS * TOPK])
        st2 = sb("st2", [P, 8])
        hs = sb("hs", [P, 3, 16])
        small = sb("small", [P, 32])
        ub = sb("ub", [P, row_slots(1), D])
        vb = sb("vb", [P, row_slots(1), D])
        diag = sb("diag", [P, DIAGS, P])
        stage = sb("stage", [P, RING], U32)
        dots = sb("dots", [P, RING])
        acts = sb("acts", [P, RING])
        fin = sb("fin", [P, D])
        gebl = sb("gebl", [P, 8])
        qT = sb("qT", [P, DA_H, T])
        AREA = 6144
        arena = sb("arena", [P, AREA])

        def parts(x, *shape):
            names = "abcd"[:len(shape)]
            if len(shape) == 1:
                return x
            return x.rearrange(f"p ({' '.join(names)}) -> p {' '.join(names)}", **{c: s for c, s in zip(names[1:], shape[1:])})

        def area(at, *shape):
            assert at + int(np.prod(shape)) <= AREA
            return parts(arena[:, at:at + int(np.prod(shape))], *shape)

        sq = area(AREA - 1024, 1024)
        wT = area(AREA - 1024, SEQ)
        w_rows = W[:, :, :].rearrange("p i n -> p (i n)").rearrange("p (r d) -> p r d", d=D)
        more = row_slots(STEPS) - row_slots(1)
        u_rows = [ub[:, i, :] for i in range(row_slots(1))] + [w_rows[:, i, :] for i in range(more)]
        v_rows = [vb[:, i, :] for i in range(row_slots(1))] + [w_rows[:, more + i, :] for i in range(more)]
        lam_in = area(2048, 4 * DA_D)
        sq_front = area(1024, 1024)
        kn = qn = area(2048, NT, 2 * DA_H, DA_D)
        gqk = area(0, 4, T)
        gb = area(1024, 2, T)
        xq = area(3584, NT, XA_H, XA_D)
        ggT = area(4608, T)[0:GL_R, :]
        xqT = area(1536, XA_H, T)
        px = area(2560, XA_H, T)
        pxT = area(3584, XA_H, 2, P)
        pw = area(1536, 2, SEQ)
        p1 = area(3584, SEQ)
        oda = parts(xs[:, 0, :], NT, DA_H, DA_V)
        ogl = parts(xs[:, 1, :], NT, GL_H, GL_V)
        soft = sb("soft", [P, 2, T])
        gqi = area(1536, 2, T)
        gqt = area(2048, 2, T)
        gkt = area(2560, 2, 4, 256)
        gkd = area(4608, 2, T)
        kdT = area(0, NT, 2, P)
        at_s = area(512, NT, 2, GL_H, CH)
        gv = area(AREA - 1024, NT, GL_H * GL_V)
        gr = area(0, NT, GL_H * GL_V)
        oT = [area(4096, 4, T), area(5120, 4, T), oT_xa]
        merged = area(0, KC, T)
        sg = area(2048, 4, T)
        tmp = area(3072, 4, T)
        sc = area(0, NT, 4, NKEY)
        xn2T = area(1024, KC, T)
        qp = area(3072, 2, 4 * T)
        hot = area(0, HEADS // 2, TOPK, TOPK)
        cand = area(3072, HEADS, CAND)
        bv = area(3072 + HEADS * CAND, HEADS, TOPK)
        bj = area(4096, 4, HEADS, TOPK).bitcast(U32)
        tif = area(4608, 16, TOPK)
        bf = sb("bf", [P, 8, HEADS, TOPK])
        tv = area(5120, NT, 16, TOPK)
        ti = area(5632, NT, 16, TOPK).bitcast(U32)

        bank = [ctx.enter_context(nc.psum_tensor(f"bank{i}", [P, 1024], F32)) for i in range(NBANK)]
        acc = ctx.enter_context(nc.psum_tensor("acc", [P, D], F32))

        bank_full = [sem(f"bank_full{i}") for i in range(NBANK)]
        bank_free = [sem(f"bank_free{i}") for i in range(NBANK)]
        consts_in = sem("consts_in")
        x_in = [sem(f"x_in{t}") for t in range(NT)]
        w_in = [sem(f"w_in{i}") for i in range(W_SLOTS)]
        w_half = sem("w_half")
        x1_out = sem("x1_out")
        fin_in = sem("fin_in")
        y_out = sem("y_out")
        const_ready = sem("const_ready")
        lam_exp = sem("lam_exp")
        norm_sq = sem("norm_sq")
        norm_rs = sem("norm_rs")
        xhat_ready = sem("xhat_ready")
        hn_sq = sem("hn_sq")
        hn_ss = sem("hn_ss")
        hn_rt = sem("hn_rt")
        hn_done = sem("hn_done")
        sig_ready = sem("sig_ready")
        gla_ln = sem("gla_ln")
        gla_args = sem("gla_args")
        gla_exps = sem("gla_exps")
        gla_ops = sem("gla_ops")
        gr_ready = sem("gr_ready")
        state_zero = sem("state_zero")
        smax_ready = sem("smax_ready")
        wgt_ready = sem("wgt_ready")
        xmax_ready = sem("xmax_ready")
        px_ready = sem("px_ready")
        merged_ready = sem("merged_ready")
        xn2_ready = sem("xn2_ready")
        top_done = sem("top_done")
        sm_arg = sem("sm_arg")
        sm_exp = sem("sm_exp")
        route_done = sem("route_done")
        staged = sem("staged")
        u_landed = [sem(f"u_landed{k}") for k in range(row_slots(STEPS))]
        v_landed = [sem(f"v_landed{k}") for k in range(row_slots(STEPS))]
        dot_done = sem("dot_done")
        gelu_done = sem("gelu_done")
        diag_ready = sem("diag_ready")
        rows_added = sem("rows_added")
        y_ready = sem("y_ready")
        act_own = sem("act_own")
        dve_own = sem("dve_own")

        def claim(eng, job):
            b, n = PLACE[job]
            if n:
                eng.wait_ge(bank_free[b], n)
            return bank[b], bank_full[b]

        def filled(job):
            b, n = PLACE[job]
            return bank_full[b], n + 1

        def evacuated(job):
            b, n = PLACE[job]
            return bank_free[b], n + 1

        def free_sem(job):
            return bank_free[PLACE[job][0]]

        def view(job, *shape):
            return parts(bank[PLACE[job][0]][:, 0:int(np.prod(shape))], *shape)

        def hold(eng, s, value):
            if not isinstance(value, int):
                value = eng.to_reg(value)
                eng.wait_ge(consts_in, 16)
            eng.wait_ge(s, value)

        def w_slot(job, part=0):
            i = W_AT[job, part]
            k = KC if W_BLOCKS[i][3][0] == "cols" else KC // 2
            return parts(W[:, i % W_SLOTS, :], k, KC * HALF // 2 // k), w_in[i % W_SLOTS], 16 * (i // W_SLOTS + 1)

        def norm_no(what, n):
            return NORMS.index((what, n)) + 1

        def landed(n, b, q):
            slots, was = row_slots(n), row_slots(n - 1)
            first = NT * NB * (n - 1)
            before = 16 * (first // was) if q % slots < was else 0
            return (b - first - q % slots) * (16 // slots) + 16 + before

        block = ctx.enter_context(nc.Block())

        CONST_LOADS = [
            (consts[:, :], a["consts"]), (w_cols[:, 0, :], a["mem_w"]), (w_cols[:, 1, :], a["mix_w"]),
            (w_q64[:, :], a["q_w"].partition_broadcast(P)), (w_k64[:, :], a["k_w"].partition_broadcast(P)),
            (w_dao[:, :], a["dao_w"].partition_broadcast(P)), (w_glo[:, :], a["glo_w"].partition_broadcast(P)),
            (w_xq[:, :], a["xq_w"].partition_broadcast(P)), (w_xk[:, :], a["xk_w"].partition_broadcast(P)),
            (w_ffn[:, :], a["ffn_w"].partition_broadcast(P)), (lam_in[:, :], a["lam"].partition_broadcast(P)),
            (b_gate[:, :], a["b_gate"]), (w_gate[:, :], a["w_gate"]),
            (w_gg[:, :, :], a["w_in"][:, C_GG:C_GG + GL_R].rearrange("(k p) n -> p k n", p=P)),
            (keysT[:, :, :], a["keysT"]),
        ]
        N_CONST = 16 * len(CONST_LOADS)
        x_tiles = a["x"].rearrange("(g p) d -> g p d", p=P)
        mem_tiles = a["mem"].rearrange("(g p) d -> g p d", p=P)
        y_tiles = a["y"].rearrange("(g p) d -> g p d", p=P)
        w_dram = {"in": a["w_in"].rearrange("(k p) n -> p k n", p=P), "mkv": a["w_mkv"].rearrange("(k p) n -> p k n", p=P),
                  **{f"br{b}": a[f"br{b}"].rearrange("(k p) n -> p k n", p=P) for b in range(3)},
                  "out": a["w_out"].rearrange("(k p) n -> p k n", p=P), "wq": a["w_q"].rearrange("(k p) n -> p k n", p=P)}

        @block.sync
        def _(sp):
            for t in range(NT):
                sp.dma_start(xs[:, t, :], mem_tiles[t]).then_inc(x_in[t], 16)
            for dst, src in CONST_LOADS:
                sp.dma_start(dst, src).then_inc(consts_in, 16)
            loaded = [0]

            def load_blocks(last_job):
                end = max(i for i, block in enumerate(W_BLOCKS) if block[2] == last_job) + 1
                for i in range(loaded[0], end):
                    kind, col, job, (how, part) = W_BLOCKS[i]
                    if i >= W_SLOTS:
                        _, _, was, (was_how, was_part) = W_BLOCKS[i - W_SLOTS]
                        if was_how == "all" or was_part:
                            sp.wait_ge(*filled(was))
                        else:
                            sp.wait_ge(w_half, W_FIRST.index(was) + 1)
                    w = w_dram[kind]
                    if how == "rows":
                        w = w[:, part * (KC // 2):(part + 1) * (KC // 2), col:col + HALF]
                    elif how == "cols":
                        w = w[:, :, col + part * (HALF // 2):col + (part + 1) * (HALF // 2)]
                    else:
                        w = w[:, :, col:col + HALF]
                    dst, s, _ = w_slot(job, part)
                    sp.dma_start(dst, w).then_inc(s, 16)
                loaded[0] = end

            def load_x(n):
                for t in range(NT):
                    sp.dma_start(xs[:, t, :], x_tiles[NT * (n - 1) + t]).then_inc(x_in[t], 16)

            load_blocks(("MV", 0))
            sp.wait_ge(*filled(("XT", 0, 1)))
            load_x(1)
            load_blocks(("GQK", 1))
            for n in range(1, STEPS + 1):
                load_blocks(("GATE", n, 0, 0))
                sp.wait_ge(*filled(("OT", n, 1)))
                load_x(n)
                load_blocks(("WO", n, 1))
                sp.wait_ge(*evacuated(("WO", n, 1)))
                for t in range(NT):
                    sp.dma_start(y_tiles[NT * (n - 1) + t], xs[:, t, :]).then_inc(x1_out, 16)
                load_blocks(("WQ", n, 0))
                if n < STEPS:
                    sp.wait_ge(x1_out, 16 * NT * n)
                    sp.wait_ge(xn2_ready, NT * n)
                    load_x(n + 1)
                load_blocks(("WQ", n, 3))
                if n < STEPS:
                    load_blocks(("GQK", n + 1))
            sp.wait_ge(y_out, 16 * SEQ // P)

        @block.gpsimd
        def _(pool):
            def gather_u(n, b, q):
                slots = row_slots(n)
                hold(pool, staged, b + 1)
                if not isinstance(b, int) or b >= slots:
                    hold(pool, dot_done, b - slots + 1)
                pool.indirect_dma_start(u_rows[q % slots], None, a["peer_u"],
                                        bass.IndirectOffsetOnAxis(ap=stage[:, q:q + 1], axis=0)).then_inc(u_landed[q % slots], 16)

            def gather_v(n, b, q):
                slots = row_slots(n)
                if not isinstance(b, int) or b >= slots:
                    hold(pool, rows_added, b - slots + 1)
                pool.indirect_dma_start(v_rows[q % slots], None, a["peer_v"],
                                        bass.IndirectOffsetOnAxis(ap=stage[:, q:q + 1], axis=0)).then_inc(v_landed[q % slots], 16)

            def x1_back(n, t):
                g = NT * (n - 1) + t
                pool.wait_ge(x1_out, 16 * NT * n)
                if g:
                    pool.wait_ge(y_out, 16 * g)
                pool.dma_start(fin[:, :], y_tiles[g]).then_inc(fin_in, 16)

            def store(n, t):
                g = NT * (n - 1) + t
                pool.wait_ge(y_ready, g + 1)
                pool.dma_start(y_tiles[g], fin[:, :]).then_inc(y_out, 16)

            pool.wait_ge(consts_in, N_CONST)
            for n in range(1, STEPS + 1):
                first = NT * NB * (n - 1)
                if n == STEPS:
                    pool.wait_ge(*filled(("WQ", n, 3)))
                for i in range(LAG):
                    gather_u(n, first + i, i)
                x1_back(n, 0)

                def turn(at, edge):
                    for q in range(RING):
                        gather_v(n, at + q, q)
                        if edge is None or edge * RING + q + LAG < NT * NB:
                            gather_u(n, at + q + LAG, (q + LAG) % RING)
                        if edge is not None and edge * RING + q == NB + 8:
                            store(n, 0)
                            x1_back(n, 1)

                for t in range(NT):
                    per = NB // RING
                    turn(first + t * NB, t * per)
                    with pool.Fori(1, per - 1) as j:
                        turn(j * RING + (first + t * NB), None)
                    turn(first + (t + 1) * NB - RING, (t + 1) * per - 1)
                store(n, 1)

        @block.tensor
        def _(pe):
            def token_major(job, out_of):
                ps, full = claim(pe, job)
                for part in range(2):
                    w, s, v = w_slot(job, part)
                    pe.wait_ge(s, v)
                    for t in range(NT):
                        if part or t:
                            picks.upto(job, (2 * part + t) / 4)
                        for k in range(KC // 2):
                            mm = pe.matmul(ps[:, t * HALF:(t + 1) * HALF], out_of[:, part * (KC // 2) + k, t * P:(t + 1) * P], w[:, k, :],
                                           start=part == 0 and k == 0, stop=part == 1 and k == KC // 2 - 1)
                    mm.then_inc(full if part else w_half, 1)
                picks.upto(job)

            def channel_major(job, rhs):
                ps, full = claim(pe, job)
                for c in range(4):
                    w, s, v = w_slot(job, c // 2)
                    if c % 2 == 0:
                        pe.wait_ge(s, v)
                    if c:
                        picks.upto(job, c / 4)
                    for k in range(KC):
                        mm = pe.matmul(ps[:, c * T:(c + 1) * T], w[:, k, (c % 2) * P:(c % 2 + 1) * P], rhs[:, k, :],
                                       start=k == 0, stop=k == KC - 1)
                    if c == 1:
                        mm.then_inc(w_half, 1)
                mm.then_inc(full, 1)
                picks.upto(job)

            def turn(job, blocks, after):
                picks.upto(job)
                ps, full = claim(pe, job)
                for w in after:
                    pe.wait_ge(*w)
                for i, src in enumerate(blocks):
                    mm = pe.transpose(ps[:, i * P:(i + 1) * P], src, ident)
                mm.then_inc(full, 1)

            def turn_x(n):
                for t in range(NT):
                    turn(("XT", n, t), [xs[:, t, k * P:(k + 1) * P] for k in range(KC)], [(xhat_ready, NT * n + t + 1)])

            def project_front(n):
                pe.wait_ge(*evacuated(("XT", n, 1)))
                token_major(("K", n), xnT)
                token_major(("V", n), xnT)
                for t in range(NT):
                    turn(("KT", n, t), [kn[:, t, 2 * h:2 * h + 2, :].rearrange("p a b -> p (a b)") for h in range(DA_H)],
                         [(hn_done, norm_no("K", n))])
                token_major(("Q", n), xnT)
                if n > 2:
                    catch_up(n - 2)
                channel_major(("GQK", n), xnT)
                for t in range(NT):
                    turn(("QT", n, t), [qn[:, t, 2 * h:2 * h + 2, :].rearrange("p a b -> p (a b)") for h in range(DA_H)],
                         [(hn_done, norm_no("Q", n))])

            def project(n):
                picks.upto(("GG", n))
                ps, full = claim(pe, ("GG", n))
                for k in range(KC):
                    mm = pe.matmul(ps[0:GL_R, 0:T], w_gg[:, k, :], xnT[:, k, :], start=k == 0, stop=k == KC - 1)
                mm.then_inc(full, 1)
                picks.upto(("GL", n))
                ps, full = claim(pe, ("GL", n))
                pe.wait_ge(*evacuated(("GG", n)))
                for hp in range(2):
                    mm = pe.matmul(ps[:, hp * T:(hp + 1) * T], w_gate[:, hp * P:(hp + 1) * P], ggT, start=True, stop=True)
                mm.then_inc(full, 1)
                token_major(("XQ", n), xnT)

            def memory_attention(n):
                turn(("XQT", n), [xq[:, t, h, :] for h in range(XA_H) for t in range(NT)], [(hn_done, norm_no("XQ", n))])
                for t in range(NT):
                    picks.upto(("XS", n, t))
                    ps, full = claim(pe, ("XS", n, t))
                    pe.wait_ge(*evacuated(("XQT", n)))
                    for h in range(XA_H):
                        mm = pe.matmul(ps[:, h * T:(h + 1) * T], xqT[:, h, t * P:(t + 1) * P], mkT[:, h, :], start=True, stop=True)
                    mm.then_inc(full, 1)
                for t in range(NT):
                    turn(("XPT", n, t), [px[:, h, m * P:(m + 1) * P] for h in range(XA_H) for m in range(2)],
                         [(px_ready, NT * (n - 1) + t + 1)])
                    picks.upto(("XO", n, t))
                    ps, full = claim(pe, ("XO", n, t))
                    pe.wait_ge(*evacuated(("XPT", n, t)))
                    for h in range(XA_H):
                        for m in range(2):
                            mm = pe.matmul(ps[:, h * P:(h + 1) * P], mv[:, m, h * XA_D:(h + 1) * XA_D], pxT[:, h, m, :],
                                           start=m == 0, stop=m == 1)
                    mm.then_inc(full, 1)

            def diff_attention(n):
                us = units()

                def scores(u):
                    t, h = us[u]
                    cols = (NT * (n - 1) + t + 1) * P
                    for m in range(2):
                        picks.upto(("S", n, u, m))
                        ps, full = claim(pe, ("S", n, u, m))
                        if u == 0 and m == 0:
                            pe.wait_ge(*evacuated(("QT", n, 1)))
                            pe.wait_ge(*evacuated(("KT", n, 1)))
                        rows = slice(DA_D * m, DA_D * (m + 1))
                        for c in range(0, cols, HALF):
                            w = min(HALF, cols - c)
                            mm = pe.matmul(ps[:, c:c + w], qT[rows, h, t * P:(t + 1) * P], kT[rows, h, c:c + w], start=True, stop=True)
                        mm.then_inc(full, 1)

                def values(u):
                    t, h = us[u]
                    nb = NT * (n - 1) + t + 1
                    turn(("WT", n, u), [pw[:, u % 2, k * P:(k + 1) * P] for k in range(nb)],
                         [(wgt_ready, len(us) * (n - 1) + u + 1)])
                    picks.upto(("OV", n, u))
                    ps, full = claim(pe, ("OV", n, u))
                    pe.wait_ge(*evacuated(("WT", n, u)))
                    for k in range(nb):
                        mm = pe.matmul(ps[:, 0:P], wT[:, k * P:(k + 1) * P], V[:, k, h * DA_V:(h + 1) * DA_V], start=k == 0, stop=k == nb - 1)
                    mm.then_inc(full, 1)

                for u in range(len(us)):
                    scores(u)
                    if u:
                        values(u - 1)
                values(len(us) - 1)

            def gla(n):
                token_major(("GV", n), xnT)
                turn(("KD", n), [gkd[:, hp, t * P:(t + 1) * P] for t in range(NT) for hp in range(2)], [(gla_ops, n)])
                for t in range(NT):
                    picks.upto(("AT", n, t))
                    ps, full = claim(pe, ("AT", n, t))
                    for c2 in range(2):
                        c = 2 * t + c2
                        for h in range(GL_H):
                            rows = slice(GL_K * (h % 2), GL_K * (h % 2 + 1))
                            for i in range(CH // SUB):
                                at = (h % 2) * HALF + (h // 2) * CH + i * SUB
                                mm = pe.matmul(ps[CH * c2:CH * (c2 + 1), at:at + SUB],
                                               gkt[rows, h // 2, c, i * CH:(i + 1) * CH],
                                               gqt[rows, h // 2, c * CH + i * SUB:c * CH + (i + 1) * SUB], start=True, stop=True)
                    mm.then_inc(full, 1)
                for c in range(T // CH):
                    t, c2 = c // 2, c % 2
                    tok = slice(CH * c2, CH * (c2 + 1))
                    picks.upto(("GO", n, c))
                    ps, full = claim(pe, ("GO", n, c))
                    if c == 0:
                        pe.wait_ge(*evacuated(("KD", n)))
                        pe.wait_ge(*evacuated(("GV", n)))
                        pe.wait_ge(*(evacuated(("SU", n - 1, T // CH - 1)) if n > 1 else (state_zero, 1)))
                    else:
                        pe.wait_ge(*evacuated(("SU", n, c - 1)))
                    pe.wait_ge(*evacuated(("AT", n, t)))
                    for h in range(GL_H):
                        pe.matmul(ps[tok, h * GL_V:(h + 1) * GL_V], gqi[:, h // 2, c * CH:(c + 1) * CH], state[:, h, :],
                                  start=True, stop=False)
                        mm = pe.matmul(ps[tok, h * GL_V:(h + 1) * GL_V], at_s[:, t, c2, h, :], gv[:, t, h * GL_V:(h + 1) * GL_V],
                                       start=False, stop=True)
                    mm.then_inc(full, 1)
                    picks.upto(("SU", n, c))
                    ps, full = claim(pe, ("SU", n, c))
                    for h in range(GL_H):
                        rows = slice(GL_K * (h % 2), GL_K * (h % 2 + 1))
                        mm = pe.matmul(ps[rows, (h // 2) * GL_V:(h // 2 + 1) * GL_V], kdT[tok, t, h // 2, GL_K * (h % 2):GL_K * (h % 2 + 1)],
                                       gv[tok, t, h * GL_V:(h + 1) * GL_V], start=True, stop=True)
                    mm.then_inc(full, 1)

            def merge(n):
                token_major(("GR", n), xnT)
                turn(("OT", n, 0), [oda[:, t, h, :] for h in range(4) for t in range(NT)], [(hn_done, norm_no("DA", n))])
                turn(("OT", n, 1), [ogl[:, t, h, :] for h in range(4) for t in range(NT)], [(hn_done, norm_no("GLA", n))])
                for hf in range(2):
                    for b in range(3):
                        channel_major(("GATE", n, hf, b), xnT)
                        ps, full = claim(pe, ("BR", n, hf, b))
                        w, s, v = w_slot(("BR", n, hf, b))
                        pe.wait_ge(s, v)
                        pe.wait_ge(*evacuated(("OT", n, b) if b < 2 else ("XO", n, 1)))
                        for c in range(4):
                            if c:
                                picks.upto(("BR", n, hf, b), c / 4)
                            for k in range(4):
                                mm = pe.matmul(ps[:, c * T:(c + 1) * T], w[:, k, c * P:(c + 1) * P], oT[b][:, k, :], start=k == 0, stop=k == 3)
                        mm.then_inc(full, 1)
                        picks.upto(("BR", n, hf, b))
                pe.wait_ge(merged_ready, n)
                for nb in range(2):
                    token_major(("WO", n, nb), merged)

            def route(n):
                for t in range(NT):
                    turn(("X2T", n, t), [xn2[:, n % 2, t, k * P:(k + 1) * P] for k in range(KC)], [(xn2_ready, NT * (n - 1) + t + 1)])

                def score(j):
                    picks.upto(("SC", n, j))
                    ps, full = claim(pe, ("SC", n, j))
                    pe.wait_ge(*evacuated(("WQ", n, j)))
                    for t in range(NT):
                        for i in range(4):
                            mm = pe.matmul(ps[:, (4 * t + i) * NKEY:(4 * t + i + 1) * NKEY], qp[:, j % 2, i * T + t * P:i * T + (t + 1) * P],
                                           keysT[:, i % 2, :], start=True, stop=True)
                    mm.then_inc(full, 1)

                pe.wait_ge(*evacuated(("X2T", n, 1)))
                for j in range(4):
                    channel_major(("WQ", n, j), xn2T)
                    if j:
                        score(j - 1)
                    if j == 2 and n < STEPS:
                        turn_x(n + 1)
                score(3)

            def add_row(n, b, q, start=False, stop=False):
                hold(pe, diag_ready, b + 1)
                hold(pe, v_landed[q % row_slots(n)], landed(n, b, q))
                for c in range(2):
                    mm = pe.matmul(acc[:, c * HALF:(c + 1) * HALF], diag[:, q % DIAGS, :], v_rows[q % row_slots(n)][:, c * HALF:(c + 1) * HALF],
                                   start=start, stop=stop)
                mm.then_inc(rows_added, 1)

            def slot(b):
                if b % (NT * NB) >= BEHIND:
                    add(b - BEHIND)

            def catch_up(n):
                for b in range(NT * NB * n - BEHIND, NT * NB * n):
                    add(b)

            def add(b):
                if b % NB == 0 and b:
                    pe.wait_ge(y_ready, b // NB)
                add_row(b // (NT * NB) + 1, b, b % RING, start=b % NB == 0, stop=b % NB == NB - 1)

            picks = Picks(slot)

            pe.wait_ge(consts_in, N_CONST)
            for n in range(STEPS + 1):
                if n == 0:
                    turn_x(0)
                    pe.wait_ge(*evacuated(("XT", n, 1)))
                    token_major(("MK", 0), xnT)
                    token_major(("MV", 0), xnT)
                    turn(("MKT", 0), [xq[:, t, h, :] for h in range(XA_H) for t in range(NT)], [(hn_done, 1)])
                    turn_x(1)
                    project_front(1)
                    continue
                project(n)
                memory_attention(n)
                diff_attention(n)
                gla(n)
                merge(n)
                route(n)
                if n < STEPS:
                    project_front(n + 1)
            picks.upto(("R", n, 0, RANKS - 1))
            first = NT * NB * (STEPS - 1)
            catch_up(STEPS - 1)
            picks.upto(("R", n, 1, RANKS - 1))
            for t in range(NT):
                for b in range(first + t * NB if t else first + RING - BEHIND, first + t * NB + RING):
                    add(b)
                with pe.Fori(1, NB // RING - 1) as j:
                    for q in range(RING):
                        add_row(STEPS, j * RING + (first + t * NB + q), q)
                for b in range(first + (t + 1) * NB - RING, first + (t + 1) * NB):
                    add(b)

        @block.scalar
        def _(act):
            own = [0]

            def after(ins):
                own[0] += 1
                ins.then_inc(act_own, 1)
                act.wait_ge(act_own, own[0])

            def copy(job, dst, *shape):
                picks.upto(job)
                act.wait_ge(*filled(job))
                act.activation(dst, view(job, *shape), ACT.Copy).then_inc(free_sem(job), 1)

            def norm_rows(ready, squares):
                for t in range(NT):
                    act.wait_ge(*ready[t])
                    after(act.activation(squares, xs[:, t, :], ACT.Square, accum_out=st2[:, t:t + 1]))
                act.activation(st2[:, 2:4], st2[:, 0:2], ACT.Sqrt, scale=1.0 / D, bias=eps[:, 0:1]).then_inc(norm_sq, 1)

            def norm_heads(no, job, src, ready, groups, width, squares=sq):
                picks.upto(job)
                act.wait_ge(*ready)
                if no > 1:
                    act.wait_ge(hn_ss, no - 1)
                act.activation(squares, src, ACT.Square).then_inc(hn_sq, 1)
                act.wait_ge(hn_ss, no)
                act.activation(hs[:, 1, 0:groups], hs[:, 0, 0:groups], ACT.Sqrt, scale=1.0 / width, bias=eps[:, 0:1]).then_inc(hn_rt, 1)

            def square_x(n):
                if n:
                    act.wait_ge(*filled(("MV", 0) if n == 1 else ("GATE", n - 1, 1, 2)))
                norm_rows([(x_in[t], 16 * max(2 * n, 1)) for t in range(NT)], xnT[:, 0:4, :].rearrange("p a b -> p (a b)"))

            def scale_x(n):
                act.wait_ge(norm_rs, n + 1)
                for t in range(NT):
                    act.activation(xs[:, t, :], xs[:, t, :], ACT.Copy, scale=st2[:, 4 + t:5 + t]).then_inc(xhat_ready, 1)

            def project_front(n):
                norm_heads(norm_no("K", n), ("K", n), view(("K", n), 1024), filled(("K", n)), 16, DA_D, sq_front)
                g = NT * (n - 1)
                copy(("V", n), V[:, g:g + NT, :].rearrange("p a b -> p (a b)"), 1024)
                if n > 1:
                    ranked(n - 1, 0)
                for t in range(NT):
                    copy(("KT", n, t), kT[:, :, (g + t) * P:(g + t + 1) * P], DA_H, P)
                norm_heads(norm_no("Q", n), ("Q", n), view(("Q", n), 1024), filled(("Q", n)), 16, DA_D, sq_front)
                if n > 1:
                    first_gelus(n - 1)
                    ranked(n - 1, 1)
                else:
                    copy(("GQK", n), gqk.rearrange("p a b -> p (a b)"), 1024)
                for t in range(NT):
                    copy(("QT", n, t), qT[:, :, t * P:(t + 1) * P], DA_H, P)
                if n > 1:
                    picks.upto(("R", n - 1, 1, RANKS - 1))
                    act.wait_ge(route_done, NT * (n - 1))
                    copy(("GQK", n), gqk.rearrange("p a b -> p (a b)"), 1024)

            def project(n):
                picks.upto(("GG", n))
                act.wait_ge(*filled(("GG", n)))
                act.activation(ggT, view(("GG", n), T)[0:GL_R, :], ACT.Copy).then_inc(free_sem(("GG", n)), 1)
                picks.upto(("GL", n))
                act.wait_ge(*filled(("GL", n)))
                for hp in range(2):
                    ins = act.activation(gb[:, hp, :], view(("GL", n), 2, T)[:, hp, :], ACT.Identity, bias=b_gate[:, hp:hp + 1])
                ins.then_inc(free_sem(("GL", n)), 1)
                act.wait_ge(*evacuated(("GL", n)))
                ln = soft[:, :, :].rearrange("p a b -> p (a b)")
                after(act.activation(ln, gb.rearrange("p a b -> p (a b)"), ACT.Abs))
                after(act.activation(ln, ln, ACT.Exp, scale=-1.0))
                act.activation(ln, ln, ACT.Ln, bias=1.0).then_inc(gla_ln, 1)
                norm_heads(norm_no("XQ", n), ("XQ", n), view(("XQ", n), 1024), filled(("XQ", n)), 8, XA_D)

            def gla_prepare(n):
                a1 = gqi.rearrange("p a b -> p (a b)")
                picks.upto(("GV", n), 0.3)
                act.wait_ge(gla_args, n)
                act.activation(a1, gb.rearrange("p a b -> p (a b)"), ACT.Exp, scale=1.0 / GL_TAU)
                a2 = gqt.rearrange("p a b -> p (a b)")
                act.activation(a2, a2, ACT.Exp, scale=1.0 / GL_TAU)
                a3 = gkt.rearrange("p a b c -> p (a b c)")
                act.activation(a3, a3, ACT.Exp, scale=1.0 / GL_TAU)
                a4 = gkd.rearrange("p a b -> p (a b)")
                act.activation(a4, a4, ACT.Exp, scale=1.0 / GL_TAU)
                picks.upto(("GV", n), 0.6)
                last = gb.rearrange("p a (c s) -> p (a c) s", s=CH)[:, :, CH - 1]
                act.activation(gebl[:, :], last, ACT.Exp, scale=1.0 / GL_TAU).then_inc(gla_exps, 1)

            def memory_attention(n):
                copy(("XQT", n), xqT.rearrange("p a b -> p (a b)"), 1024)
                for t in range(NT):
                    job = ("XS", n, t)
                    picks.upto(job)
                    act.wait_ge(xmax_ready, NT * (n - 1) + t + 1)
                    if t:
                        picks.upto(("XPT", n, t - 1))
                        act.wait_ge(*filled(("XPT", n, t - 1)))
                    for h in range(XA_H):
                        ins = act.activation(px[:, h, :], view(job, XA_H, T)[:, h, :], ACT.Exp, scale=XA_D ** -0.5,
                                             bias=small[:, 4 + h:5 + h], accum_out=small[:, 8 + h:9 + h])
                    ins.then_inc(free_sem(job), 1)
                    copy(("XPT", n, t), pxT.rearrange("p a b c -> p (a b c)"), 1024)
                    copy(("XO", n, t), oT[2][:, :, t * P:(t + 1) * P], 4, P)

            def diff_attention(n):
                us = units()

                def exps(u):
                    t, h = us[u]
                    cols = (NT * (n - 1) + t + 1) * P
                    for m in range(2):
                        job = ("S", n, u, m)
                        picks.upto(job)
                        act.wait_ge(smax_ready, 16 * (n - 1) + 2 * u + m + 1)
                        if m == 0 and u >= 2:
                            picks.upto(("WT", n, u - 2))
                            act.wait_ge(*filled(("WT", n, u - 2)))
                        if m == 1 and u:
                            act.wait_ge(wgt_ready, 8 * (n - 1) + u)
                        dst = pw[:, u % 2, 0:cols] if m == 0 else p1[:, 0:cols]
                        act.activation(dst, view(job, cols), ACT.Exp, scale=SLOPE[h], bias=small[:, 14 + 2 * (u % 2) + m:15 + 2 * (u % 2) + m],
                                       accum_out=small[:, 18 + 2 * (u % 2) + m:19 + 2 * (u % 2) + m]).then_inc(free_sem(job), 1)

                def evacuate(u):
                    t, h = us[u]
                    cols = (NT * (n - 1) + t + 1) * P
                    copy(("WT", n, u), wT[:, 0:cols], cols)

                for u in range(len(us)):
                    exps(u)
                    if u:
                        evacuate(u - 1)
                evacuate(len(us) - 1)

            def gla(n):
                norm_heads(norm_no("DA", n), ("GV", n), oda[:, :, :, :].rearrange("p a b c -> p (a b c)"), evacuated(("OV", n, 7)), 8, DA_V)
                copy(("GV", n), gv.rearrange("p a b -> p (a b)"), 1024)
                copy(("KD", n), kdT.rearrange("p a b c -> p (a b c)"), 512)
                for c in range(T // CH):
                    t, c2 = c // 2, c % 2
                    tok = slice(CH * c2, CH * (c2 + 1))
                    job = ("GO", n, c)
                    picks.upto(job)
                    act.wait_ge(*filled(job))
                    act.activation(ogl[tok, t, :, :].rearrange("p a b -> p (a b)"), view(job, 512)[tok, :], ACT.Copy).then_inc(free_sem(job), 1)

            def merge(n):
                picks.upto(("GR", n))
                act.wait_ge(*filled(("GR", n)))
                act.activation(gr.rearrange("p a b -> p (a b)"), view(("GR", n), 1024), ACT.Sigmoid).then_inc(sig_ready, 1)
                act.wait_ge(*evacuated(("GO", n, T // CH - 1)))
                norm_heads(norm_no("GLA", n), ("GR", n), ogl[:, :, :, :].rearrange("p a b c -> p (a b c)"), evacuated(("GO", n, T // CH - 1)), 8, GL_V)
                copy(("OT", n, 0), oT[0].rearrange("p a b -> p (a b)"), 1024)
                copy(("OT", n, 1), oT[1].rearrange("p a b -> p (a b)"), 1024)
                for i in range(6):
                    job = ("GATE", n, i // 3, i % 3)
                    picks.upto(job)
                    act.wait_ge(*filled(job))
                    if i:
                        act.wait_ge(*evacuated(("BR", n, (i - 1) // 3, (i - 1) % 3)))
                    act.activation(sg.rearrange("p a b -> p (a b)"), view(job, 1024), ACT.Sigmoid).then_inc(free_sem(job), 1)

            def route(n):
                picks.upto(("WO", n, 1))
                norm_rows([evacuated(("WO", n, 1))] * NT, sq)
                for t in range(NT):
                    copy(("X2T", n, t), xn2T[:, :, t * P:(t + 1) * P], KC, P)

                def scores(j):
                    if j:
                        act.wait_ge(top_done, 4 * (n - 1) + j)
                    copy(("SC", n, j), sc.rearrange("p a b c -> p (a b c)"), 1024)

                for j in range(4):
                    if j == 2 and n < STEPS:
                        square_x(n + 1)
                    copy(("WQ", n, j), qp[:, j % 2, :], 1024)
                    if j:
                        scores(j - 1)
                    if j == 2 and n < STEPS:
                        scale_x(n + 1)
                scores(3)

            def ranked(n, t):
                picks.upto(("R", n, t, 1))
                act.wait_ge(sm_arg, NT * (n - 1) + t + 1)
                act.activation(bf[:, 4, :, :].rearrange("p a b -> p (a b)"), bf[:, 4, :, :].rearrange("p a b -> p (a b)"), ACT.Exp).then_inc(sm_exp, 1)

            def gelu(b, q):
                hold(act, dot_done, b + 1)
                act.activation(acts[:, q:q + 1], dots[:, q:q + 1], ACT.Gelu).then_inc(gelu_done, 1)

            def first_gelus(n):
                for b in range(NT * NB * (n - 1), NT * NB * (n - 1) + LEAD):
                    gelu(b, b % RING)

            def slot(b):
                if b % (NT * NB) + LEAD < NT * NB:
                    gelu(b + LEAD, (b + LEAD) % RING)

            picks = Picks(slot)
            act.wait_ge(const_ready, 1)
            act.activation(lam[:, 2:4], lam[:, 0:2], ACT.Exp).then_inc(lam_exp, 1)
            for n in range(STEPS + 1):
                if n == 0:
                    square_x(0)
                    scale_x(0)
                    norm_heads(1, ("MK", 0), view(("MK", 0), 1024), filled(("MK", 0)), 8, XA_D)
                    copy(("MV", 0), mv[:, :, :].rearrange("p a b -> p (a b)"), 1024)
                    copy(("MKT", 0), mkT[:, :, :].rearrange("p a b -> p (a b)"), 1024)
                    square_x(1)
                    scale_x(1)
                    project_front(1)
                    continue
                project(n)
                memory_attention(n)
                diff_attention(n)
                gla_prepare(n)
                gla(n)
                merge(n)
                route(n)
                if n < STEPS:
                    project_front(n + 1)
            ranked(STEPS, 0)
            picks.upto(("R", STEPS, 0, RANKS - 1))
            first_gelus(STEPS)
            ranked(STEPS, 1)
            picks.upto(("R", STEPS, 1, RANKS - 1))
            first = NT * NB * (STEPS - 1)
            with act.Fori(1, NT * NB // RING - 1) as j:
                for q in range(RING):
                    gelu(j * RING + (first + LEAD + q), (LEAD + q) % RING)
            for b in range(first + NT * NB - RING + LEAD, first + NT * NB):
                gelu(b, b % RING)

        @block.vector
        def _(dve):
            own = [0]

            def after(ins):
                own[0] += 1
                ins.then_inc(dve_own, 1)
                dve.wait_ge(dve_own, own[0])

            def flat(x):
                names = "abcd"[:len(x.shape) - 1]
                return x.rearrange(f"p {' '.join(names)} -> p ({' '.join(names)})")

            def wide(x, *shape):
                return x.broadcast_to([x.shape[0], *shape])

            def norm_rows(no):
                dve.wait_ge(norm_sq, no)
                ins = dve.reciprocal(st2[:, 4:6], st2[:, 2:4])
                return ins

            def norm_heads(no, src, dst, groups, width, weight, release=None, squares=sq):
                if release is not None:
                    picks.upto(release)
                dve.wait_ge(hn_sq, no)
                dve.tensor_reduce(hs[:, 0, 0:groups], squares.rearrange("p (g d) -> p g d", d=width), AX, ALU.add).then_inc(hn_ss, 1)
                dve.wait_ge(hn_rt, no)
                after(dve.reciprocal(hs[:, 2, 0:groups], hs[:, 1, 0:groups]))
                ins = dve.tensor_tensor(dst, src, wide(hs[:, 2, 0:groups].unsqueeze(2), groups, width), ALU.mult)
                if release is not None:
                    ins.then_inc(free_sem(release), 1)
                    dve.wait_ge(*evacuated(release))
                else:
                    after(ins)
                dve.tensor_tensor(weight[0](dst), weight[0](dst), weight[1], ALU.mult).then_inc(hn_done, 1)

            def grouped(x):
                return x

            def by_tile(x):
                return x.rearrange("p (t g) d -> p t g d", t=NT)

            def heads_of(x):
                return x.rearrange("p a b c -> p (a b) c")

            def take_x(n):
                for t in range(NT):
                    job = ("XT", n, t)
                    picks.upto(job)
                    dve.wait_ge(*filled(job))
                    dve.tensor_tensor(xnT[:, :, t * P:(t + 1) * P], view(job, KC, P), wide(w_cols[:, min(n, 1), :].unsqueeze(2), KC, P),
                                      ALU.mult).then_inc(free_sem(job), 1)

            def keys(n):
                norm_heads(norm_no("K", n), view(("K", n), 16, DA_D), heads_of(kn), 16, DA_D,
                           (grouped, wide(w_k64[:, :].unsqueeze(1), 16, DA_D)), ("K", n), sq_front)

            def queries(n):
                picks.upto(("Q", n))
                dve.wait_ge(*filled(("KT", n, 1)))
                norm_heads(norm_no("Q", n), view(("Q", n), 16, DA_D), heads_of(qn), 16, DA_D,
                           (by_tile, wide(w_qs[:, :, :].unsqueeze(1), NT, 2 * DA_H, DA_D)), ("Q", n), sq_front)

            def project(n):
                picks.upto(("GL", n))
                dve.wait_ge(gla_ln, n)
                after(dve.scalar_tensor_tensor(flat(soft[:, :, :]), flat(gb), 0.0, flat(soft[:, :, :]), ALU.min, ALU.subtract))
                for hp in range(2):
                    ins = dve.tensor_tensor_scan(gb[:, hp, :], reset, soft[:, hp, :], 0.0, ALU.mult, ALU.add)
                after(ins)
                norm_heads(norm_no("XQ", n), view(("XQ", n), 8, XA_D), heads_of(xq), 8, XA_D,
                           (grouped, wide(w_xq[:, :].unsqueeze(1), 8, XA_D)), ("XQ", n))

            def gla_prepare(n):
                dve.wait_ge(*evacuated(("OV", n, 7)))
                blocks = gb.rearrange("p a (i s) -> p (a i) s", s=SUB)
                ref = blocks[:, :, SUB // 2]
                dve.tensor_tensor(gqt.rearrange("p a (i s) -> p (a i) s", s=SUB), blocks,
                                  wide(ref.unsqueeze(2), 2 * T // SUB, SUB), ALU.subtract)
                chunks = gb.rearrange("p a (c s) -> p a c s", s=CH)
                for hp in range(2):
                    r = gb[:, hp, :].rearrange("p (c i s) -> p c i s", i=CH // SUB, s=SUB)[:, :, :, SUB // 2]
                    dve.tensor_tensor(gkt[:, hp, :, :].rearrange("p c (i s) -> p c i s", s=CH),
                                      wide(r.unsqueeze(3), T // CH, CH // SUB, CH),
                                      wide(chunks[:, hp, :, :].unsqueeze(2), T // CH, CH // SUB, CH), ALU.subtract)
                c2 = gb.rearrange("p a (c s) -> p (a c) s", s=CH)
                after(dve.tensor_tensor(gkd.rearrange("p a (c s) -> p (a c) s", s=CH), wide(c2[:, :, CH - 1:CH], 2 * T // CH, CH), c2, ALU.subtract))
                picks.upto(("GV", n), 0.3)
                dve.tensor_scalar(flat(gqt), flat(gqt), CLAMP, None, ALU.min)
                dve.tensor_scalar(flat(gkt), flat(gkt), CLAMP, None, ALU.min).then_inc(gla_args, 1)
                picks.upto(("GV", n), 0.6)
                dve.wait_ge(gla_exps, n)
                q = flat(gqk[:, 0:2, :])
                dve.scalar_tensor_tensor(flat(gqi), q, GL_K ** -0.5, flat(gqi), ALU.mult, ALU.mult)
                dve.scalar_tensor_tensor(flat(gqt), q, GL_K ** -0.5, flat(gqt), ALU.mult, ALU.mult)
                for hp in range(2):
                    x = gkt[:, hp, :, :].rearrange("p c (i s) -> p c i s", s=CH)
                    k = gqk[:, 2 + hp, :].rearrange("p (c s) -> p c s", s=CH)
                    dve.tensor_tensor(x, x, wide(k.unsqueeze(2), T // CH, CH // SUB, CH), ALU.mult)
                dve.tensor_tensor(flat(gkd), flat(gkd), flat(gqk[:, 2:4, :]), ALU.mult).then_inc(gla_ops, 1)

            def memory_attention(n):
                for t in range(NT):
                    job = ("XS", n, t)
                    picks.upto(job)
                    dve.wait_ge(*filled(job))
                    after(dve.tensor_reduce(small[:, 0:4], view(job, XA_H, T), AX, ALU.max))
                    dve.tensor_scalar(small[:, 4:8], small[:, 0:4], -XA_D ** -0.5, None, ALU.mult).then_inc(xmax_ready, 1)
                    if t:
                        picks.upto(("XO", n, 0))
                    dve.wait_ge(*evacuated(job))
                    after(dve.reciprocal(small[:, 8:12], small[:, 8:12]))
                    dve.tensor_tensor(px, px, wide(small[:, 8:12].unsqueeze(2), XA_H, T), ALU.mult).then_inc(px_ready, 1)

            def diff_attention(n):
                us = units()

                def maxima(u):
                    t, h = us[u]
                    g = NT * (n - 1) + t
                    cols = (g + 1) * P
                    for m in range(2):
                        job = ("S", n, u, m)
                        i = 2 * (u % 2) + m
                        picks.upto(job)
                        dve.wait_ge(*filled(job))
                        ps = view(job, cols)
                        after(dve.tensor_tensor_reduce(out=ps, in0=ps, in1=dist[:, SEQ - P - g * P:SEQ - P - g * P + cols], scale=1.0, scalar=LOWEST,
                                                       op0=ALU.add, op1=ALU.max, accum_out=small[:, 22 + i:23 + i]))
                        dve.tensor_scalar(small[:, 14 + i:15 + i], small[:, 22 + i:23 + i], -SLOPE[h], None, ALU.mult).then_inc(smax_ready, 1)

                def combine(u):
                    t, h = us[u]
                    cols = (NT * (n - 1) + t + 1) * P
                    z = 18 + 2 * (u % 2)
                    dve.wait_ge(*evacuated(("S", n, u, 0)))
                    dve.wait_ge(*evacuated(("S", n, u, 1)))
                    after(dve.reciprocal(small[:, z:z + 2], small[:, z:z + 2]))
                    after(dve.tensor_scalar(p1[:, 0:cols], p1[:, 0:cols], small[:, z + 1:z + 2], lam[:, 0:1], ALU.mult, ALU.mult))
                    w = pw[:, u % 2, 0:cols]
                    dve.scalar_tensor_tensor(w, w, small[:, z:z + 1], p1[:, 0:cols], ALU.mult, ALU.add).then_inc(wgt_ready, 1)

                def values(u):
                    t, h = us[u]
                    job = ("OV", n, u)
                    picks.upto(job)
                    dve.wait_ge(*filled(job))
                    dve.tensor_copy(oda[:, t, h, :], view(job, P)).then_inc(free_sem(job), 1)

                for u in range(len(us)):
                    maxima(u)
                    if u:
                        values(u - 1)
                    combine(u)
                values(len(us) - 1)

            def gla(n):
                picks.upto(("GV", n))
                norm_heads(norm_no("DA", n), heads_of(oda[:, :, :, :]), heads_of(oda[:, :, :, :]), 8, DA_V,
                           (grouped, wide(w_dao[:, :].unsqueeze(1), 8, DA_V)))
                dve.wait_ge(gla_ops, n)
                after(dve.memset(at_s, 0.0))
                for t in range(NT):
                    job = ("AT", n, t)
                    picks.upto(job)
                    dve.wait_ge(*filled(job))
                    ps = view(job, 2, HALF)[:, :, 0:2 * CH].rearrange("p two (hp s) -> p two hp s", s=CH)
                    for c2 in range(2):
                        tok = slice(CH * c2, CH * (c2 + 1))
                        ins = dve.tensor_tensor(at_s[tok, t, c2, :, :].rearrange("p (hp two) s -> p two hp s", two=2), ps[tok, :, :, :],
                                                tri[tok, :].unsqueeze(1).unsqueeze(1).broadcast_to([CH, 2, 2, CH]), ALU.mult)
                    ins.then_inc(free_sem(job), 1)
                for c in range(T // CH):
                    job = ("SU", n, c)
                    picks.upto(job)
                    dve.wait_ge(*filled(job))
                    for h in range(GL_H):
                        i = 4 * (h // 2) + c
                        rows = slice(GL_K * (h % 2), GL_K * (h % 2 + 1))
                        ins = dve.scalar_tensor_tensor(state[rows, h, :], state[rows, h, :], gebl[rows, i:i + 1], view(job, 2, GL_V)[rows, h // 2, :],
                                                       ALU.mult, ALU.add)
                    ins.then_inc(free_sem(job), 1)
                    dve.wait_ge(*evacuated(job))

            def merge(n):
                job = ("GR", n)
                picks.upto(job)
                dve.wait_ge(sig_ready, n)
                g2 = flat(gr)
                dve.tensor_tensor(g2, view(job, 1024), g2, ALU.mult).then_inc(free_sem(job), 1)
                dve.wait_ge(*evacuated(job))
                g3 = gr.rearrange("p t (h d) -> p (t h) d", d=GL_V)
                dve.tensor_tensor(g3, g3, wide(w_glo[:, :].unsqueeze(1), 8, GL_V), ALU.mult).then_inc(gr_ready, 1)
                dve.wait_ge(gr_ready, n)
                norm_heads(norm_no("GLA", n), heads_of(ogl[:, :, :, :]), heads_of(ogl[:, :, :, :]), 8, GL_V,
                           (grouped, gr.rearrange("p t (h d) -> p (t h) d", d=GL_V)))
                for hf in range(2):
                    m = flat(merged[:, 4 * hf:4 * hf + 4, :])
                    for b in range(3):
                        job = ("BR", n, hf, b)
                        picks.upto(("GATE", n, hf, b))
                        dve.wait_ge(*evacuated(("GATE", n, hf, b)))
                        picks.upto(job)
                        dve.wait_ge(*filled(job))
                        dve.tensor_tensor(m if b == 0 else flat(tmp), view(job, 1024), flat(sg), ALU.mult).then_inc(free_sem(job), 1)
                        dve.wait_ge(*evacuated(job))
                        if b:
                            ins = dve.tensor_tensor(m, m, flat(tmp), ALU.add)
                            if (hf, b) == (1, 2):
                                ins.then_inc(merged_ready, 1)
                            else:
                                after(ins)
                for t in range(NT):
                    dve.wait_ge(x_in[t], 16 * (2 * n + 1))
                for nb in range(2):
                    job = ("WO", n, nb)
                    picks.upto(job)
                    dve.wait_ge(*filled(job))
                    x = xs[:, :, nb * HALF:(nb + 1) * HALF]
                    dve.tensor_tensor(x, view(job, NT, HALF), x, ALU.add).then_inc(free_sem(job), 1)

            def top16(values, best, where, between=()):
                for step in range(2):
                    s = slice(8 * step, 8 * step + 8)
                    for v, b in zip(values, best):
                        ins = dve.max(b[:, s], v)
                    after(ins)
                    for v, b, w in zip(values, best, where):
                        ins = dve.max_index(w[:, s], b[:, s], v)
                    after(ins)
                    if between:
                        picks.upto(*between[step])
                    if step == 0:
                        for v, b in zip(values, best):
                            ins = dve.match_replace(v, b[:, s], v, LOWEST)
                        after(ins)

            def route(n):
                picks.upto(("WO", n, 1))
                after(norm_rows(2 * n + 1))
                for t in range(NT):
                    dve.scalar_tensor_tensor(xn2[:, n % 2, t, :], xs[:, t, :], st2[:, 4 + t:5 + t], w_ffn[:, :], ALU.mult, ALU.mult).then_inc(xn2_ready, 1)
                order = [("WQ", n, 2), ("WQ", n, 3), ("SC", n, 3), ("K", n + 1)]
                for j in range(4):
                    if n < STEPS and j == 1:
                        norm_rows(2 * n + 2).then_inc(norm_rs, 1)
                    if n < STEPS and j == 2:
                        take_x(n + 1)
                    picks.upto(("SC", n, j))
                    dve.wait_ge(*evacuated(("SC", n, j)))
                    rows = [(t, i) for t in range(NT) for i in range(4)]
                    top16([sc[:, t, i, :] for t, i in rows], [tv[:, t, 4 * j + i, :] for t, i in rows], [ti[:, t, 4 * j + i, :] for t, i in rows],
                          [(order[j], 0.4), (order[j], 0.8)] if j < 2 else [])
                    dve.memset(st2[:, 7:8], 0.0).then_inc(top_done, 1)
                if n < STEPS:
                    keys(n + 1)
                rank(n, 0)
                if n < STEPS:
                    queries(n + 1)
                picks.upto(("R", n, 0, RANKS - 1))
                if n > 1:
                    finish(n - 1, 1)
                begin(n)
                rank(n, 1)

            def rank(n, t):
                def part(i):
                    picks.upto(("R", n, t, i))

                part(0)
                v = tv[:, t, :, :].rearrange("p (h two) k -> p h two k", two=2)
                dve.tensor_tensor(cand[:, :, 0:WHOLE * TOPK].rearrange("p h (a b) -> p h a b", b=TOPK),
                                  wide(v[:, :, 0, 0:WHOLE].unsqueeze(3), HEADS, WHOLE, TOPK), wide(v[:, :, 1, :].unsqueeze(2), HEADS, WHOLE, TOPK), ALU.add)
                after(dve.tensor_tensor(cand[:, :, WHOLE * TOPK:].rearrange("p h (a b) -> p h a b", b=SHORT),
                                        wide(v[:, :, 0, WHOLE:].unsqueeze(3), HEADS, TOPK - WHOLE, SHORT),
                                        wide(v[:, :, 1, 0:SHORT].unsqueeze(2), HEADS, TOPK - WHOLE, SHORT), ALU.add))
                pos = flat(bj[:, 0, :, :])
                top16([cand[:, h, :] for h in range(HEADS)], [bv[:, h, :] for h in range(HEADS)], [bj[:, 0, h, :] for h in range(HEADS)])
                dve.tensor_tensor(bf[:, 4, :, :], bv, wide(bv[:, :, 0:1], HEADS, TOPK), ALU.subtract).then_inc(sm_arg, 1)
                part(1)
                dve.tensor_copy(flat(bf[:, 5, :, :]), pos)
                dve.tensor_scalar(flat(bj[:, 1, :, :]), pos, 4, None, ALU.logical_shift_right)
                dve.tensor_scalar(flat(bj[:, 2, :, :]), pos, 2, None, ALU.logical_shift_right)
                dve.tensor_scalar(flat(bj[:, 3, :, :]), pos, SHORT - 1, None, ALU.bitwise_and)
                after(dve.tensor_copy(flat(tif), flat(ti[:, t, :, :])))
                dve.tensor_copy(flat(bf[:, 0, :, :]), flat(bj[:, 1, :, :]))
                dve.tensor_copy(flat(bf[:, 1, :, :]), flat(bj[:, 2, :, :]))
                after(dve.tensor_copy(flat(bf[:, 2, :, :]), flat(bj[:, 3, :, :])))
                after(dve.tensor_scalar(pos, pos, TOPK - SHORT, None, ALU.bitwise_and))
                dve.tensor_copy(flat(bf[:, 3, :, :]), pos)
                after(dve.scalar_tensor_tensor(flat(bf[:, 0, :, :]), flat(bf[:, 1, :, :]), float(WHOLE - WHOLE * TOPK // SHORT), flat(bf[:, 0, :, :]),
                                               ALU.add, ALU.max))
                after(dve.scalar_tensor_tensor(flat(bf[:, 1, :, :]), flat(bf[:, 5, :, :]), float(WHOLE * TOPK), flat(bf[:, 3, :, :]), ALU.is_lt, ALU.mult))
                after(dve.tensor_tensor(flat(bf[:, 1, :, :]), flat(bf[:, 1, :, :]), flat(bf[:, 2, :, :]), ALU.add))
                key = tif.rearrange("p (h two) k -> p h two k", two=2)
                for s in range(2):
                    for half in range(2):
                        if s or half:
                            part(1 + 2 * s + half)
                        hh = slice(half * HEADS // 2, (half + 1) * HEADS // 2)
                        after(dve.tensor_tensor(hot, wide(bf[:, s, hh, :].unsqueeze(3), HEADS // 2, TOPK, TOPK),
                                                wide(iota.unsqueeze(1).unsqueeze(1), HEADS // 2, TOPK, TOPK), ALU.is_equal))
                        after(dve.tensor_tensor(hot, hot, wide(key[:, hh, s, :].unsqueeze(2), HEADS // 2, TOPK, TOPK), ALU.mult))
                        ins = dve.tensor_reduce(flat(bf[:, 2 + s, hh, :]), hot.rearrange("p h a b -> p (h a) b"), AX, ALU.add)
                        after(ins)
                part(5)
                dve.scalar_tensor_tensor(idx[:, n % 2, t * P:(t + 1) * P], flat(bf[:, 2, :, :]), float(NKEY), flat(bf[:, 3, :, :]), ALU.mult, ALU.add)
                dve.wait_ge(sm_exp, NT * (n - 1) + t + 1)
                after(dve.tensor_reduce(bf[:, 6, :, 0], bf[:, 4, :, :], AX, ALU.add))
                after(dve.reciprocal(bf[:, 6, :, 1], bf[:, 6, :, 0]))
                dve.tensor_tensor(gw[:, n % 2, t * P:(t + 1) * P].rearrange("p (h k) -> p h k", k=TOPK), bf[:, 4, :, :],
                                  wide(bf[:, 6, :, 1].unsqueeze(2), HEADS, TOPK), ALU.mult).then_inc(route_done, 1)
                dve.wait_ge(route_done, NT * (n - 1) + t + 1)

            def put(n, rel, q):
                dve.tensor_copy(stage[:, q:q + 1], idx[:, n % 2, bass.ds(rel, 1)]).then_inc(staged, 1)

            def dot(n, t, rel, q):
                u = u_rows[q % row_slots(n)]
                hold(dve, u_landed[q % row_slots(n)], landed(n, rel + NT * NB * (n - 1), q))
                dve.tensor_tensor_reduce(out=u, in0=u, in1=xn2[:, n % 2, t, :], scale=1.0, scalar=0.0, op0=ALU.mult, op1=ALU.add,
                                         accum_out=dots[:, q:q + 1]).then_inc(dot_done, 1)

            def weigh(n, rel, q):
                b = rel + NT * NB * (n - 1)
                hold(dve, gelu_done, b + 1)
                if not isinstance(b, int) or b >= DIAGS:
                    hold(dve, rows_added, b - DIAGS + 1)
                dve.tensor_scalar(diag[:, q % DIAGS, :], ident, acts[:, q:q + 1],
                                  gw[:, n % 2, bass.ds(rel, 1)], ALU.mult, ALU.mult).then_inc(diag_ready, 1)

            def begin(n):
                for rel in range(PUT):
                    put(n, rel, rel)
                for rel in range(LAG):
                    dot(n, 0, rel, rel)

            def take(n, t, rel, q):
                inside = not isinstance(rel, int)
                if not inside and rel == NB + 2:
                    finish(n, 0)
                if inside or rel + LAG < NT * NB:
                    dot(n, t, rel + LAG, (q + LAG) % RING)
                weigh(n, rel, q)
                if inside or rel + PUT < NT * NB:
                    put(n, rel + PUT, (q + PUT) % RING)

            def finish(n, t):
                g = NT * (n - 1) + t
                dve.wait_ge(fin_in, 16 * (g + 1))
                dve.wait_ge(rows_added, (g + 1) * NB)
                dve.tensor_tensor(fin[:, :], acc[:, :], fin[:, :], ALU.add).then_inc(y_ready, 1)

            def slot(b):
                n, rel = b // (NT * NB) + 1, b % (NT * NB)
                take(n, min(rel + LAG, NT * NB - 1) // NB, rel, rel % RING)

            picks = Picks(slot)

            dve.memset(eps[:, :], EPS)
            dve.memset(state[:, :, :], 0.0).then_inc(state_zero, 1)
            dve.wait_ge(consts_in, N_CONST)
            dve.tensor_tensor(w_qs[:, :, :], wide(w_q64[:, :].unsqueeze(1), 2 * DA_H, DA_D), wide(qscale.unsqueeze(2), 2 * DA_H, DA_D), ALU.mult)
            dve.tensor_scalar(w_dao[:, :], w_dao[:, :], 1.0 - LAM_INIT, None, ALU.mult)
            for i in range(2):
                x, z = lam_in[:, 2 * i * DA_D:(2 * i + 1) * DA_D], lam_in[:, (2 * i + 1) * DA_D:(2 * i + 2) * DA_D]
                ins = dve.tensor_tensor_reduce(out=x, in0=x, in1=z, scale=1.0, scalar=0.0, op0=ALU.mult, op1=ALU.add, accum_out=lam[:, i:i + 1])
            ins.then_inc(const_ready, 1)
            dve.wait_ge(lam_exp, 1)
            after(dve.tensor_tensor(lam[:, 1:2], lam[:, 3:4], lam[:, 2:3], ALU.subtract))
            after(dve.tensor_scalar(lam[:, 0:1], lam[:, 1:2], -LAM_INIT, None, ALU.add))

            for n in range(STEPS + 1):
                if n == 0:
                    norm_rows(1).then_inc(norm_rs, 1)
                    take_x(0)
                    norm_heads(1, view(("MK", 0), 8, XA_D), heads_of(xq), 8, XA_D, (grouped, wide(w_xk[:, :].unsqueeze(1), 8, XA_D)), ("MK", 0))
                    norm_rows(2).then_inc(norm_rs, 1)
                    take_x(1)
                    keys(1)
                    queries(1)
                    continue
                project(n)
                memory_attention(n)
                diff_attention(n)
                gla_prepare(n)
                gla(n)
                merge(n)
                route(n)
            n = STEPS
            for t in range(NT):
                for rel in range(t * NB if t else RING, t * NB + RING):
                    take(n, t, rel, rel % RING)
                with dve.Fori(1, NB // RING - 1) as j:
                    for q in range(RING):
                        take(n, t, j * RING + (t * NB + q), q)
                for rel in range((t + 1) * NB - RING, (t + 1) * NB):
                    take(n, min(rel + LAG, NT * NB - 1) // NB, rel, rel % RING)
            finish(n, 1)


def kernel(x, mem, mix_norm_w, w_in, da_q_norm_w, da_k_norm_w, da_lambda, da_out_norm_w,
           gla_w_gate, gla_b_gate, gla_out_norm_w, mem_norm_w, w_mem_kv, xa_q_norm_w, xa_k_norm_w,
           w_br_da, w_br_gla, w_br_xa, w_out, ffn_norm_w, peer_w_q, peer_sub_keys, peer_u, peer_v):
    import concourse.bacc as bacc
    from concourse.bass_utils import run_bass_kernel_spmd

    def cols(w):
        return np.ascontiguousarray(np.asarray(w).reshape(-1, P).T)

    arrays = {
        "x": np.asarray(x)[0], "mem": np.asarray(mem)[0], "consts": constant_table(),
        "mix_w": cols(mix_norm_w), "mem_w": cols(mem_norm_w), "w_in": np.asarray(w_in)[0],
        "q_w": np.asarray(da_q_norm_w)[0], "k_w": np.asarray(da_k_norm_w)[0], "lam": np.asarray(da_lambda).reshape(-1),
        "dao_w": np.asarray(da_out_norm_w)[0], "w_gate": np.asarray(gla_w_gate)[0], "b_gate": cols(gla_b_gate),
        "glo_w": np.asarray(gla_out_norm_w)[0], "w_mkv": np.asarray(w_mem_kv)[0], "xq_w": np.asarray(xa_q_norm_w)[0],
        "xk_w": np.asarray(xa_k_norm_w)[0], "br0": np.asarray(w_br_da)[0], "br1": np.asarray(w_br_gla)[0],
        "br2": np.asarray(w_br_xa)[0], "w_out": np.asarray(w_out)[0], "ffn_w": np.asarray(ffn_norm_w)[0],
        "w_q": np.asarray(peer_w_q)[0], "keysT": np.ascontiguousarray(np.asarray(peer_sub_keys)[0].transpose(2, 0, 1)),
        "peer_u": np.asarray(peer_u)[0], "peer_v": np.asarray(peer_v)[0],
    }
    nc = bacc.Bacc("TRN2", target_bir_lowering=False, num_devices=1)
    args = {}
    feed = {}
    for name, v in arrays.items():
        feed[f"in_{name}"] = np.ascontiguousarray(v)
        args[name] = nc.dram_tensor(f"in_{name}", v.shape, mybir.dt.from_np(v.dtype), kind="ExternalInput").ap()
    args["y"] = nc.dram_tensor("out_y", (SEQ, D), F32, kind="ExternalOutput").ap()
    build(nc, args)
    r = run_bass_kernel_spmd(nc, [feed], core_ids=[0])
    return r.results[0]["out_y"].reshape(1, SEQ, D)
```
